# Optimizing a Trainium2 kernel written in Bass

```python
import math
import jax, jax.numpy as jnp
from jax import lax
import numpy as np

D_MODEL = 1024
BATCH = 1
SEQ = 256
DEPTH = 1

GRID_W = 64
CTX_LEN = 256

SSD_EXPAND = 2
D_INNER = SSD_EXPAND * D_MODEL
SSD_HEADDIM = 64
SSD_HEADS = D_INNER // SSD_HEADDIM
SSD_GROUPS = 4
SSD_STATE = 128
SSD_CONV = 5
SSD_CHUNK = 128
D_BC = SSD_GROUPS * SSD_STATE
D_XBC = D_INNER + 2 * D_BC

POOL_WINDOWS = (2, 4, 8, 16)
POOL_WIDTH = D_MODEL
POOL_GROUPS = len(POOL_WINDOWS)
POOL_GROUP_DIM = POOL_WIDTH // POOL_GROUPS

IN_SPLITS = (D_INNER, D_INNER + D_XBC, D_INNER + D_XBC + 2 * SSD_HEADS,
             D_INNER + D_XBC + 2 * SSD_HEADS + POOL_WIDTH)
IN_COLS = IN_SPLITS[-1] + 2 * D_MODEL

MOE_GROUPS = 4
MOE_EXPERTS_PER_GROUP = 8
MOE_EXPERTS = MOE_GROUPS * MOE_EXPERTS_PER_GROUP
MOE_TOP_K = 2
D_EXPERT = 512
MOE_BLOCK = 256

DEEPNORM_ALPHA = (2.0 * DEPTH) ** 0.25
DEEPNORM_BETA = (8.0 * DEPTH) ** -0.25
NORM_EPS = 1e-5


def layer_norm(x, g, b):
    xf = x.astype(jnp.float32)
    mu = xf.mean(-1, keepdims=True)
    var = jnp.square(xf - mu).mean(-1, keepdims=True)
    return ((xf - mu) * lax.rsqrt(var + NORM_EPS) * g.astype(jnp.float32) + b.astype(jnp.float32)).astype(x.dtype)

def post_norm(x, y, g, b):
    return layer_norm(DEEPNORM_ALPHA * x + y, g, b)

def modulate(x, shift, scale):
    return x * (1 + scale) + shift

def rms_norm_gated(y, z, g):
    yz = y.astype(jnp.float32) * jax.nn.silu(z.astype(jnp.float32))
    return yz * lax.rsqrt(jnp.mean(yz * yz, -1, keepdims=True) + NORM_EPS) * g.astype(jnp.float32)

def flip_seq(t):
    return t[:, ::-1]

def conv_centred(u, w, b):
    ch = u.shape[-1]
    y = lax.conv_general_dilated(u, w[:, None, :].astype(u.dtype), window_strides=(1,),
                                 padding=((SSD_CONV // 2, SSD_CONV // 2),),
                                 dimension_numbers=('NWC', 'WIO', 'NWC'), feature_group_count=ch)
    return y + b

def ssd_decay(dt_raw, lp):
    b, l, _ = dt_raw.shape
    dt = jax.nn.softplus(dt_raw.reshape(b, l, 2, SSD_HEADS).astype(jnp.float32) + lp['dt_bias'].astype(jnp.float32))
    a = dt * -jnp.exp(lp['a_log'].astype(jnp.float32))
    return dt, a

def ssd_scan(xdt, a, bm, cm, h0):
    b, l = a.shape[:2]
    r = SSD_HEADS // SSD_GROUPS
    q = SSD_CHUNK
    nc = l // q

    def chunks(t):
        return jnp.moveaxis(t.reshape((b, nc, q) + t.shape[2:]), 1, 0)

    xs = (chunks(xdt.reshape(b, l, SSD_GROUPS, r, SSD_HEADDIM)), chunks(a.reshape(b, l, SSD_GROUPS, r)),
          chunks(bm), chunks(cm))
    lower = jnp.tril(jnp.ones((q, q), dtype=bool))[None, :, :, None, None]

    def step(state, inp):
        xc, ac, bc, cc = inp
        acs = jnp.cumsum(ac, axis=1)
        seg = acs[:, :, None] - acs[:, None, :]
        decay = jnp.exp(jnp.where(lower, seg, -jnp.inf))
        cb = jnp.einsum('bign,bjgn->bijg', cc, bc)
        y_diag = jnp.einsum('bijg,bijgr,bjgrp->bigrp', cb, decay, xc)
        y_off = jnp.einsum('bign,bgrpn->bigrp', cc, state) * jnp.exp(acs)[..., None]
        tail = jnp.exp(acs[:, -1:] - acs)
        state = state * jnp.exp(acs[:, -1])[..., None, None] + jnp.einsum('bjgn,bjgr,bjgrp->bgrpn', bc, tail, xc)
        return state, y_diag + y_off

    h_final, ys = lax.scan(step, h0.reshape(b, SSD_GROUPS, r, SSD_HEADDIM, SSD_STATE), xs)
    y = jnp.moveaxis(ys, 0, 1).reshape(b, l, SSD_HEADS, SSD_HEADDIM)
    return y, h_final.reshape(b, SSD_HEADS, SSD_HEADDIM, SSD_STATE)

def ssd_final_state(xdt, a, bm):
    b, l = a.shape[:2]
    r = SSD_HEADS // SSD_GROUPS
    acs = jnp.cumsum(a, axis=1)
    tail = jnp.exp(acs[:, -1:] - acs).reshape(b, l, SSD_GROUPS, r)
    st = jnp.einsum('blgn,blgr,blgrp->bgrpn', bm, tail, xdt.reshape(b, l, SSD_GROUPS, r, SSD_HEADDIM))
    return st.reshape(b, SSD_HEADS, SSD_HEADDIM, SSD_STATE)

def ssd_branch(z, xbc, dt_raw, lp, h0_f, h0_b):
    b, l, _ = z.shape
    xbc = jax.nn.silu(conv_centred(xbc, lp['conv_w'], lp['conv_b'])).astype(jnp.float32)
    xs, bm, cm = jnp.split(xbc, (D_INNER, D_INNER + D_BC), axis=-1)
    xs = xs.reshape(b, l, SSD_HEADS, SSD_HEADDIM)
    bm = bm.reshape(b, l, SSD_GROUPS, SSD_STATE)
    cm = cm.reshape(b, l, SSD_GROUPS, SSD_STATE)
    dt, a = ssd_decay(dt_raw, lp)
    y_f, s_f = ssd_scan(xs * dt[:, :, 0, :, None], a[:, :, 0], bm, cm, h0_f)
    y_b, s_b = ssd_scan(flip_seq(xs * dt[:, :, 1, :, None]), flip_seq(a[:, :, 1]), flip_seq(bm), flip_seq(cm), h0_b)
    y = y_f + flip_seq(y_b) + xs * lp['d_skip'].astype(jnp.float32)[:, None]
    y = rms_norm_gated(y.reshape(b, l, D_INNER), z, lp['ssd_norm_g'])
    return y.astype(z.dtype), s_f, s_b

def ssd_context_states(hc, lp):
    b, l, _ = hc.shape
    w = lp['w_in']
    xb = hc @ w[:, IN_SPLITS[0]:IN_SPLITS[0] + D_INNER + D_BC]
    dt_raw = hc @ w[:, IN_SPLITS[1]:IN_SPLITS[2]]
    xb = jax.nn.silu(conv_centred(xb, lp['conv_w'][:, :D_INNER + D_BC], lp['conv_b'][:D_INNER + D_BC])).astype(jnp.float32)
    xs, bm = jnp.split(xb, (D_INNER,), axis=-1)
    xs = xs.reshape(b, l, SSD_HEADS, SSD_HEADDIM)
    bm = bm.reshape(b, l, SSD_GROUPS, SSD_STATE)
    dt, a = ssd_decay(dt_raw, lp)
    s_f = ssd_final_state(xs * dt[:, :, 0, :, None], a[:, :, 0], bm)
    s_b = ssd_final_state(flip_seq(xs * dt[:, :, 1, :, None]), flip_seq(a[:, :, 1]), flip_seq(bm))
    return s_f, s_b

def window_sum(u, axis, k):
    n = u.shape[axis]
    pad = [(0, 0)] * u.ndim
    pad[axis] = (1, 0)
    cs = jnp.cumsum(jnp.pad(u, pad), axis=axis)
    pos = jnp.arange(n)
    lo = jnp.clip(pos - k // 2, 0, n)
    hi = jnp.clip(pos - k // 2 + k, 0, n)
    s = jnp.take(cs, hi, axis=axis) - jnp.take(cs, lo, axis=axis)
    return s, (hi - lo).astype(jnp.float32)

def pool_grid(uf):
    b, l = uf.shape[:2]
    rows = l // GRID_W
    ug_all = uf.reshape(b, rows, GRID_W, POOL_GROUPS, POOL_GROUP_DIM)
    outs = []
    for gi, k in enumerate(POOL_WINDOWS):
        ug = ug_all[:, :, :, gi]
        s, cnt_r = window_sum(ug, 1, k)
        s, cnt_c = window_sum(s, 2, k)
        outs.append(s / (cnt_r[:, None] * cnt_c[None, :])[None, :, :, None])
    return jnp.stack(outs, axis=3).reshape(b, l, POOL_GROUPS, POOL_GROUP_DIM)

def pool_seq(uf):
    outs = []
    for gi, k in enumerate(POOL_WINDOWS):
        s, cnt = window_sum(uf[:, :, gi], 1, k)
        outs.append(s / cnt[None, :, None])
    return jnp.stack(outs, axis=2)

def pool_branch(u, lp, on_grid):
    b, l, _ = u.shape
    uf = u.astype(jnp.float32).reshape(b, l, POOL_GROUPS, POOL_GROUP_DIM)
    mean = pool_grid(uf) if on_grid else pool_seq(uf)
    y = jnp.einsum('blgc,gcd->blgd', mean - uf, lp['pool_w'].astype(jnp.float32)).reshape(b, l, POOL_WIDTH)
    return (y * lp['pool_scale'].astype(jnp.float32)).astype(u.dtype)

def mix_stream(h, lp, on_grid, h0_f, h0_b):
    z, xbc, dt_raw, u, gates = jnp.split(h @ lp['w_in'], IN_SPLITS, axis=-1)
    y_a, s_f, s_b = ssd_branch(z, xbc, dt_raw, lp, h0_f, h0_b)
    y_p = pool_branch(u, lp, on_grid)
    g = jax.nn.sigmoid((gates + lp['b_gate']).astype(jnp.float32)).astype(h.dtype)
    g_a, g_p = jnp.split(g, 2, axis=-1)
    merged = g_a * (y_a @ lp['w_branch_a']) + g_p * (y_p @ lp['w_branch_b'])
    return merged @ lp['w_out'], s_f, s_b

def swiglu(xb, wg, wu, wd):
    return (jax.nn.silu(xb @ wg) * (xb @ wu)) @ wd

def hier_moe(h, lp):
    t, d = h.shape
    hf = h.astype(jnp.float32)
    lg = hf @ lp['w_rg'].astype(jnp.float32) + lp['b_rg'].astype(jnp.float32)
    grp = jnp.argmax(lg, axis=-1)
    p_grp = jnp.take_along_axis(jax.nn.softmax(lg, axis=-1), grp[:, None], axis=-1)
    le = jnp.einsum('td,gde->tge', hf, lp['w_re'].astype(jnp.float32)) + lp['b_re'].astype(jnp.float32)
    le = jnp.take_along_axis(le, grp[:, None, None], axis=1)[:, 0]
    top_v, top_i = lax.top_k(le, MOE_TOP_K)
    w = p_grp * jax.nn.softmax(top_v, axis=-1)
    eid = grp[:, None].astype(jnp.int32) * MOE_EXPERTS_PER_GROUP + top_i.astype(jnp.int32)
    n_assign = t * MOE_TOP_K
    flat_e = eid.reshape(-1)
    flat_t = jnp.repeat(jnp.arange(t, dtype=jnp.int32), MOE_TOP_K)
    order = jnp.argsort(flat_e)
    se, st, sw = flat_e[order], flat_t[order], w.reshape(-1)[order]
    counts = jnp.bincount(flat_e, length=MOE_EXPERTS)
    padded = (counts + MOE_BLOCK - 1) // MOE_BLOCK * MOE_BLOCK
    pad_end = jnp.cumsum(padded)
    pad_start = pad_end - padded
    start = jnp.cumsum(counts) - counts
    dest = pad_start[se] + jnp.arange(n_assign, dtype=jnp.int32) - start[se]
    n_blocks = -(-n_assign // MOE_BLOCK) + MOE_EXPERTS
    n_rows = n_blocks * MOE_BLOCK
    row_tok = jnp.full((n_rows,), t, jnp.int32).at[dest].set(st)
    block_e = jnp.minimum(jnp.searchsorted(pad_end, jnp.arange(n_blocks, dtype=jnp.int32) * MOE_BLOCK, side='right'),
                          MOE_EXPERTS - 1)
    h_pad = jnp.concatenate([h, jnp.zeros((1, d), h.dtype)], axis=0)
    xin = h_pad[row_tok].reshape(n_blocks, MOE_BLOCK, d)

    def expert_block(args):
        xb, e = args
        return swiglu(xb, lp['w_eg'][e], lp['w_eu'][e], lp['w_ed'][e])

    yb = lax.map(expert_block, (xin, block_e)).reshape(n_rows, d)
    return jax.ops.segment_sum(yb[dest] * sw[:, None].astype(h.dtype), st, num_segments=t)

def first_inputs(seed: int = 0) -> dict:
    key = jax.random.key(seed)
    ks = jax.random.split(key, 32)
    f32 = jnp.float32
    L, D = DEPTH, D_MODEL

    def nrm(k, shape, scale):
        return jax.random.normal(k, shape, f32) * scale

    dt0 = jnp.exp(jax.random.uniform(ks[8], (L, 2, SSD_HEADS), f32, math.log(1e-3), math.log(1e-1)))
    return {
        'x': nrm(ks[0], (BATCH, SEQ, D), 1.0),
        'c': nrm(ks[1], (BATCH, D), 1.0),
        'ctx': nrm(ks[2], (BATCH, CTX_LEN, D), 1.0),
        'c_ctx': nrm(ks[3], (D,), 1.0),
        'w_ada': nrm(ks[4], (L, D, 6 * D), D ** -0.5),
        'b_ada': nrm(ks[5], (L, 6 * D), 0.02),
        'w_in': nrm(ks[6], (L, D, IN_COLS), D ** -0.5),
        'b_gate': nrm(ks[7], (L, 2 * D), 0.1),
        'conv_w': nrm(ks[9], (L, SSD_CONV, D_XBC), SSD_CONV ** -0.5),
        'conv_b': nrm(ks[10], (L, D_XBC), 0.02),
        'dt_bias': dt0 + jnp.log(-jnp.expm1(-dt0)),
        'a_log': jnp.log(jax.random.uniform(ks[11], (L, 2, SSD_HEADS), f32, 1.0, 16.0)),
        'd_skip': 1.0 + nrm(ks[12], (L, SSD_HEADS), 0.1),
        'ssd_norm_g': 1.0 + nrm(ks[13], (L, D_INNER), 0.1),
        'pool_w': nrm(ks[14], (L, POOL_GROUPS, POOL_GROUP_DIM, POOL_GROUP_DIM), POOL_GROUP_DIM ** -0.5),
        'pool_scale': 1.0 + nrm(ks[15], (L, POOL_WIDTH), 0.1),
        'w_branch_a': nrm(ks[16], (L, D_INNER, D), D_INNER ** -0.5),
        'w_branch_b': nrm(ks[17], (L, POOL_WIDTH, D), POOL_WIDTH ** -0.5),
        'w_out': nrm(ks[18], (L, D, D), D ** -0.5 * DEEPNORM_BETA),
        'ln1_g': 1.0 + nrm(ks[19], (L, D), 0.1),
        'ln1_b': nrm(ks[20], (L, D), 0.02),
        'ln2_g': 1.0 + nrm(ks[21], (L, D), 0.1),
        'ln2_b': nrm(ks[22], (L, D), 0.02),
        'w_router_group': nrm(ks[23], (L, D, MOE_GROUPS), D ** -0.5),
        'b_router_group': nrm(ks[24], (L, MOE_GROUPS), 0.01),
        'w_router_expert': nrm(ks[25], (L, MOE_GROUPS, D, MOE_EXPERTS_PER_GROUP), D ** -0.5),
        'b_router_expert': nrm(ks[26], (L, MOE_GROUPS, MOE_EXPERTS_PER_GROUP), 0.01),
        'w_expert_gate': nrm(ks[27], (L, MOE_EXPERTS, D, D_EXPERT), D ** -0.5),
        'w_expert_up': nrm(ks[28], (L, MOE_EXPERTS, D, D_EXPERT), D ** -0.5),
        'w_expert_down': nrm(ks[29], (L, MOE_EXPERTS, D_EXPERT, D), D_EXPERT ** -0.5 * DEEPNORM_BETA),
    }

def first_block(x, c, ctx, c_ctx, w_ada, b_ada, w_in, b_gate, conv_w, conv_b, dt_bias, a_log, d_skip,
              ssd_norm_g, pool_w, pool_scale, w_branch_a, w_branch_b, w_out, ln1_g, ln1_b, ln2_g, ln2_b,
              w_router_group, b_router_group, w_router_expert, b_router_expert,
              w_expert_gate, w_expert_up, w_expert_down):
    b, l, d = x.shape
    lc = ctx.shape[1]
    xl, xc = x, ctx
    zero_state = jnp.zeros((b, SSD_HEADS, SSD_HEADDIM, SSD_STATE), jnp.float32)
    for i in range(DEPTH):
        last = i == DEPTH - 1
        lp = {'w_in': w_in[i], 'b_gate': b_gate[i], 'conv_w': conv_w[i], 'conv_b': conv_b[i],
              'dt_bias': dt_bias[i], 'a_log': a_log[i], 'd_skip': d_skip[i], 'ssd_norm_g': ssd_norm_g[i],
              'pool_w': pool_w[i], 'pool_scale': pool_scale[i], 'w_branch_a': w_branch_a[i],
              'w_branch_b': w_branch_b[i], 'w_out': w_out[i],
              'w_rg': w_router_group[i], 'b_rg': b_router_group[i],
              'w_re': w_router_expert[i], 'b_re': b_router_expert[i],
              'w_eg': w_expert_gate[i], 'w_eu': w_expert_up[i], 'w_ed': w_expert_down[i]}
        mod_l = jnp.split((jax.nn.silu(c) @ w_ada[i] + b_ada[i])[:, None, :], 6, axis=-1)
        mod_c = jnp.split((jax.nn.silu(c_ctx) @ w_ada[i] + b_ada[i])[None, None, :], 6, axis=-1)

        hc = modulate(xc, mod_c[0], mod_c[1])
        hl = modulate(xl, mod_l[0], mod_l[1])
        if last:
            s_f, s_b = ssd_context_states(hc, lp)
        else:
            out_c, s_f, s_b = mix_stream(hc, lp, False, zero_state, zero_state)
            xc = post_norm(xc, mod_c[2] * out_c, ln1_g[i], ln1_b[i])
        out_l, _, _ = mix_stream(hl, lp, True, s_f, s_b)
        xl = post_norm(xl, mod_l[2] * out_l, ln1_g[i], ln1_b[i])

        hl = modulate(xl, mod_l[3], mod_l[4]).reshape(b * l, d)
        if last:
            yl = hier_moe(hl, lp)
        else:
            hc = modulate(xc, mod_c[3], mod_c[4]).reshape(b * lc, d)
            y = hier_moe(jnp.concatenate([hl, hc], axis=0), lp)
            yl, yc = y[:b * l], y[b * l:]
            xc = post_norm(xc, mod_c[5] * yc.reshape(b, lc, d), ln2_g[i], ln2_b[i])
        xl = post_norm(xl, mod_l[5] * yl.reshape(b, l, d), ln2_g[i], ln2_b[i])
    return xl


DEPTH_2 = 2


D_FF = 2816

GLA_HEADS = 4
GLA_DK = 64
GLA_DV = 128
GLA_QK = GLA_HEADS * GLA_DK
GLA_V = GLA_HEADS * GLA_DV
GLA_RANK = 16
GLA_TAU = 16.0
GLA_CHUNK = 64

MLA_HEADS = 4
MLA_D_NOPE = 128
MLA_D_ROPE = 64
MLA_D_V = 128
MLA_D_CQ = 384
MLA_D_CKV = 128
MLA_SCALE = (MLA_D_NOPE + MLA_D_ROPE) ** -0.5

NA_HEADS = 16
NA_HEAD_DIM = 64
NA_KH = 8
NA_KW = 16

ROPE_BASE = 10000.0
Q_BLOCK = 128
EPS = 1e-6
N_EVEN = (DEPTH_2 + 1) // 2
N_ODD = DEPTH_2 // 2
ALPHA = (2 * DEPTH_2) ** 0.25
BETA = (8 * DEPTH_2) ** -0.25

EVEN_SIZES = (GLA_QK, GLA_QK, GLA_V, GLA_V, GLA_RANK, GLA_RANK, MLA_D_CQ, MLA_D_CKV, MLA_D_ROPE)
EVEN_OUT_IN = GLA_V + MLA_HEADS * MLA_D_V
NA_WIDTH = NA_HEADS * NA_HEAD_DIM


def layer_norm_2(x):
    xf = x.astype(jnp.float32)
    mu = jnp.mean(xf, axis=-1, keepdims=True)
    var = jnp.mean(jnp.square(xf - mu), axis=-1, keepdims=True)
    return ((xf - mu) * lax.rsqrt(var + EPS)).astype(x.dtype)

def rms_norm(x, g):
    xf = x.astype(jnp.float32)
    y = xf * lax.rsqrt(jnp.mean(jnp.square(xf), axis=-1, keepdims=True) + EPS)
    return y.astype(x.dtype) * g

def modulate_2(x, shift, scale):
    return x * (1.0 + scale) + shift

def post_norm_2(x, y):
    return layer_norm_2(ALPHA * x + y)

def swiglu_2(h, w_in, w_out):
    gate, up = jnp.split(h @ w_in, 2, axis=-1)
    return (jax.nn.silu(gate) * up) @ w_out

def axial_rope(n_tokens):
    t = jnp.arange(n_tokens)
    row = (t // GRID_W).astype(jnp.float32)
    col = (t % GRID_W).astype(jnp.float32)
    n_freq = MLA_D_ROPE // 4
    inv = ROPE_BASE ** (-jnp.arange(n_freq, dtype=jnp.float32) / n_freq)
    ang = jnp.concatenate([row[:, None] * inv, col[:, None] * inv], axis=-1)
    return jnp.cos(ang), jnp.sin(ang)

def apply_rope(x, cos, sin):
    x2 = x.reshape(*x.shape[:-1], -1, 2).astype(jnp.float32)
    x0, x1 = x2[..., 0], x2[..., 1]
    out = jnp.stack([x0 * cos - x1 * sin, x0 * sin + x1 * cos], axis=-1)
    return out.reshape(x.shape).astype(x.dtype)

def dense_attention(q, k, v, scale):
    B, T, H, dk = q.shape
    nb = T // Q_BLOCK
    qb = q.reshape(B, nb, Q_BLOCK, H, dk).transpose(1, 0, 2, 3, 4)

    def block(qi):
        s = jnp.einsum('bqhd,bkhd->bhqk', qi, k).astype(jnp.float32) * scale
        p = jax.nn.softmax(s, axis=-1).astype(v.dtype)
        return jnp.einsum('bhqk,bkhd->bqhd', p, v)

    o = lax.map(block, qb)
    return o.transpose(1, 0, 2, 3, 4).reshape(B, T, H, v.shape[-1])

def gla_chunked(q, k, v, log_g, s0, include_diag):
    B, T, H, DK = q.shape
    DV = v.shape[-1]
    n = T // GLA_CHUNK

    def to_chunks(a):
        return a.reshape(B, n, GLA_CHUNK, H, a.shape[-1]).transpose(1, 0, 3, 2, 4)

    idx = jnp.arange(GLA_CHUNK)
    mask = (idx[:, None] >= idx[None, :]) if include_diag else (idx[:, None] > idx[None, :])

    def step(s, inp):
        qi, ki, vi, gi = inp
        b = jnp.cumsum(gi.astype(jnp.float32), axis=-2)
        diff = b[:, :, :, None, :] - b[:, :, None, :, :]
        decay = jnp.exp(jnp.where(mask[:, :, None], diff, -jnp.inf)).astype(qi.dtype)
        att = jnp.einsum('bhid,bhjd,bhijd->bhij', qi, ki, decay)
        o_intra = jnp.einsum('bhij,bhjv->bhiv', att, vi)
        o_inter = jnp.einsum('bhid,bhdv->bhiv', qi * jnp.exp(b).astype(qi.dtype), s)
        b_last = b[:, :, -1:, :]
        k_dec = ki * jnp.exp(b_last - b).astype(ki.dtype)
        s_new = s * jnp.exp(b_last[:, :, 0, :])[..., None].astype(s.dtype) + jnp.einsum('bhjd,bhjv->bhdv', k_dec, vi)
        return s_new, o_intra + o_inter

    s_fin, o = lax.scan(step, s0, (to_chunks(q), to_chunks(k), to_chunks(v), to_chunks(log_g)))
    return o.transpose(1, 0, 3, 2, 4).reshape(B, T, H, DV), s_fin

def gla_log_gate(lr, wg2, bg):
    return jax.nn.log_sigmoid((lr @ wg2 + bg).astype(jnp.float32)) / GLA_TAU

def gla_out(o, r, norm_g):
    B, T = o.shape[:2]
    return rms_norm(o, norm_g).reshape(B, T, GLA_V) * jax.nn.silu(r)

def even_project(h, w_in, wg2_f, bg_f, wg2_b, bg_b, q_norm_g, kv_norm_g, w_uq, w_ukv):
    B, T, _ = h.shape
    split_points = np.cumsum(EVEN_SIZES)[:-1].tolist()
    q_g, k_g, v_g, r_g, lr_f, lr_b, c_q, c_kv, k_r = jnp.split(h @ w_in, split_points, axis=-1)
    heads = lambda a, n: a.reshape(B, T, n, -1)
    gla = (heads(q_g, GLA_HEADS) * GLA_DK ** -0.5, heads(k_g, GLA_HEADS), heads(v_g, GLA_HEADS),
           heads(gla_log_gate(lr_f, wg2_f, bg_f), GLA_HEADS), heads(gla_log_gate(lr_b, wg2_b, bg_b), GLA_HEADS), r_g)
    q = heads(rms_norm(c_q, q_norm_g) @ w_uq, MLA_HEADS)
    kv = heads(rms_norm(c_kv, kv_norm_g) @ w_ukv, MLA_HEADS)
    mla = (q[..., :MLA_D_NOPE], q[..., MLA_D_NOPE:], kv[..., :MLA_D_NOPE], k_r, kv[..., MLA_D_NOPE:])
    return gla, mla

def even_mixer(hc, hl, cos, sin, w_in, wg2_f, bg_f, wg2_b, bg_b, gla_norm_g, q_norm_g, kv_norm_g,
               w_uq, w_ukv, w_out, with_ctx_out):
    B, S, _ = hl.shape
    args = (w_in, wg2_f, bg_f, wg2_b, bg_b, q_norm_g, kv_norm_g, w_uq, w_ukv)
    (gq_c, gk_c, gv_c, gf_c, gb_c, r_c), (qn_c, qr_c, kn_c, kr_c, v_c) = even_project(hc, *args)
    (gq_l, gk_l, gv_l, gf_l, gb_l, r_l), (qn_l, qr_l, kn_l, kr_l, v_l) = even_project(hl, *args)

    s0 = jnp.zeros((B, GLA_HEADS, GLA_DK, GLA_DV), hl.dtype)
    flip = lambda a: a[:, ::-1]
    o_cf, s_cf = gla_chunked(gq_c, gk_c, gv_c, gf_c, s0, True)
    o_cb, s_cb = gla_chunked(flip(gq_c), flip(gk_c), flip(gv_c), flip(gb_c), s0, False)
    o_lf, _ = gla_chunked(gq_l, gk_l, gv_l, gf_l, s_cf, True)
    o_lb, _ = gla_chunked(flip(gq_l), flip(gk_l), flip(gv_l), flip(gb_l), s_cb, False)
    gla_l = gla_out(o_lf + flip(o_lb), r_l, gla_norm_g)

    rope_shape = kn_l.shape[:-1] + (MLA_D_ROPE,)
    q_l = jnp.concatenate([qn_l, apply_rope(qr_l, cos[None, :, None], sin[None, :, None])], axis=-1)
    kr_l_rot = apply_rope(kr_l, cos[None], sin[None])
    k_l = jnp.concatenate([kn_l, jnp.broadcast_to(kr_l_rot[:, :, None], rope_shape)], axis=-1)
    k_c = jnp.concatenate([kn_c, jnp.broadcast_to(kr_c[:, :, None], kn_c.shape[:-1] + (MLA_D_ROPE,))], axis=-1)
    k_all = jnp.concatenate([k_c, k_l], axis=1)
    v_all = jnp.concatenate([v_c, v_l], axis=1)
    mla_l = dense_attention(q_l, k_all, v_all, MLA_SCALE).reshape(B, S, -1)

    yl = jnp.concatenate([gla_l, mla_l], axis=-1) @ w_out
    yc = None
    if with_ctx_out:
        Tc = hc.shape[1]
        gla_c = gla_out(o_cf + flip(o_cb), r_c, gla_norm_g)
        q_c = jnp.concatenate([qn_c, qr_c], axis=-1)
        mla_c = dense_attention(q_c, k_c, v_c, MLA_SCALE).reshape(B, Tc, -1)
        yc = jnp.concatenate([gla_c, mla_c], axis=-1) @ w_out
    return yc, yl

def neighbourhood_attention(q, k, v, k_ctx, v_ctx, rpb):
    B, S, H, d = q.shape
    rows = S // GRID_W
    kh = min(NA_KH, rows)
    scale = d ** -0.5
    qg = q.reshape(B, rows, GRID_W, H, d)
    kg = k.reshape(B, rows, GRID_W, H, d)
    vg = v.reshape(B, rows, GRID_W, H, d)
    col = jnp.arange(GRID_W)
    col_start = jnp.clip(col - NA_KW // 2, 0, GRID_W - NA_KW)
    col_idx = col_start[:, None] + jnp.arange(NA_KW)[None, :]
    bias_col = rpb[:, :, col_idx - col[:, None] + (NA_KW - 1)]

    def row_block(r):
        r_start = jnp.clip(r - kh // 2, 0, rows - kh)
        k_win = lax.dynamic_slice_in_dim(kg, r_start, kh, axis=1)[:, :, col_idx]
        v_win = lax.dynamic_slice_in_dim(vg, r_start, kh, axis=1)[:, :, col_idx]
        q_r = lax.dynamic_index_in_dim(qg, r, axis=1, keepdims=False)
        rel_row = r_start + jnp.arange(kh) - r + (NA_KH - 1)
        bias = jnp.take(bias_col, rel_row, axis=1).transpose(0, 2, 1, 3)
        s_nb = jnp.einsum('bchd,brcwhd->bhcrw', q_r, k_win).astype(jnp.float32) * scale + bias[None]
        s_cx = jnp.einsum('bchd,bkhd->bhck', q_r, k_ctx).astype(jnp.float32) * scale
        p = jax.nn.softmax(jnp.concatenate([s_nb.reshape(B, H, GRID_W, kh * NA_KW), s_cx], axis=-1), axis=-1)
        p = p.astype(v.dtype)
        p_nb = p[..., :kh * NA_KW].reshape(B, H, GRID_W, kh, NA_KW)
        p_cx = p[..., kh * NA_KW:]
        return (jnp.einsum('bhcrw,brcwhd->bchd', p_nb, v_win)
                + jnp.einsum('bhck,bkhd->bchd', p_cx, v_ctx))

    o = lax.map(row_block, jnp.arange(rows))
    return o.transpose(1, 0, 2, 3, 4).reshape(B, S, H, d)

def odd_mixer(hc, hl, w_in, rpb, w_out, with_ctx_out):
    def project(h):
        B, T, _ = h.shape
        q, k, v = jnp.split(h @ w_in, 3, axis=-1)
        return (q.reshape(B, T, NA_HEADS, NA_HEAD_DIM), k.reshape(B, T, NA_HEADS, NA_HEAD_DIM),
                v.reshape(B, T, NA_HEADS, NA_HEAD_DIM))

    B, S, _ = hl.shape
    q_c, k_c, v_c = project(hc)
    q_l, k_l, v_l = project(hl)
    yl = neighbourhood_attention(q_l, k_l, v_l, k_c, v_c, rpb).reshape(B, S, NA_WIDTH) @ w_out
    yc = None
    if with_ctx_out:
        o_c = dense_attention(q_c, k_c, v_c, NA_HEAD_DIM ** -0.5)
        yc = o_c.reshape(B, hc.shape[1], NA_WIDTH) @ w_out
    return yc, yl

def second_inputs(seed: int = 0) -> dict:
    key = jax.random.key(seed)
    it = iter(list(jax.random.split(key, 32)))
    nrm = lambda shape, scale: jax.random.normal(next(it), shape, jnp.float32) * scale
    D = D_MODEL
    gate_base = jnp.tile(jnp.concatenate([jnp.zeros((2 * D,), jnp.float32), jnp.ones((D,), jnp.float32)]), 3)
    return {
        'x': nrm((BATCH, SEQ, D), 1.0),
        'c': nrm((BATCH, D), 1.0),
        'ctx': nrm((BATCH, CTX_LEN, D), 1.0),
        'c_ctx': nrm((D,), 1.0),
        'ada_w': nrm((DEPTH_2, D, 9 * D), 0.5 * D ** -0.5),
        'ada_b': gate_base + nrm((DEPTH_2, 9 * D), 0.02),
        'ffn1_w_in': nrm((DEPTH_2, D, 2 * D_FF), D ** -0.5),
        'ffn1_w_out': nrm((DEPTH_2, D_FF, D), BETA * D_FF ** -0.5),
        'ffn2_w_in': nrm((DEPTH_2, D, 2 * D_FF), D ** -0.5),
        'ffn2_w_out': nrm((DEPTH_2, D_FF, D), BETA * D_FF ** -0.5),
        'even_w_in': nrm((N_EVEN, D, sum(EVEN_SIZES)), D ** -0.5),
        'gla_wg2_f': nrm((N_EVEN, GLA_RANK, GLA_QK), GLA_RANK ** -0.5),
        'gla_bg_f': nrm((N_EVEN, GLA_QK), 0.5),
        'gla_wg2_b': nrm((N_EVEN, GLA_RANK, GLA_QK), GLA_RANK ** -0.5),
        'gla_bg_b': nrm((N_EVEN, GLA_QK), 0.5),
        'gla_norm_g': 1.0 + nrm((N_EVEN, GLA_DV), 0.02),
        'mla_q_norm_g': 1.0 + nrm((N_EVEN, MLA_D_CQ), 0.02),
        'mla_kv_norm_g': 1.0 + nrm((N_EVEN, MLA_D_CKV), 0.02),
        'mla_w_uq': nrm((N_EVEN, MLA_D_CQ, MLA_HEADS * (MLA_D_NOPE + MLA_D_ROPE)), MLA_D_CQ ** -0.5),
        'mla_w_ukv': nrm((N_EVEN, MLA_D_CKV, MLA_HEADS * (MLA_D_NOPE + MLA_D_V)), MLA_D_CKV ** -0.5),
        'even_w_out': nrm((N_EVEN, EVEN_OUT_IN, D), BETA * EVEN_OUT_IN ** -0.5),
        'na_w_in': nrm((N_ODD, D, 3 * NA_WIDTH), D ** -0.5),
        'na_rpb': nrm((N_ODD, NA_HEADS, 2 * NA_KH - 1, 2 * NA_KW - 1), 0.5),
        'na_w_out': nrm((N_ODD, NA_WIDTH, D), BETA * NA_WIDTH ** -0.5),
    }

def second_block(x, c, ctx, c_ctx, ada_w, ada_b, ffn1_w_in, ffn1_w_out, ffn2_w_in, ffn2_w_out,
              even_w_in, gla_wg2_f, gla_bg_f, gla_wg2_b, gla_bg_b, gla_norm_g, mla_q_norm_g, mla_kv_norm_g,
              mla_w_uq, mla_w_ukv, even_w_out, na_w_in, na_rpb, na_w_out):
    S = x.shape[1]
    cos, sin = axial_rope(S)
    xl, xc = x, ctx
    for l in range(DEPTH_2):
        last = l == DEPTH_2 - 1
        i = l // 2
        mod_l = jax.nn.silu(c) @ ada_w[l] + ada_b[l]
        mod_c = jax.nn.silu(c_ctx) @ ada_w[l] + ada_b[l]
        sh1, sc1, g1, sh2, sc2, g2, sh3, sc3, g3 = [m[:, None, :] for m in jnp.split(mod_l, 9, axis=-1)]
        csh1, csc1, cg1, csh2, csc2, cg2, csh3, csc3, cg3 = jnp.split(mod_c, 9)

        xl = post_norm_2(xl, 0.5 * g1 * swiglu_2(modulate_2(xl, sh1, sc1), ffn1_w_in[l], ffn1_w_out[l]))
        xc = post_norm_2(xc, 0.5 * cg1 * swiglu_2(modulate_2(xc, csh1, csc1), ffn1_w_in[l], ffn1_w_out[l]))

        hl = modulate_2(xl, sh2, sc2)
        hc = modulate_2(xc, csh2, csc2)
        if l % 2 == 0:
            yc, yl = even_mixer(hc, hl, cos, sin, even_w_in[i], gla_wg2_f[i], gla_bg_f[i], gla_wg2_b[i], gla_bg_b[i],
                                gla_norm_g[i], mla_q_norm_g[i], mla_kv_norm_g[i], mla_w_uq[i], mla_w_ukv[i],
                                even_w_out[i], not last)
        else:
            yc, yl = odd_mixer(hc, hl, na_w_in[i], na_rpb[i], na_w_out[i], not last)
        xl = post_norm_2(xl, g2 * yl)

        xl = post_norm_2(xl, 0.5 * g3 * swiglu_2(modulate_2(xl, sh3, sc3), ffn2_w_in[l], ffn2_w_out[l]))
        if not last:
            xc = post_norm_2(xc, cg2 * yc)
            xc = post_norm_2(xc, 0.5 * cg3 * swiglu_2(modulate_2(xc, csh3, csc3), ffn2_w_in[l], ffn2_w_out[l]))
    return xl


def setup_inputs(seed=0):
    out = dict(first_inputs(seed))
    for name, value in second_inputs(seed + 1).items():
        if name != "x":
            out[name + "_2"] = value
    return out


def reference(
    x, c, ctx, c_ctx, w_ada, b_ada, w_in, b_gate, conv_w, conv_b, dt_bias, a_log, d_skip,
    ssd_norm_g, pool_w, pool_scale, w_branch_a, w_branch_b, w_out, ln1_g, ln1_b, ln2_g, ln2_b,
    w_router_group, b_router_group, w_router_expert, b_router_expert, w_expert_gate,
    w_expert_up, w_expert_down, c_2, ctx_2, c_ctx_2, ada_w_2, ada_b_2, ffn1_w_in_2,
    ffn1_w_out_2, ffn2_w_in_2, ffn2_w_out_2, even_w_in_2, gla_wg2_f_2, gla_bg_f_2, gla_wg2_b_2,
    gla_bg_b_2, gla_norm_g_2, mla_q_norm_g_2, mla_kv_norm_g_2, mla_w_uq_2, mla_w_ukv_2,
    even_w_out_2, na_w_in_2, na_rpb_2, na_w_out_2,
):
    x = first_block(
        x, c, ctx, c_ctx, w_ada, b_ada, w_in, b_gate, conv_w, conv_b, dt_bias, a_log, d_skip,
        ssd_norm_g, pool_w, pool_scale, w_branch_a, w_branch_b, w_out, ln1_g, ln1_b, ln2_g,
        ln2_b, w_router_group, b_router_group, w_router_expert, b_router_expert, w_expert_gate,
        w_expert_up, w_expert_down,
    )
    return second_block(
        x, c_2, ctx_2, c_ctx_2, ada_w_2, ada_b_2, ffn1_w_in_2, ffn1_w_out_2, ffn2_w_in_2,
        ffn2_w_out_2, even_w_in_2, gla_wg2_f_2, gla_bg_f_2, gla_wg2_b_2, gla_bg_b_2,
        gla_norm_g_2, mla_q_norm_g_2, mla_kv_norm_g_2, mla_w_uq_2, mla_w_ukv_2, even_w_out_2,
        na_w_in_2, na_rpb_2, na_w_out_2,
    )


_drawn_inputs = setup_inputs


def setup_inputs(seed=0):
    import zlib

    import numpy as np

    out = dict(_drawn_inputs(seed))
    spreads = {}
    factors = {'ctx': 3.426,
     'b_gate': 3.067,
     'conv_b': 5.387,
     'd_skip': 8.0,
     'b_router_group': 8.0,
     'b_router_expert': 3.37,
     'gla_wg2_b_2': 2.858,
     'gla_norm_g_2': 8.0,
     'mla_q_norm_g_2': 8.0,
     'mla_kv_norm_g_2': 8.0,
     'na_rpb_2': 5.151}
    for name, (base, spread) in spreads.items():
        noise = np.random.default_rng([zlib.crc32(name.encode()), seed]).standard_normal(out[name].shape)
        drawn = base * np.exp(spread * noise) if base else spread * noise
        out[name] = __import__('jax').numpy.asarray(drawn.astype(out[name].dtype))
    for name, factor in factors.items():
        out[name] = (out[name] * factor).astype(out[name].dtype)
    return out
```

```python
from contextlib import ExitStack

import concourse.bass as bass
from concourse import mybir
import numpy as np

F32 = mybir.dt.float32
F32R = mybir.dt.float32r
U32 = mybir.dt.uint32
ALU = mybir.AluOpType
ACT = mybir.ActivationFunctionType
AX = mybir.AxisListType
MUL, ADD, SUB, MIN, MAX = ALU.mult, ALU.add, ALU.subtract, ALU.min, ALU.max
ALPHA1 = 2.0 ** 0.25
ALPHA2 = 4.0 ** 0.25
NSLOT = 3
SLOT = 2048

VEC = [("c", 8), ("cc", 8), ("b_ada", 48), ("b_gate", 16), ("conv_w", 120), ("conv_b", 24), ("ng", 16),
       ("pscale", 8), ("ln1g", 8), ("ln1b", 8), ("ln2g", 8), ("ln2b", 8), ("dskip", 16), ("dtb", 1),
       ("alog", 1), ("c2", 8), ("cc2", 8), ("ada_b", 144), ("bgf", 2), ("bgb", 2), ("gng", 1), ("qng", 3),
       ("kvng", 1)]
VOFF, _n = {}, 0
for _k, _c in VEC:
    VOFF[_k] = _n
    _n += _c
NVEC = _n

CST = [("ident", 128), ("triu", 128), ("tril", 128), ("rsw", 64), ("cos", 256), ("sin", 256), ("pool", 1024),
       ("namask", 64), ("glam", 15 * 128), ("iota8", 8),
       ("iotar", 128), ("iotac", 1)]
COFF, _n = {}, 0
for _k, _c in CST:
    COFF[_k] = _n
    _n += _c
NCST = _n


def constants():
    out = np.zeros((128, NCST), np.float32)

    def put(key, a):
        out[:a.shape[0], COFF[key]:COFF[key] + a.shape[1]] = a

    i = np.arange(128)
    put("ident", np.eye(128, dtype=np.float32))
    put("triu", (i[:, None] <= i[None, :]).astype(np.float32))
    put("tril", (i[:, None] >= i[None, :]).astype(np.float32))
    r = np.zeros((64, 64), np.float32)
    for a in range(32):
        r[2 * a + 1, 2 * a] = -1.0
        r[2 * a, 2 * a + 1] = 1.0
    put("rsw", np.concatenate([r, r]))
    t = np.arange(256)
    inv = (np.float32(10000.0) ** (-np.arange(16, dtype=np.float32) / np.float32(16))).astype(np.float32)
    ang = np.concatenate([(t // 64).astype(np.float32)[:, None] * inv, (t % 64).astype(np.float32)[:, None] * inv], -1)
    put("cos", np.tile(np.repeat(np.cos(ang).T, 2, axis=0), (2, 1)).astype(np.float32))
    put("sin", np.tile(np.repeat(np.sin(ang).T, 2, axis=0), (2, 1)).astype(np.float32))
    p = np.zeros((4, 4, 64), np.float32)
    for g, k in enumerate((2, 4, 8, 16)):
        def cnt(n):
            a = np.arange(n)
            return (np.clip(a - k // 2 + k, 0, n) - np.clip(a - k // 2, 0, n)).astype(np.float32)
        p[g] = 1.0 / (cnt(4)[:, None] * cnt(64)[None, :])
    put("pool", np.broadcast_to(p.reshape(1, 1024), (128, 1024)))
    c = np.arange(128) % 64
    s = np.clip(c - 8, 0, 48)[:, None]
    k = np.arange(64)[None, :]
    put("namask", np.where((k >= s) & (k < s + 16), 0.0, -1e30).astype(np.float32))
    m = np.zeros((128, 15, 128), np.float32)
    for lv in range(7):
        h = 1 << lv
        same = (i[:, None] // (2 * h)) == (i[None, :] // (2 * h))
        low = (i[:, None] // h) % 2 == 0
        up = (i[None, :] // h) % 2 == 1
        m[:, lv] = same & low & up
        m[:, 7 + lv] = m[:, lv].T
    m[:, 14] = np.eye(128)
    put("glam", m.reshape(128, -1))
    put("iota8", np.broadcast_to(8.0 - np.arange(8, dtype=np.float32)[None], (128, 8)))
    put("iotar", np.broadcast_to(np.arange(128, dtype=np.float32)[None], (128, 128)))
    put("iotac", np.arange(128, dtype=np.float32)[:, None])
    return out


class Queue:

    def __init__(self, sem):
        self.sem, self.n, self.items, self.seen = sem, 0, [], {}

    def wait(self, *toks):
        for s, v in toks:
            if self.seen.get(id(s), 0) < v:
                self.seen[id(s)] = v
                self.items.append(lambda e, s=s, v=v: e.wait_ge(s, v))

    @property
    def last(self):
        return (self.sem, self.n)

    def run(self, eng):
        for f in self.items:
            f(eng)


class Vec(Queue):

    def do(self, f, *toks, c=1):
        if c and self.n:
            self.wait((self.sem, self.n))
        self.wait(*toks)
        self.n += 1
        self.items.append(lambda e: f(e).then_inc(self.sem, 1))
        return self.last

    def tt(self, o, a, b, op, *t, c=1):
        return self.do(lambda e: e.tensor_tensor(o, a, b, op), *t, c=c)

    def ts(self, o, a, s1, s2, o1, o2, *t, c=1):
        if s2 is None:
            return self.do(lambda e: e.tensor_scalar(o, a, s1, None, o1), *t, c=c)
        return self.do(lambda e: e.tensor_scalar(o, a, s1, s2, o1, o2), *t, c=c)

    def stt(self, o, a, s, b, o1, o2, *t, c=1):
        return self.do(lambda e: e.scalar_tensor_tensor(out=o, in0=a, scalar=s, in1=b, op0=o1, op1=o2), *t, c=c)

    def cp(self, o, a, *t, c=1):
        return self.do(lambda e: e.tensor_copy(o, a), *t, c=c)

    def rec(self, x, *t, c=1):
        return self.do(lambda e: e.reciprocal(x, x), *t, c=c)

    def red(self, o, a, op, *t, c=1):
        return self.do(lambda e: e.tensor_reduce(o, a, AX.X, op), *t, c=c)

    def act(self, o, a, f, *t, c=1, **k):
        return self.do(lambda e: e.activation(o, a, f, **k), *t, c=c)


class Mat(Queue):

    def mm(self, o, w, x, start, stop, skip=False):
        self.items.append([o, w, x, start, stop, skip, None])

    def tr(self, o, a, ident):
        self.items.append([o, a, ident, None, None, None, None])

    def mark(self):
        it = self.items[-1]
        if it[6] is None:
            self.n += 1
            it[6] = True
        return self.last

    def run(self, eng):
        for it in self.items:
            if not isinstance(it, list):
                it(eng)
                continue
            o, w, x, start, stop, skip, inc = it
            if start is None:
                r = eng.transpose(o, w, x)
            elif skip:
                r = eng.matmul(o, w, x, start=start, stop=stop, skip_group_check=True)
            else:
                r = eng.matmul(o, w, x, start=start, stop=stop)
            if inc:
                r.then_inc(self.sem, 1)


class Bank:
    def __init__(self, t):
        self.t, self.free = t, []


class Arena:
    def __init__(self, t, n):
        self.t, self.n, self.at = t, n, 0

    def get(self, *dims):
        k = 1
        for d in dims:
            k *= d
        a = self.t[:, self.at:self.at + k]
        self.at += k
        assert self.at <= self.n, (self.at, self.n)
        if len(dims) == 2:
            return a.rearrange("p (a b) -> p a b", a=dims[0])
        if len(dims) == 3:
            return a.rearrange("p (a b c) -> p a b c", a=dims[0], b=dims[1])
        return a


class Ring:

    def __init__(self, K, plan, sems):
        self.K, self.plan, self.asked, self.sems = K, plan, [], sems
        self.until = 10 ** 9
        self.loaded = self.cut = self.used = self.base = 0
        self.raw_free, self.done, self.part, self.cuts = {}, {}, {}, {}

    def spec(self, j):
        return self.plan[j]

    def advance(self):
        K = self.K
        while True:
            j = self.loaded
            moved = False
            if j < min(len(self.plan), self.until) and (j < self.base + NSLOT or j - NSLOT in self.raw_free):
                name, lead, row, kt, col, cols, split = self.plan[j]
                if j >= self.base + NSLOT:
                    K.D.wait(*self.raw_free[j - NSLOT])
                src = K.dram[name] if lead is None else K.dram[name][lead]
                src = src[row:row + kt * 128, col:col + cols].rearrange("(k p) n -> p k n", p=128)
                dst = K.RAW[:, j % NSLOT, 0:kt * cols].rearrange("p (k n) -> p k n", k=kt)
                K.dma(dst, src, self.sems[j % NSLOT])
                self.loaded += 1
                moved = True
            j = self.cut
            if j < self.loaded and j <= self.used + 2 and (j < self.base + NSLOT or j - NSLOT in self.done):
                name, lead, row, kt, col, cols, split = self.plan[j]
                here = (self.sems[j % NSLOT], 16 * (j // NSLOT + 1))
                if split:
                    n = kt * cols
                    free = self.done[j - NSLOT] if j >= self.base + NSLOT else []
                    raw = K.RAW[:, j % NSLOT, 0:n]
                    a = K.S.act(K.HR[:, j % NSLOT, 0:n], raw, ACT.Copy, here, *free, c=0)
                    b = K.V.tt(K.LR[:, j % NSLOT, 0:n], raw, K.HR[:, j % NSLOT, 0:n].bitcast(F32), SUB, here, a,
                               *free, c=0)
                    self.cuts[j] = [a, b]
                    self.raw_free[j] = [b]
                else:
                    self.cuts[j] = [here]
                self.cut += 1
                moved = True
            if not moved:
                return

    def get(self, *spec):
        self.asked.append(spec)
        j = len(self.asked) - 1
        if self.plan is None or j >= len(self.plan):
            self.plan = (self.plan or []) + [spec]
        assert self.plan[j] == spec and j < self.until, (j, self.plan[j], spec)
        self.used = j
        self.advance()
        assert self.cut > j, j
        return W(self, j, spec)


class W:
    def __init__(self, ring, j, spec):
        K = ring.K
        _, _, _, kt, _, cols, split = spec
        self.ring, self.j, self.split, self.toks = ring, j, split, ring.cuts[j]

        def view(t):
            return t[:, j % NSLOT, 0:kt * cols].rearrange("p (k n) -> p k n", k=kt)

        if split:
            self.hi, self.lo = view(K.HR), view(K.LR)
        else:
            self.f = view(K.RAW)

    def end(self, tok):
        self.ring.done[self.j] = [tok]
        if not self.split:
            self.ring.raw_free[self.j] = [tok]


class X3:

    def __init__(self, hi, lo):
        self.hi, self.lo, self.ready, self.free = hi, lo, [], []


class Kern:
    def __init__(self, nc, dram, plan, ctx):
        self.nc, self.dram, self.ctx = nc, dram, ctx
        sem = self.sem
        self.T, self.V, self.S, self.G = Mat(sem("s_pe")), Vec(sem("s_dve")), Vec(sem("s_act")), Vec(sem("s_pool"))
        self.D = Queue(None)
        plan = plan or {}
        self.plans, self.asked = plan, {}
        self.s_in, self.n_in, self.groups = None, 0, 0
        self.ring = Ring(self, plan.get("main"), [sem(f"s_ring{i}") for i in range(NSLOT)])
        self.ring.until = plan.get("split", 10 ** 9)
        self.asked["main"] = self.ring.asked
        sb = self.sb
        self.RAW = sb("RAW", [128, NSLOT, SLOT], F32)
        self.HR = sb("HR", [128, NSLOT, SLOT], F32R)
        self.LR = sb("LR", [128, NSLOT, SLOT], F32R)
        self.X = sb("X", [128, 8, 512], F32)
        self.AH = sb("AH", [128, 4096], F32R)
        self.AL = sb("AL", [128, 4096], F32R)
        self.vec = sb("vec", [128, NVEC], F32)
        self.ident = sb("ident", [128, 128], F32)
        self.onesD = sb("onesD", [128, 128], F32)
        self.ones = sb("ones", [128, 256], F32)
        self.eps = sb("eps", [128, 2], F32)
        self.mod1 = sb("mod1", [128, 48, 2], F32)
        self.mod2 = [sb(f"mod2{i}", [128, 72, 2], F32) for i in range(2)]
        self.csil = sb("csil", [128, 8, 4], F32)
        self.CS = sb("CS", [128, 184], F32R)
        self.mrow = [sb(f"mrow{i}", [8, 256], F32) for i in range(2)]
        self.mst = [sb(f"mst{i}", [128, 8, 8], F32) for i in range(2)]
        self.row_free, self.mst_free, self.jobs, self.nrow = [[], []], [[], []], [], 0
        self.lo, self.hi = 0, 8
        self.banks = [Bank(ctx.enter_context(nc.psum_tensor(f"ps{i}", [128, 512], F32))) for i in range(8)]
        self.bi = 0
        self.A = X3(self.AH, self.AL)

    def sem(self, name):
        return self.ctx.enter_context(self.nc.semaphore(name))

    def sb(self, name, shape, dt, ctx=None):
        return (ctx or self.ctx).enter_context(self.nc.sbuf_tensor(name, shape, dt))

    def v(self, key, i=0, n=1):
        return self.vec[:, VOFF[key] + i:VOFF[key] + i + n]

    def dma(self, dst, src, sem):
        self.D.items.append(lambda e: e.dma_start(dst, src).then_inc(sem, 16))

    def load(self, dst, src):
        if self.s_in is None:
            self.s_in, self.n_in = self.sem(f"s_in{self.groups}"), 0
            self.groups += 1
        self.dma(dst, src, self.s_in)
        self.n_in += 16

    def landed(self):
        t, self.s_in = (self.s_in, self.n_in), None
        return t

    def cst(self, key, dst, rows=128, off=0, n=None):
        n = n or dict(CST)[key]
        self.load(dst, self.dram["cst"][0:rows, COFF[key] + off:COFF[key] + off + n])

    def phase(self, name):
        pass

    def step(self, n=1):
        while n and self.jobs:
            if next(self.jobs[0], None) is None:
                self.jobs.pop(0)
            else:
                n -= 1

    def finish(self, job):
        while job in self.jobs:
            self.step()
        self.V.wait(self.V.last)
        return self.V.last

    def bank(self, lo=None, hi=None):
        lo, hi = self.lo if lo is None else lo, self.hi if hi is None else hi
        self.bi += 1
        if self.bi >= hi or self.bi < lo:
            self.bi = lo
        b = self.banks[self.bi]
        self.T.wait(*b.free)
        return b

    def barrier(self, pe=True):
        ends = [q.last for q in (self.T, self.V, self.S, self.G) if q.n]
        for q in (self.T, self.V, self.S, self.G, self.D)[0 if pe else 1:]:
            q.wait(*ends)

    def prod(self, o, w, ws, x, xs, first, last, skip=False):
        if w.split:
            self.T.mm(o, w.hi[ws], x.hi[xs], first, False, skip)
            self.T.mm(o, w.hi[ws], x.lo[xs], False, False, skip)
            self.T.mm(o, w.lo[ws], x.hi[xs], False, last, skip)
        else:
            self.T.mm(o, w.f[ws], x[xs], first, last, skip)

    def linear(self, name, lead, kt, c0, nt, x, n, evac, row=0, split=True, xtoks=(), bg=True, per=None):
        T = self.T
        per = per or SLOT // kt // 128
        xk = xtoks if xtoks and isinstance(xtoks[0], list) else []
        if xk:
            xtoks = ()
        for a in range(0, nt, per):
            m = min(per, nt - a)
            w = self.ring.get(name, lead, row, kt, c0 + a * 128, m * 128, split)
            T.wait(*w.toks, *xtoks)
            for i in range(m):
                b = self.bank()
                for k in range(kt):
                    if k < len(xk) and a == 0 and i == 0:
                        T.wait(*xk[k])
                    self.prod(b.t[:, 0:n], w, (slice(None), k, slice(i * 128, i * 128 + 128)), x,
                              (slice(None), k, slice(0, n)), k == 0, k == kt - 1)
                tok = T.mark()
                if i == m - 1:
                    w.end(tok)
                b.free = evac(a + i, b.t[:, 0:n], tok)
            if bg:
                self.step()
        return T.last

    def split(self, dst_hi, dst_lo, src, *toks):
        a = self.S.act(dst_hi, src, ACT.Copy, *toks, c=0)
        b = self.V.tt(dst_lo, src, dst_hi.bitcast(F32), SUB, a, *toks, c=0)
        return [a, b]

    def reopen(self):
        self.ring.until = 10 ** 9
        self.asked["split"] = len(self.ring.asked)
        self.ring.base = len(self.ring.asked)

    def branch(self, name, flag, taken, body):
        self.barrier()
        main = self.T, self.V, self.S, self.G, self.D, self.ring
        sem = self.sem
        self.T, self.V, self.S, self.G = Mat(sem(f"{name}_pe")), Vec(sem(f"{name}_dve")), \
            Vec(sem(f"{name}_act")), Vec(sem(f"{name}_pool"))
        self.D = Queue(None)
        self.ring = Ring(self, self.plans.get(name), [sem(f"{name}_ring{i}") for i in range(NSLOT)])
        self.asked[name] = self.ring.asked
        for b in self.banks:
            b.free = []
        self.A.free = []
        body()
        self.barrier()
        for b in self.banks:
            b.free = []
        self.A.free = []
        subs = self.T, self.V, self.S, self.G, self.D
        self.T, self.V, self.S, self.G, self.D, self.ring = main
        for q, sub in zip(main, subs):
            def part(e, sub=sub):
                v = e.value_load(flag)
                with e.If(v > 0) if taken else e.If(v < 1):
                    sub.run(e)
            q.items.append(part)

    def mean_begin(self, n):
        self.hi = 7
        self.mb = self.banks[7]
        self.mb_n, self.mb_k = n, 0
        self.T.wait(*self.mb.free)

    def mean_add(self, xk, tok):
        self.T.wait(tok)
        self.T.mm(self.mb.t[:, 0:self.mb_n], self.onesD[:, :], xk, self.mb_k == 0, self.mb_k == 7)
        self.mb_k += 1
        self.T.mark()

    def layer_norm(self, x, n, eps, sq, rs, post):
        T, V, S = self.T, self.V, self.S
        b, b2 = self.mb, self.banks[6]
        self.hi = 6
        T.wait(*b2.free)
        t = T.last
        for k in range(8):
            t1 = V.tt(x[:, k, :], x[:, k, :], b.t[:, 0:n], SUB, t, c=0)
            t2 = S.act(sq[:, k, :], x[:, k, :], ACT.Square, t1, c=0)
            T.wait(t2)
            T.mm(b2.t[:, 0:n], self.onesD[:, :], sq[:, k, :], k == 0, k == 7)
        b.free = [t1]
        t = T.mark()
        t = S.act(rs, b2.t[:, 0:n], ACT.Sqrt, t, bias=self.eps[:, eps:eps + 1])
        b2.free = [t]
        self.hi = 8
        t = V.rec(rs, t)
        out = []
        for k in range(8):
            t1 = V.tt(x[:, k, :], x[:, k, :], rs, MUL, t, c=0)
            out.append(post(k, t1) or [t1])
        return out

    def transpose_to(self, blocks, width):
        b = self.bank()
        for src, col in blocks:
            q, p = src.shape[0], src.shape[1]
            sp = src.start_partition()
            self.T.tr(b.t[0:p, col:col + q], src, self.ident[sp:sp + q, sp:sp + q])
        return b, self.T.mark()


def setup(K):
    T, V, S, G, D = K.T, K.V, K.S, K.G, K.D
    K.load(K.vec[:, :], K.dram["vec"])
    K.cst("ident", K.ident[:, :])
    K.load(K.X[:, :, 256:512], K.dram["xT"].rearrange("(k p) n -> p k n", p=128))
    K.load(K.X[:, :, 0:256], K.dram["ctxT"].rearrange("(k p) n -> p k n", p=128))
    t = K.t_in = K.landed()
    G.do(lambda e: e.memset(K.onesD[:, :], 1.0 / 1024), c=0)
    G.do(lambda e: e.memset(K.ones[:, :], 1.0), c=0)
    G.do(lambda e: e.memset(K.eps[:, 0:1], 1e-5), c=0)
    G.do(lambda e: e.memset(K.eps[:, 1:2], 1e-6), c=0)
    for i, key in enumerate(("c", "cc", "c2", "cc2")):
        t = S.act(K.csil[:, :, i], K.v(key, 0, 8), ACT.Silu, t, c=0)
    V.do(lambda e: e.memset(K.CS[:, :].bitcast(F32), 0.0), c=0)
    cs = K.CS[:, 0:64].rearrange("p (k c) -> p k c", k=8)
    V.cp(cs[:, :, 0:4], K.csil[:, :, :], t)
    K.t_cs = V.tt(cs[:, :, 4:8], K.csil[:, :, :], cs[:, :, 0:4].bitcast(F32), SUB)
    K.barrier()


def conditioning(K, name, lead, t0, nt, v0, bias, dst, fix):
    T, V, S = K.T, K.V, K.S
    for g in range(t0, t0 + nt, 8):
        j = (g // 8) % 2
        st = K.mst[j]
        for a in range(0, 8, 2):
            w = K.ring.get(name, lead, 0, 8, (g + a) * 128, 256, True)
            T.wait(K.t_cs, *w.toks)
            b = K.bank()
            for k in range(8):
                T.mm(b.t[:, 0:256], K.CS[:, 8 * k:8 * k + 128], w.hi[:, k, :], k == 0, False)
                T.mm(b.t[:, 0:256], K.CS[:, 8 * k:8 * k + 128], w.lo[:, k, :], False, k == 7)
            tk = T.mark()
            w.end(tk)
            i = K.nrow % 2
            K.nrow += 1
            row = K.mrow[i]
            t = S.act(row[:, :], b.t[0:8, 0:256], ACT.Copy, tk, *K.row_free[i], c=0)
            b.free = [t]
            yield True
            T.wait(t)
            b, tk = K.transpose_to([(row[:, q * 128:q * 128 + 128], 8 * q) for q in range(2)], 8)
            K.row_free[i] = [tk]
            t = S.act(st[:, a:a + 2, :], b.t[:, 0:16].rearrange("p (q c) -> p q c", q=2), ACT.Copy, tk,
                      *K.mst_free[j], c=0)
            b.free = [t]
        o = dst[:, g:g + 8, :]
        V.tt(o, st[:, :, v0:v0 + 2], st[:, :, 4 + v0:6 + v0], ADD, t)
        K.mst_free[j] = [V.last]
        V.tt(o, o, bias[:, g:g + 8].unsqueeze(2).broadcast_to([128, 8, 2]), ADD)
        how = fix.get(g // 8)
        if how == 1:
            V.ts(o, o, 1.0, None, ADD, None)
        elif how == 2:
            V.ts(o, o, 0.5, None, MUL, None)


def scaled_split(K, src, k, n, dst, mods, tmp, used, toks):
    S = K.S
    halves = [(0, 256, 1), (256, 512, 0)] if n == 512 else [(0, 256, 0)]
    tb = tmp[:, k % 2, 0:n]
    for a, z, v in halves:
        sc, sh = mods(k, v)
        t = S.act(tb[:, a:z], src[:, a:z], ACT.Identity, *toks, *used[k % 2], *dst.free, c=0, scale=sc, bias=sh)
    used[k % 2] = K.split(dst.hi[:, k * n:(k + 1) * n], dst.lo[:, k * n:(k + 1) * n], tb, t)
    return used[k % 2]


def modulated(K, src, dst, n, sc, sh, tmp, toks):
    V = K.V
    used = [[], []]
    ready = []
    halves = [(0, 256, 1), (256, 512, 0)] if n == 512 else [(0, 256, 0)]
    for k in range(8):
        tb = tmp[:, k % 2, 0:n]
        for a, z, v in halves:
            t = V.ts(tb[:, a:z], src[:, k, a:z], sc(k, v), sh(k, v), MUL, ADD, *toks, *used[k % 2],
                     *dst.free, c=0)
        used[k % 2] = K.split(dst.hi[:, k * n:(k + 1) * n], dst.lo[:, k * n:(k + 1) * n], tb, t)
        ready = used[k % 2]
    dst.ready = ready
    return ready


class View3:
    split = True

    def __init__(self, x, kt, n):
        self.hi = x.hi[:, 0:kt * n].rearrange("p (k n) -> p k n", k=kt)
        self.lo = x.lo[:, 0:kt * n].rearrange("p (k n) -> p k n", k=kt)


def block_one(K, stop=None):
    T, V, S, G, D = K.T, K.V, K.S, K.G, K.D
    ctx = ExitStack()
    NAR = 19900
    A = Arena(K.sb("ar1", [128, NAR], F32, ctx), NAR)
    X, A3 = K.X, K.A
    mod = K.mod1
    fix = {1: 1, 4: 1}
    K.phase("start")
    first = conditioning(K, "w_ada", None, 0, 16, 0, K.v("b_ada", 0, 48), mod, fix)
    K.jobs.append(first)
    t_mod = K.finish(first)
    rest = conditioning(K, "w_ada", None, 16, 32, 0, K.v("b_ada", 0, 48), mod, fix)
    K.jobs.append(rest)
    fix2 = {1: 1, 4: 1, 7: 1, 2: 2, 8: 2}
    K.ada2 = [conditioning(K, "ada_w", l, 0, 72, 2, K.v("ada_b", 72 * l, 72), K.mod2[l], fix2) for l in range(2)]
    K.jobs.append(K.ada2[0])

    def mcol(i):
        return lambda k, v: mod[:, 8 * i + k, v:v + 1]

    xsC, xsL = A.get(16, 256), A.get(16, 256)
    BT, CT = A.get(4, 512), A.get(4, 256)
    dtT, aT, acs = A.get(512), A.get(512), A.get(512)
    tokC, tokL, dtL = A.get(2, 64), A.get(2, 64), A.get(2, 64)
    triu, tril = A.get(128), A.get(128)
    K.cst("triu", triu)
    K.cst("tril", tril)
    tri_t = K.landed()
    base = A.at
    tmp = A.get(2, 512)
    h = View3(A3, 8, 512)
    used, ht = [[], []], []
    for k in range(8):
        ht.append(scaled_split(K, X[:, k, :], k, 512, A3, lambda k, v: (mcol(1)(k, v), mcol(0)(k, v)), tmp, used,
                               [t_mod, K.t_in]))
    K.phase("xbc")
    e1, e2, e3 = A.get(512), A.get(512), A.get(512)
    negA = A.get(1)
    r = slice(0, 64)
    K.linear("w_in", None, 8, 5120, 1, h, 512, lambda m, ps, tok: [
        V.ts(dtT[r], ps[r, :], K.v("dtb")[r], None, ADD, None, tok, c=0)], xtoks=ht)
    t = V.stt(e1[r], dtT[r], -1.0, dtT[r], MUL, MIN)
    t = S.act(e1[r], e1[r], ACT.Exp, t)
    t = V.ts(e2[r], e1[r], 1.0, None, ADD, None, t)
    t = S.act(e3[r], e2[r], ACT.Ln, t)
    t = V.ts(aT[r], e2[r], 1.0, None, ALU.is_equal, None, t)
    t = V.stt(e2[r], e2[r], -1.0, aT[r], ADD, ADD, t)
    t = V.tt(e3[r], e3[r], aT[r], ADD)
    t = V.rec(e2[r])
    t = V.tt(e3[r], e3[r], e1[r], MUL)
    t = V.tt(e3[r], e3[r], e2[r], MUL)
    t = V.stt(dtT[r], dtT[r], 0.0, e3[r], MAX, ADD)
    t = S.act(negA[r], K.v("alog")[r], ACT.Exp)
    t = V.ts(negA[r], negA[r], -1.0, None, MUL, None, t)
    t = V.ts(aT[r], dtT[r], negA[r], None, MUL, None, t)
    for s in (0, 256):
        t = V.do(lambda e, s=s: e.tensor_tensor_scan(acs[0:32, s:s + 256], K.ones[0:32, 0:256],
                                                     aT[0:32, s:s + 256], 0.0, MUL, ADD))
        t = V.do(lambda e, s=s: e.tensor_tensor_scan(acs[32:64, s:s + 256][:, ::-1], K.ones[32:64, 0:256],
                                                     aT[32:64, s:s + 256][:, ::-1], 0.0, MUL, ADD), c=0)
    ta = S.act(e1[0:32, 0:256], acs[0:32, 0:256], ACT.Exp, t, bias=acs[0:32, 255:256], scale=-1.0)
    ta = S.act(e1[32:64, 0:256], acs[32:64, 0:256], ACT.Exp, t, bias=acs[32:64, 0:1], scale=-1.0)
    t = V.tt(e1[r, 0:256], e1[r, 0:256], dtT[r, 0:256], MUL, ta)
    T.wait(t)
    b, tk = K.transpose_to([(src[0:64, s + j * 128:s + j * 128 + 128], 64 * (2 * i + j))
                            for i, (src, s) in enumerate(((e1, 0), (acs, 256), (dtT, 256))) for j in range(2)], 64)
    for i, dst in enumerate((tokC, tokL, dtL)):
        t = V.cp(dst, b.t[:, 128 * i:128 * i + 128].rearrange("p (j c) -> p j c", j=2), tk, c=0)
    b.free = [t]
    t_tok = t
    pads = [A.get(2, 260) for _ in range(3)]
    accs = [A.get(2, 256) for _ in range(2)]
    zt = []
    for p in pads:
        G.do(lambda e, p=p: e.memset(p[:, :, 0:2], 0.0), c=0)
        zt.append(G.do(lambda e, p=p: e.memset(p[:, :, 258:260], 0.0), c=0))
    pad_free, acc_free = [[z] for z in zt], [[], []]

    def conv_tile(m, ps, tok):
        p, a = pads[m % 3], accs[m % 2]
        lat = m >= 20
        sl = slice(1, 2) if lat else slice(0, 2)
        n = 1 if lat else 2
        src = ps.rearrange("p (s n) -> p s n", s=n)
        t1 = S.act(p[:, sl, 2:258], src, ACT.Copy, tok, *pad_free[m % 3], c=0)
        t2 = V.ts(a[:, sl, :], p[:, sl, 0:256], K.v("conv_w", m), K.v("conv_b", m), MUL, ADD, t1,
                  *acc_free[m % 2], c=0)
        for i in range(1, 5):
            t2 = V.stt(a[:, sl, :], p[:, sl, i:i + 256], K.v("conv_w", 24 * i + m), a[:, sl, :], MUL, ADD)
        pad_free[m % 3] = [t2]
        if m < 16:
            S.act(xsC[:, m, :], a[:, 0, :], ACT.Silu, t2, c=0)
            t3 = S.act(xsL[:, m, :], a[:, 1, :], ACT.Silu, t2, c=0)
        elif m < 20:
            t3 = S.act(BT[:, m - 16, :].rearrange("p (s n) -> p s n", s=2), a[:, :, :], ACT.Silu, t2, c=0)
        else:
            t3 = S.act(CT[:, m - 20, :], a[:, 1, :], ACT.Silu, t2, c=0)
        acc_free[m % 2] = [t3]
        return [t1]

    K.linear("w_in", None, 8, 2048, 20, h, 512, conv_tile, xtoks=ht)
    hl = HalfView(h, 256)
    K.linear("w_in", None, 8, 4608, 4, hl, 256, lambda m, ps, tok: conv_tile(20 + m, ps, tok), xtoks=ht)
    K.barrier()
    K.phase('ssd')
    A.at = base
    Bk = A.get(2, 128)
    xd = A.get(2, 2, 512)
    S0 = A.get(2, 512)
    CB = A.get(2, 384)
    SEG = [A.get(384) for _ in range(3)]
    EC = [A.get(256) for _ in range(3)]
    seg_free = [[] for _ in range(4)]
    n = 0
    s0_t, yfree = [], []
    for g in range(4):
        b, tk = K.transpose_to([(BT[:, g, j * 128:j * 128 + 128], 128 * j) for j in range(2)], 128)
        tB = S.act(Bk, b.t[:, 0:256].rearrange("p (j c) -> p j c", j=2), ACT.Copy, tk, *s0_t, c=0)
        b.free = [tB]
        prev_s = s0_t
        for j in range(2):
            b, tk = K.transpose_to([(xsC[:, 4 * g + q, j * 128:j * 128 + 128], 128 * q) for q in range(4)], 128)
            for d in range(2):
                wcol = tokC[:, j, 32 * d + 8 * g:32 * d + 8 * g + 8].unsqueeze(2).broadcast_to([128, 8, 64])
                t = V.tt(xd[:, d, j, :].rearrange("p (h c) -> p h c", h=8),
                         b.t[:, :].rearrange("p (h c) -> p h c", h=8), wcol, MUL, tk, *prev_s, *yfree, c=0)
            b.free = [t]
        T.wait(t, tB)
        for d in range(2):
            b = K.bank()
            for j in range(2):
                T.mm(b.t[:, :], Bk[:, j, :], xd[:, d, j, :], j == 0, j == 1)
            tk = T.mark()
            ts = S.act(S0[:, d, :], b.t[:, :], ACT.Copy, tk, *prev_s, *yfree, c=0)
            b.free = [ts]
        s0_t = [ts]
        for j in range(2):
            b = K.bank()
            T.mm(b.t[:, 0:256], BT[:, g, 256 + j * 128:384 + j * 128], CT[:, g, :], True, True)
            tk = T.mark()
            if j == 0:
                V.tt(CB[:, 0, 0:128], b.t[:, 0:128], triu, MUL, tk, tri_t, *yfree, c=0)
                V.cp(CB[:, 0, 128:256], b.t[:, 128:256], c=0)
                t = V.tt(CB[:, 1, 0:128], b.t[:, 0:128], tril, MUL, c=0)
            else:
                V.tt(CB[:, 0, 256:384], b.t[:, 128:256], triu, MUL, tk, c=0)
                V.cp(CB[:, 1, 128:256], b.t[:, 0:128], c=0)
                t = V.tt(CB[:, 1, 256:384], b.t[:, 128:256], tril, MUL, c=0)
            b.free = [t]
        tCB = t
        for j in range(2):
            b, tk = K.transpose_to([(xsL[:, 4 * g + q, j * 128:j * 128 + 128], 128 * q) for q in range(4)], 128)
            for d in range(2):
                wcol = dtL[:, j, 32 * d + 8 * g:32 * d + 8 * g + 8].unsqueeze(2).broadcast_to([128, 8, 64])
                t = V.tt(xd[:, d, j, :].rearrange("p (h c) -> p h c", h=8),
                         b.t[:, :].rearrange("p (h c) -> p h c", h=8), wcol, MUL, tk, T.last, c=0)
            b.free = [t]
        tx = t
        pend = []

        def head_products(item, yb):
            hh, d, i, tg, tq = item
            T.wait(tg, tq, tx, *s0_t)
            po = 64 * (hh % 2)
            o = yb.t[po:po + 64, :]
            c = (hh % 8) * 64
            T.mm(o[:, 0:256], S0[:, d, c:c + 64], EC[i], d == 0, False)
            for j in range(2):
                cols = (slice(0, 256) if j == 0 else slice(128, 256)) if d == 0 else \
                    (slice(0, 128) if j == 0 else slice(0, 256))
                so = (0 if j == 0 else 256) if d == 0 else (0 if j == 0 else 128)
                T.mm(o[:, cols], xd[:, d, j, c:c + 64], SEG[i][:, so:so + cols.stop - cols.start], False,
                     d == 1 and j == 1)
            seg_free[i] = [T.mark()]

        K.hi = 6
        todo = [(hh, d) for hh in range(8 * g, 8 * g + 8) for d in range(2)]
        yb = None
        for q in range(len(todo) + 2):
            if q < len(todo):
                hh, d = todo[q]
                i = n % 3
                n += 1
                row = 32 * d + hh
                b = K.bank()
                T.mm(b.t[:, 0:256], K.ident[0:64, row:row + 1].broadcast_to([64, 128]), acs[0:64, 256:512],
                     True, True)
                tk = T.mark()
                if d == 0:
                    parts = [(slice(0, 256), slice(0, 256), 0), (slice(128, 256), slice(256, 384), 1)]
                else:
                    parts = [(slice(0, 128), slice(0, 128), 0), (slice(0, 256), slice(128, 384), 1)]
                te = S.act(EC[i], b.t[:, 0:256], ACT.Exp, tk, *seg_free[i], c=0)
                for src, dst, j in parts:
                    t = V.ts(SEG[i][:, dst], b.t[:, src], tokL[:, j, row:row + 1], 0.0, SUB, MIN, te,
                             *seg_free[i], c=0)
                b.free = [te, t]
                t2 = S.act(SEG[i], SEG[i], ACT.Exp, t, c=0)
                tq = G.tt(EC[i], EC[i], CT[:, g, :], MUL, te, c=0)
                tg = V.tt(SEG[i], SEG[i], CB[:, d, :], MUL, t2, tCB, c=0) if d == 0 else \
                    G.tt(SEG[i], SEG[i], CB[:, d, :], MUL, t2, tCB, c=0)
                pend.append((hh, d, i, tg, tq))
            if q % 2 == 1:
                K.step()
            if q >= 2:
                item = pend.pop(0)
                if item[0] % 2 == 0 and item[1] == 0:
                    yb = K.bank(6, 8)
                head_products(item, yb)
                if item[0] % 2 == 1 and item[1] == 1:
                    m = item[0] // 2
                    t = V.stt(xsL[:, m, :], xsL[:, m, :], K.v("dskip", m), yb.t[:, 0:256], MUL, ADD, T.last,
                              c=0)
                    yb.free = [t]
        K.hi = 8
        yfree = [T.last]
        s0_t = [ts, T.last]
    K.barrier()
    K.phase('z')
    A.at = base
    gates = xsC
    u = BT.rearrange("p a b -> p (a b)").rearrange("p (m n) -> p m n", m=8)
    sil = [A.get(256) for _ in range(2)]
    sq = [A.get(256) for _ in range(2)]
    sil_free = [[], []]
    ssq = K.banks[7]
    T.wait(*ssq.free)
    sqt = []

    def z_tile(m, ps, tok):
        i = m % 2
        t1 = S.act(sil[i], ps, ACT.Silu, tok, *sil_free[i], c=0)
        t2 = V.tt(xsL[:, m, :], xsL[:, m, :], sil[i], MUL, t1, c=0)
        t3 = S.act(sq[i], xsL[:, m, :], ACT.Square, t2, *(sqt[m - 2:m - 1] if m >= 2 else []), c=0)
        sil_free[i] = [t2]
        T.wait(t3)
        T.mm(ssq.t[:, 0:256], K.onesD[:, :], sq[i], m == 0, m == 15)
        sqt.append(T.mark())
        return [t1]

    K.hi = 7
    K.linear("w_in", None, 8, 0, 16, hl, 256, z_tile)
    K.hi = 8
    rz = A.get(256)
    t = S.act(rz, ssq.t[:, 0:256], ACT.Sqrt, T.last, bias=K.eps[:, 0:1], scale=0.5)
    ssq.free = [t]
    t_rz = V.rec(rz, t)
    K.linear("w_in", None, 8, 5184, 8, hl, 256,
             lambda m, ps, tok: [S.act(u[:, m, :], ps, ACT.Copy, tok, c=0)])
    t_u = S.last
    K.linear("w_in", None, 8, 6208, 16, hl, 256,
             lambda m, ps, tok: [S.act(gates[:, m, :], ps, ACT.Sigmoid, tok, c=0, bias=K.v("b_gate", m))])
    t_g = S.last
    A3.free = [T.last]
    yv = View3(A3, 16, 256)
    ynt = []
    for m in range(16):
        t = V.ts(xsL[:, m, :], xsL[:, m, :], K.v("ng", m), None, MUL, None, c=0)
        ynt = K.split(yv.hi[:, m, :], yv.lo[:, m, :], xsL[:, m, :], t, *A3.free)
    merged = A.get(8, 256)

    def a_tile(m, ps, tok):
        V.tt(merged[:, m, :], ps, rz, MUL, tok, t_rz, c=0)
        t = V.last
        G.tt(merged[:, m, :], merged[:, m, :], gates[:, m, :], MUL, t, t_g, c=0)
        return [t]

    K.linear("w_branch_a", None, 16, 0, 8, yv, 256, a_tile, xtoks=ynt)
    A3.free = [T.last]
    K.phase('pool')
    pc = A.get(1024)
    K.cst("pool", pc)
    t_pc = K.landed()
    yp = xsL[:, 0:8, :]
    P0 = [A.get(4, 80) for _ in range(2)]
    P1 = [A.get(4, 80) for _ in range(2)]
    for p in P0:
        t_z = G.do(lambda e, p=p: e.memset(p, 0.0), c=0)
    for p in P1:
        t_z = G.do(lambda e, p=p: e.memset(p, 0.0), c=0)
    G.wait(t_z, t_u, t_pc)
    df = X[:, :, 0:256]
    for m in range(8):
        k = (2, 4, 8, 16)[m // 2]
        uu = u[:, m, :].rearrange("p (r c) -> p r c", r=4)
        a, b2 = P0[m % 2], P1[m % 2]
        c = slice(8, 72)
        if k == 2:
            G.tt(a[:, 1:4, c], uu[:, 1:4, :], uu[:, 0:3, :], ADD)
            G.cp(a[:, 0:1, c], uu[:, 0:1, :])
        elif k == 4:
            G.tt(a[:, 0, c], uu[:, 0, :], uu[:, 1, :], ADD)
            G.tt(a[:, 3, c], uu[:, 2, :], uu[:, 3, :], ADD)
            G.tt(a[:, 1, c], a[:, 0, c], uu[:, 2, :], ADD)
            G.tt(a[:, 2, c], a[:, 3, c], uu[:, 1, :], ADD)
            G.tt(a[:, 2, c], a[:, 2, c], uu[:, 0, :], ADD)
            G.tt(a[:, 3, c], a[:, 3, c], uu[:, 1, :], ADD)
        else:
            G.tt(a[:, 0, c], uu[:, 0, :], uu[:, 1, :], ADD)
            G.tt(a[:, 0, c], a[:, 0, c], uu[:, 2, :], ADD)
            G.tt(a[:, 0, c], a[:, 0, c], uu[:, 3, :], ADD)
            G.cp(a[:, 1:4, c], a[:, 0:1, c].broadcast_to([128, 3, 64]))
        src, dst = a, b2
        G.tt(dst[:, :, 1:80], src[:, :, 0:79], src[:, :, 1:80], ADD)
        src, dst = dst, src
        sh, w_ = 1, 2
        while w_ < k:
            G.tt(dst[:, :, 8:72] if w_ * 2 == k else dst[:, :, 4:76],
                 (src[:, :, 8 - sh:72 - sh] if w_ * 2 == k else src[:, :, 4 - sh:76 - sh]),
                 (src[:, :, 8 + sh:72 + sh] if w_ * 2 == k else src[:, :, 4 + sh:76 + sh]), ADD)
            src, dst = dst, src
            sh, w_ = sh * 2, w_ * 2
        d = df[:, m, :].rearrange("p (r c) -> p r c", r=4)
        G.tt(d, src[:, :, 8:72], pc[:, (m // 2) * 256:(m // 2) * 256 + 256].rearrange("p (r c) -> p r c", r=4),
             MUL)
        t_df = G.tt(d, d, uu, SUB)
        if m % 2 == 0 or True:
            G.do(lambda e, a=a: e.memset(a, 0.0))
            G.do(lambda e, b2=b2: e.memset(b2, 0.0))
    for g in range(4):
        w = K.ring.get("pool_w", g, 0, 2, 0, 256, False)
        T.wait(*w.toks, t_df)
        for i in range(2):
            b = K.bank()
            for k in range(2):
                T.mm(b.t[:, 0:256], w.f[:, k, i * 128:i * 128 + 128], df[:, 2 * g + k, :], k == 0, k == 1)
            tk = T.mark()
            if i == 1:
                w.end(tk)
            m = 2 * g + i
            t = V.ts(yp[:, m, :], b.t[:, 0:256], K.v("pscale", m), None, MUL, None, tk, c=0)
            b.free = [t]
    v8 = View3(A3, 8, 256)
    for m in range(8):
        tt_ = K.split(v8.hi[:, m, :], v8.lo[:, m, :], yp[:, m, :], t, *A3.free)
    gt = [A.get(256) for _ in range(2)]
    gfree = [[], []]

    def b_tile(m, ps, tok):
        t1 = V.tt(gt[m % 2], ps, gates[:, 8 + m, :], MUL, tok, t_g, *gfree[m % 2], c=0)
        t2 = G.tt(merged[:, m, :], merged[:, m, :], gt[m % 2], ADD, t1)
        gfree[m % 2] = [t2]
        return [t1]

    K.linear("w_branch_b", None, 8, 0, 8, v8, 256, b_tile, xtoks=tt_)
    A3.free = [T.last]
    for m in range(8):
        tt_ = K.split(v8.hi[:, m, :], v8.lo[:, m, :], merged[:, m, :], G.last, *A3.free)
    XL = X[:, :, 256:512]

    t_a = G.ts(XL, XL, ALPHA1, None, MUL, None, *ht[7])
    K.finish(rest)
    K.mean_begin(256)
    K.linear("w_out", None, 8, 0, 8, v8, 256, residual(K, XL, lambda m, v: mod[:, 16 + m, 0:1], LAT, [t_a]),
             xtoks=tt_)
    A3.free = [T.last]
    K.barrier()
    ctx.close()
    ctx = ExitStack()
    NAR = 3200
    A = Arena(K.sb("ar2", [128, NAR], F32, ctx), NAR)
    sqb, rs = X[:, :, 0:256], A.get(256)
    h32 = A.get(8, 256)

    def post1(k, t):
        V.ts(XL[:, k, :], XL[:, k, :], K.v("ln1g", k), K.v("ln1b", k), MUL, ADD)

    K.layer_norm(XL, 256, 0, sqb, rs, post1)
    t = V.last
    K.phase("moe")
    if stop == "mix":
        ctx.close()
        return
    for k in range(8):
        t = V.ts(h32[:, k, :], XL[:, k, :], mod[:, 32 + k, 0:1], mod[:, 24 + k, 0:1], MUL, ADD, c=1)
    wr = A.get(8, 36)
    K.load(wr[:, :, 0:4], K.dram["w_rg"].rearrange("(k p) n -> p k n", p=128))
    for g in range(4):
        K.load(wr[:, :, 4 + 8 * g:12 + 8 * g], K.dram["w_re"][g].rearrange("(k p) n -> p k n", p=128))
    br = A.get(36)
    K.load(br[0:1, 0:4], K.dram["b_rg"])
    K.load(br[0:1, 4:36], K.dram["b_re"])
    iota = A.get(8)
    K.cst("iota8", iota)
    t_wr = t_io = K.landed()
    lg = A.get(2, 36)
    R = [A.get(8) for _ in range(12)]
    WT = A.get(2, 32)
    MK = A.get(2, 32)
    bsel = A.get(128)
    K.cst("triu", bsel)
    t_sel = K.landed()
    T.wait(t, t_wr)
    for j in range(2):
        b = K.bank()
        for k in range(8):
            T.mm(b.t[:, 0:36], h32[:, k, j * 128:j * 128 + 128], wr[:, k, :], k == 0, False)
        T.mm(b.t[:, 0:36], K.ones[0:1, 0:128], br[0:1, :], False, True)
        tk = T.mark()
        t = V.cp(lg[:, j, :], b.t[:, 0:36], tk, c=0)
        b.free = [t]
    V.wait(t_io)
    for j in range(2):
        L, LE = lg[:, j, 0:4], lg[:, j, 4:36].rearrange("p (g e) -> p g e", g=4)
        mx, oh, key, km, ex, sm, les, o1, o2, le2, w12, tmp8 = R

        def first_of(x, n_, out, m_):
            V.red(m_, x, MAX)
            V.ts(out, x, m_, None, ALU.is_ge, None)
            V.tt(key[:, 0:n_], out, iota[:, 0:n_], MUL)
            V.red(km[:, 0:1], key[:, 0:n_], MAX)
            V.ts(out, key[:, 0:n_], km[:, 0:1], None, ALU.is_equal, None)

        first_of(L, 4, oh[:, 0:4], mx[:, 0:1])
        V.ts(ex[:, 0:4], L, mx[:, 0:1], None, SUB, None)
        t = S.act(ex[:, 0:4], ex[:, 0:4], ACT.Exp, V.last)
        V.red(sm[:, 0:1], ex[:, 0:4], ADD, t)
        V.rec(sm[:, 0:1])
        V.ts(les, LE[:, 0, :], oh[:, 0:1], None, MUL, None)
        for g in range(1, 4):
            V.stt(les, LE[:, g, :], oh[:, g:g + 1], les, MUL, ADD)
        first_of(les, 8, o1, mx[:, 1:2])
        V.stt(le2, o1, -3e38, les, MUL, ADD)
        first_of(le2, 8, o2, mx[:, 2:3])
        V.tt(w12[:, 0:1], mx[:, 2:3], mx[:, 1:2], SUB)
        t = S.act(w12[:, 0:1], w12[:, 0:1], ACT.Exp, V.last)
        V.ts(w12[:, 1:2], w12[:, 0:1], 1.0, None, ADD, None, t)
        V.rec(w12[:, 1:2])
        V.tt(w12[:, 1:2], w12[:, 1:2], sm[:, 0:1], MUL)
        V.tt(w12[:, 2:3], w12[:, 1:2], w12[:, 0:1], MUL)
        V.ts(tmp8, o1, w12[:, 1:2], None, MUL, None)
        V.stt(tmp8, o2, w12[:, 2:3], tmp8, MUL, ADD)
        for g in range(4):
            V.ts(WT[:, j, 8 * g:8 * g + 8], tmp8, oh[:, g:g + 1], None, MUL, None)
        V.tt(tmp8, o1, o2, ADD)
        for g in range(4):
            V.ts(MK[:, j, 8 * g:8 * g + 8], tmp8, oh[:, g:g + 1], None, MUL, None)
    pos = A.get(2, 32)
    cnt = A.get(4)
    flag = K.sb("flag", [128, 1], mybir.dt.int32, ctx)
    V.tt(bsel, bsel, K.ident[:, :], SUB, t_sel)
    T.wait(V.last)
    b = K.bank()
    T.mm(b.t[:, 0:32], bsel, MK[:, 0, :], True, True)
    T.mm(b.t[:, 32:64], bsel, MK[:, 1, :], True, False)
    T.mm(b.t[:, 32:64], K.ones[:, 0:128], MK[:, 0, :], False, True)
    T.mm(b.t[:, 64:96], K.ones[:, 0:128], MK[:, 0, :], True, False)
    T.mm(b.t[:, 64:96], K.ones[:, 0:128], MK[:, 1, :], False, True)
    tk = T.mark()
    V.stt(pos, b.t[:, 0:64].rearrange("p (j e) -> p j e", j=2), 1.0, MK, ADD, MUL, tk)
    V.ts(pos, pos, -1.0, None, ADD, None)
    V.red(cnt[:, 0:1], b.t[:, 64:96], MAX)
    b.free = [V.last]
    V.ts(cnt[:, 0:1], cnt[:, 0:1], CAP, None, ALU.is_gt, None)
    V.cp(flag[:, :], cnt[:, 0:1])
    K.finish(K.ada2[0])
    jobs, K.jobs = K.jobs, []
    hold = ExitStack()
    K.branch("all", flag[0:1, 0:1], True, lambda: experts_all(K, v8, h32, WT, hold))
    hold.close()
    K.branch("some", flag[0:1, 0:1], False, lambda: experts_some(K, h32, WT, pos, hold))
    hold.close()
    K.reopen()
    K.jobs = jobs
    yb = K.banks[4:8]
    K.barrier()
    A3.free = [T.last]
    t_a = G.ts(XL, XL, ALPHA1, None, MUL, None)
    T.wait(t_a)
    K.lo, K.hi = 0, 8
    K.mb, K.mb_n, K.mb_k = K.banks[3], 256, 0
    T.wait(*K.mb.free)
    K.bi = 4
    tv = []
    for m in range(8):
        t = V.stt(XL[:, m, :], yb[m // 2].t[:, 256 * (m % 2):256 * (m % 2) + 256], mod[:, 40 + m, 0:1],
                  XL[:, m, :], MUL, ADD, T.last, t_a, c=0)
        tv.append(t)
    for b in yb:
        b.free = [t]
    for m in range(8):
        K.mean_add(XL[:, m, :], tv[m])

    def post2(k, t):
        V.ts(XL[:, k, :], XL[:, k, :], K.v("ln2g", k), K.v("ln2b", k), MUL, ADD)

    K.layer_norm(XL, 256, 0, sqb, rs, post2)
    K.barrier()
    ctx.close()


def experts_all(K, v8, h32, WT, ctx):
    T, V, S, G, A3 = K.T, K.V, K.S, K.G, K.A
    NAR = 9600
    A = Arena(K.sb("ar_all", [128, NAR], F32, ctx), NAR)
    for m in range(8):
        ht = K.split(v8.hi[:, m, :], v8.lo[:, m, :], h32[:, m, :])
    b, tk = K.transpose_to([(WT[:, j, :], 128 * j) for j in range(2)], 32)
    wT = A.get(256)
    t = V.cp(wT[0:32, :], b.t[0:32, 0:256], tk)
    b.free = [t]
    T.wait(t)
    wbc = A.get(32, 256)
    for e_ in range(0, 32, 2):
        b = K.bank()
        for i in range(2):
            T.mm(b.t[:, 256 * i:256 * i + 256], K.ident[0:32, e_ + i:e_ + i + 1].broadcast_to([32, 128]),
                 wT[0:32, :], True, True)
        tk = T.mark()
        t = S.act(wbc[:, e_:e_ + 2, :], b.t[:, :].rearrange("p (i n) -> p i n", i=2), ACT.Copy, tk, c=0)
        b.free = [t]
    t_w = t
    EH = [K.sb(f"EH{i}", [128, 4, 256], F32R, ctx) for i in range(2)]
    EL = [K.sb(f"EL{i}", [128, 4, 256], F32R, ctx) for i in range(2)]
    sg, pr = [A.get(256) for _ in range(2)], [A.get(256) for _ in range(2)]
    sgf, prf, ehf = [[], []], [[], []], [[], []]
    yb = K.banks[4:8]
    K.lo, K.hi = 0, 4
    for b in yb:
        T.wait(*b.free)
    down = None
    for e_ in range(33):
        nxt = None
        if e_ < 32:
            E3 = X3(EH[e_ % 2], EL[e_ % 2])
            E3.split = True
            toks = []
            for p in range(2):
                wg = K.ring.get("w_eg", e_, 0, 8, 256 * p, 256, True)
                bs = []
                T.wait(*wg.toks, *ht)
                for i in range(2):
                    b = K.bank()
                    bs.append(b)
                    for k in range(8):
                        K.prod(b.t[:, 0:256], wg, (slice(None), k, slice(i * 128, i * 128 + 128)), v8,
                               (slice(None), k, slice(0, 256)), k == 0, k == 7)
                wg.end(T.mark())
                wu = K.ring.get("w_eu", e_, 0, 8, 256 * p, 256, True)
                T.wait(*wu.toks)
                for i in range(2):
                    b = bs[i]
                    for k in range(8):
                        K.prod(b.t[:, 256:512], wu, (slice(None), k, slice(i * 128, i * 128 + 128)), v8,
                               (slice(None), k, slice(0, 256)), k == 0, k == 7)
                    tk = T.mark()
                    if i == 1:
                        wu.end(tk)
                    m = 2 * p + i
                    q = m % 2
                    t1 = S.act(sg[q], b.t[:, 0:256], ACT.Silu, tk, *sgf[q], c=0)
                    t2 = V.tt(pr[q], sg[q], b.t[:, 256:512], MUL, t1, *prf[q], c=0)
                    sgf[q], b.free = [t2], [t2]
                    t3 = G.tt(pr[q], pr[q], wbc[:, e_, :], MUL, t2, t_w, c=0)
                    toks = K.split(E3.hi[:, m, :], E3.lo[:, m, :], pr[q], t3, *ehf[e_ % 2])
                    prf[q] = toks
            nxt = (e_, E3, toks)
        if down is not None:
            de, E3d, dt_ = down
            for half in range(2):
                w = K.ring.get("w_ed", de, 0, 4, 512 * half, 512, True)
                T.wait(*w.toks, *dt_)
                for i in range(4):
                    m = 4 * half + i
                    o = yb[m // 2].t[:, 256 * (m % 2):256 * (m % 2) + 256]
                    for k in range(4):
                        K.prod(o, w, (slice(None), k, slice(i * 128, i * 128 + 128)), E3d,
                               (slice(None), k, slice(0, 256)), de == 0 and k == 0 and m % 2 == 0,
                               de == 31 and k == 3, skip=True)
                w.end(T.mark())
            ehf[de % 2] = [T.last]
            K.step()
        down = nxt


def experts_some(K, h32, WT, pos, ctx):
    T, V, S, G, A3 = K.T, K.V, K.S, K.G, K.A

    def pair(name, *shape, n=1):
        return [[K.sb(f"{name}{q}{i}", [128, *shape], F32R, ctx) for q in "hl"] for i in range(n)]

    HTK, = pair("htk", 2, 1024)
    HT = pair("hts", 4, 128, n=2)
    YE = pair("ye", 1024, n=2)
    SEL = [K.sb(f"sel{i}", [128, 2, 512], F32R, ctx) for i in range(2)]
    SELT = [K.sb(f"selt{i}", [128, 256], F32R, ctx) for i in range(3)]
    WHL = K.sb("whl", [128, 2, 32, 2], F32R, ctx)
    NAR = 2100
    A = Arena(K.sb("ar_some", [128, NAR], F32, ctx), NAR)
    iot, pT = A.get(129), A.get(256)
    iotar, iotac = iot[:, 0:128], iot[:, 128:129]
    sg, hid, ws = [A.get(256) for _ in range(2)], [A.get(512) for _ in range(2)], A.get(32, 2)
    wsum = A.get(32)
    K.cst("iotar", iot, n=129)
    t_i = K.landed()
    XG = [K.AH[:, :].rearrange("p (k n) -> p k n", k=8), K.AL[:, :].rearrange("p (k n) -> p k n", k=8)]
    for j in range(2):
        for q in range(2):
            b, tk = K.transpose_to([(h32[:, 4 * q + m, j * 128:j * 128 + 128], 128 * m) for m in range(4)], 128)
            s = slice(512 * q, 512 * q + 512)
            a = S.act(HTK[0][:, j, s], b.t[:, :], ACT.Copy, tk, c=0)
            t_h = V.tt(HTK[1][:, j, s], b.t[:, :], HTK[0][:, j, s].bitcast(F32), SUB, a, c=0)
            b.free = [t_h]
    V.cp(WHL[:, :, :, 0], WT)
    t_whl = V.tt(WHL[:, :, :, 1], WT, WHL[:, :, :, 0].bitcast(F32), SUB)
    b, tk = K.transpose_to([(pos[:, j, :], 128 * j) for j in range(2)], 32)
    t_pT = V.cp(pT[0:32, :], b.t[0:32, 0:256], tk)
    b.free = [t_pT]
    V.wait(t_i)
    sel_free, selt_free, xg_free, sgf, hidf, htf, yef = [[], []], [[], [], []], [], [[], []], [[], []], [[], []], \
        [[], []]
    sel_t, xg_t, selt_t, ws_t, hid_t, ht_t, ye_t = {}, {}, {}, {}, {}, {}, {}

    def select(g):
        for j in range(2):
            for q in range(4):
                e_ = 4 * g + q
                t = V.ts(SEL[g % 2][:, j, 128 * q:128 * q + 128], iotar, pos[:, j, e_:e_ + 1], None, ALU.is_equal,
                         None, *sel_free[g % 2], c=0)
        sel_t[g] = t

    def gather(g):
        T.wait(sel_t[g], t_h)
        for k in range(8):
            for part in range(2):
                b = K.bank()
                for j in range(2):
                    T.mm(b.t[:, :], HTK[part][:, j, k * 128:k * 128 + 128], SEL[g % 2][:, j, :], j == 0, j == 1)
                tk = T.mark()
                if part == 0:
                    t1 = S.act(XG[0][:, k, :], b.t[:, :], ACT.Copy, tk, *xg_free, c=0)
                    b.free = [t1]
                else:
                    t2 = V.cp(XG[1][:, k, :], b.t[:, :], tk, *xg_free, c=0)
                    b.free = [t2]
        xg_t[g] = [t1, t2]
        T.wait(t_whl)
        b = K.bank()
        for q in range(4):
            for j in range(2):
                T.mm(b.t[:, 2 * q:2 * q + 2], SEL[g % 2][:, j, 128 * q:128 * q + 128], WHL[:, j, 4 * g + q, :],
                     j == 0, j == 1)
        tk = T.mark()
        sel_free[g % 2] = [tk]
        t = V.cp(ws[:, 4 * g:4 * g + 4, :], b.t[:, 0:8].rearrange("p (q c) -> p q c", c=2), tk)
        b.free = [t]
        ws_t[g] = V.tt(wsum[:, 4 * g:4 * g + 4], ws[:, 4 * g:4 * g + 4, 0], ws[:, 4 * g:4 * g + 4, 1], ADD)

    def row_select(e_):
        i = e_ % 3
        T.wait(t_pT)
        b = K.bank()
        T.mm(b.t[:, 0:256], K.ident[0:32, e_:e_ + 1].broadcast_to([32, 128]), pT[0:32, :], True, True)
        tk = T.mark()
        selt_t[e_] = V.ts(SELT[i][:, :], b.t[:, 0:256], iotac, None, ALU.is_equal, None, tk, *selt_free[i], c=0)
        b.free = [selt_t[e_]]

    def gate_up(e_):
        g, q, i = e_ // 4, e_ % 4, e_ % 2
        T.wait(*xg_t[g])
        s = slice(128 * q, 128 * q + 128)
        for p in range(2):
            b = K.bank()
            for n_, name in enumerate(("w_eg", "w_eu")):
                w = K.ring.get(name, e_, 0, 8, 256 * p, 256, True)
                T.wait(*w.toks)
                o = b.t[:, 256 * n_:256 * n_ + 256]
                for k in range(8):
                    T.mm(o, XG[0][:, k, s], w.hi[:, k, :], k == 0, False)
                    T.mm(o, XG[0][:, k, s], w.lo[:, k, :], False, False)
                    T.mm(o, XG[1][:, k, s], w.hi[:, k, :], False, k == 7)
                w.end(T.mark())
            tk = T.last
            t1 = S.act(sg[p], b.t[:, 0:256], ACT.Silu, tk, *sgf[p], c=0)
            t2 = V.stt(hid[i][:, 256 * p:256 * p + 256], b.t[:, 256:512], wsum[:, e_:e_ + 1], sg[p], MUL, MUL, t1,
                       ws_t[g], *hidf[i], c=0)
            b.free, sgf[p] = [t2], [t2]
        hid_t[e_] = t2
        if q == 3:
            del xg_free[:]
            xg_free.append(T.last)

    def turn(e_):
        i = e_ % 2
        T.wait(hid_t[e_])
        b, tk = K.transpose_to([(hid[i][:, 128 * k:128 * k + 128], 128 * k) for k in range(4)], 128)
        hidf[i] = [tk]
        src = b.t[:, :].rearrange("p (k n) -> p k n", k=4)
        a = S.act(HT[i][0][:, :, :], src, ACT.Copy, tk, *htf[i], c=0)
        t = V.tt(HT[i][1][:, :, :], src, HT[i][0][:, :, :].bitcast(F32), SUB, a, c=0)
        b.free = [t]
        ht_t[e_] = [a, t]

    def down(e_):
        i = e_ % 2
        T.wait(*ht_t[e_])
        for half in range(2):
            w = K.ring.get("w_ed", e_, 0, 4, 512 * half, 512, True)
            T.wait(*w.toks)
            b = K.bank()
            for k in range(4):
                T.mm(b.t[:, :], HT[i][0][:, k, :], w.hi[:, k, :], k == 0, False)
                T.mm(b.t[:, :], HT[i][0][:, k, :], w.lo[:, k, :], False, False)
                T.mm(b.t[:, :], HT[i][1][:, k, :], w.hi[:, k, :], False, k == 3)
            tk = T.mark()
            w.end(tk)
            s = slice(512 * half, 512 * half + 512)
            a = S.act(YE[i][0][:, s], b.t[:, :], ACT.Copy, tk, *yef[i], c=0)
            t = V.tt(YE[i][1][:, s], b.t[:, :], YE[i][0][:, s].bitcast(F32), SUB, a, c=0)
            b.free = [t]
        htf[i] = [T.last]
        ye_t[e_] = [a, t]

    def scatter(e_):
        i = e_ % 2
        T.wait(*ye_t[e_], selt_t[e_])
        for m in range(8):
            o = yb[m // 2].t[:, 256 * (m % 2):256 * (m % 2) + 256]
            for part in range(2):
                T.mm(o, YE[i][part][:, m * 128:m * 128 + 128], SELT[e_ % 3][:, :],
                     e_ == 0 and part == 0 and m % 2 == 0, e_ == 31 and part == 1, True)
        tk = T.mark()
        yef[i], selt_free[e_ % 3] = [tk], [tk]

    yb = K.banks[4:8]
    K.lo, K.hi = 0, 4
    select(0)
    gather(0)
    select(1)
    for e_ in range(34):
        if e_ < 32:
            gate_up(e_)
            row_select(e_)
        if e_ % 4 == 3 and e_ < 31:
            gather(e_ // 4 + 1)
            if e_ < 27:
                select(e_ // 4 + 2)
        if e_ >= 2:
            scatter(e_ - 2)
        if 1 <= e_ <= 32:
            down(e_ - 1)
        if e_ < 32:
            turn(e_)
    K.lo, K.hi = 0, 8


CAP = 128.0


class HalfView:
    split = True

    def __init__(self, v, s):
        self.hi, self.lo = v.hi[:, :, s:s + 256], v.lo[:, :, s:s + 256]


def lead_in(K, l, base, n, x, tmp, alpha):
    mod = K.mod2[l] if l is not None else K.mod1
    used = [[], []]
    K.x_ready = []

    def post(k, t):
        r = scaled_split(K, x[:, k, :], k, n, K.A, lambda k, v: (mod[:, base + 8 + k, v:v + 1],
                                                                mod[:, base + k, v:v + 1]), tmp, used, [t])
        K.x_ready = [K.G.ts(x[:, k, :], x[:, k, :], alpha, None, MUL, None, *r, c=0)]
        return r

    return post


def residual(K, x, gate, halves, toks):
    wait = []

    def put(m, ps, tok):
        for a, z, v in halves:
            t = K.V.stt(x[:, m, a:z], ps[:, a:z], gate(m, v), x[:, m, a:z], MUL, ADD, tok, *toks, c=0)
        if wait:
            K.mean_add(*wait.pop())
        wait.append((x[:, m, :], t))
        if m == 7:
            K.mean_add(*wait.pop())
        return [t]

    return put


BOTH, LAT = [(0, 256, 1), (256, 512, 0)], [(0, 256, 0)]


def ffn(K, l, win, wout, base, n, nxt, jobs=()):
    T, V, S, G = K.T, K.V, K.S, K.G
    ctx = ExitStack()
    BH, BL = (K.sb(f"{q}{win}{l}", [128, 12, 512], F32R, ctx) for q in ("BH", "BL"))
    NAR = 7680
    A = Arena(K.sb(f"arf{win}{l}", [128, NAR], F32, ctx), NAR)
    sq, rs, tmp, sg, pr = A.get(8, 512)[:, :, 0:n], A.get(512)[:, 0:n], A.get(2, 512), A.get(2, 512), A.get(2, 512)
    X = K.X[:, :, 512 - n:512]
    mod = K.mod2[l]
    ht, t_a = K.h_ready, K.x_ready
    h = View3(K.A, 8, n)
    hid = X3(BH, BL)
    hid.split = True
    f = {"sg": [[], []], "pr": [[], []]}
    hfree = []
    for first, cnt in ((0, 12), (12, 10)):
        toks = []
        for p in range(cnt // 2):
            c0 = (first + 2 * p) * 128
            wg = K.ring.get(win, l, 0, 8, c0, 256, True)
            T.wait(*wg.toks)
            bs = []
            for i in range(2):
                b = K.bank()
                bs.append((b, K.bank()))
                for k in range(8):
                    T.wait(*ht[k])
                    K.prod(b.t[:, 0:n], wg, (slice(None), k, slice(i * 128, i * 128 + 128)), h,
                           (slice(None), k, slice(0, n)), k == 0, k == 7)
            wg.end(T.mark())
            wu = K.ring.get(win, l, 0, 8, 2816 + c0, 256, True)
            T.wait(*wu.toks)
            for i in range(2):
                b, b2 = bs[i]
                for k in range(8):
                    K.prod(b2.t[:, 0:n], wu, (slice(None), k, slice(i * 128, i * 128 + 128)), h,
                           (slice(None), k, slice(0, n)), k == 0, k == 7)
                tk = T.mark()
                if i == 1:
                    wu.end(tk)
                m = 2 * p + i
                t1 = S.act(sg[:, i, 0:n], b.t[:, 0:n], ACT.Silu, tk, *f["sg"][i], c=0)
                b.free = [t1]
                t2 = V.tt(pr[:, i, 0:n], sg[:, i, 0:n], b2.t[:, 0:n], MUL, t1, *f["pr"][i], c=0)
                b2.free, f["sg"][i] = [t2], [t2]
                toks = K.split(BH[:, m, 0:n], BL[:, m, 0:n], pr[:, i, 0:n], t2, *hfree)
                f["pr"][i] = toks

            K.step()
        if first == 0:
            def down(m, ps, tok):
                for a, z, v in (BOTH if n == 512 else LAT):
                    t = V.stt(X[:, m, a:z], ps[:, a:z], mod[:, base + 16 + m, v:v + 1], X[:, m, a:z], MUL, ADD,
                              tok, *t_a, c=0)
                return [t]
        else:
            K.mean_begin(n)
            down = residual(K, X, lambda m, v: mod[:, base + 16 + m, v:v + 1], BOTH if n == 512 else LAT, t_a)
        K.linear(wout, l, cnt, 0, 8, hid, n, down, row=first * 128, xtoks=toks)
        hfree = [T.last]
    K.A.free = [T.last]
    for j in jobs:
        K.finish(j)
    post = lead_in(K, *nxt[:3], X, tmp, ALPHA2) if nxt else lambda k, t: None
    K.h_ready = K.layer_norm(X, n, 1, sq, rs, post)
    K.barrier(pe=False)
    ctx.close()


def log1p_exp(K, dst, z, e1, e2, tz):
    V, S = K.V, K.S
    V.stt(e1, z, -1.0, z, MUL, MIN, tz)
    t = S.act(e1, e1, ACT.Exp, V.last)
    V.ts(e2, e1, 1.0, None, ADD, None, t)
    t = S.act(dst, e2, ACT.Ln, V.last)
    one = z_eq = K.lp
    V.ts(one, e2, 1.0, None, ALU.is_equal, None, t)
    V.stt(e2, e2, -1.0, one, ADD, ADD)
    V.tt(dst, dst, z_eq, ADD)
    V.rec(e2)
    V.tt(dst, dst, e1, MUL)
    return V.tt(dst, dst, e2, MUL)


def token_rows(K, name, lead, c0, ncol, h, ht, dst):
    T, S = K.T, K.S
    for a in range(0, ncol, 256):
        w = K.ring.get(name, lead, 0, 8, c0 + a, 256, True)
        T.wait(*w.toks)
        for tt in range(4):
            b = K.bank()
            o = b.t[:, 0:256]
            for k in range(8):
                s = (slice(None), k, slice(tt * 128, tt * 128 + 128))
                T.mm(o, h.hi[s], w.hi[:, k, :], k == 0, False)
                T.mm(o, h.hi[s], w.lo[:, k, :], False, False)
                T.mm(o, h.lo[s], w.hi[:, k, :], False, k == 7)
            tk = T.mark()
            if tt == 3:
                w.end(tk)
            t = S.act(dst[:, tt, a:a + 256], o, ACT.Copy, tk, c=0)
            b.free = [t]
    return t


def even(K):
    T, V, S, G = K.T, K.V, K.S, K.G
    ctx = ExitStack()
    NAR = 19900
    A = Arena(K.sb("ar3", [128, NAR], F32, ctx), NAR)
    X = K.X[:, :, :]
    mod = K.mod2[0]
    oT = A.get(4, 512)
    base = A.at
    ht, t_alpha = K.h_ready, K.x_ready
    h = View3(K.A, 8, 512)
    A.at = base
    qT, kT, vt, r = A.get(2, 512), A.get(2, 512), A.get(4, 512), A.get(4, 512)
    bs = [A.get(2, 512) for _ in range(2)]
    glam = A.get(15, 128)
    K.cst("glam", glam.rearrange("p a b -> p (a b)"))
    KQ = [A.get(2, 512) for _ in range(2)]
    ST = [[A.get(2, 128) for _ in range(3)] for _ in range(2)]
    att_at = A.at
    lr, WG, e1, e2, K.lp, z = A.get(512), A.get(2, 256), A.get(512), A.get(512), A.get(512), A.get(512)
    t_z = G.do(lambda e: e.memset(WG[0:32], 0.0))
    K.D.wait(t_z)
    K.load(WG[0:16, 0, :], K.dram["wg2f"])
    K.load(WG[16:32, 1, :], K.dram["wg2b"])
    t_wg = K.landed()
    K.linear("ewi", None, 8, 1536, 1, h, 512, lambda m, ps, tok: [S.act(lr[0:32], ps[0:32], ACT.Copy, tok)],
             xtoks=ht)
    t_lr = S.last
    zt = None
    T.wait(t_lr, t_wg)
    for d in range(2):
        for ft in range(2):
            b = K.bank()
            T.mm(b.t[:, :], WG[0:32, d, ft * 128:ft * 128 + 128], lr[0:32, :], True, True)
            tk = T.mark()
            V.ts(z, b.t[:, :], K.v("bgf" if d == 0 else "bgb", ft), None, ADD, None, tk)
            b.free = [V.last]
            e3 = KQ[0][:, 0, :]
            log1p_exp(K, e3, z, e1, e2, V.last)
            V.ts(z, z, 0.0, 0.0625, MIN, MUL)
            V.stt(z, e3, -0.0625, z, MUL, ADD)
            for tt in range(4):
                s = slice(tt * 128, tt * 128 + 128)
                o, i = (bs[d][:, ft, s], z[:, s]) if d == 0 else (bs[d][:, ft, s][:, ::-1], z[:, s][:, ::-1])
                V.do(lambda e, o=o, i=i: e.tensor_tensor_scan(o, K.ones[:, 0:128], i, 0.0, MUL, ADD), c=tt == 0)
    t_b = V.last
    K.linear("ewi", None, 8, 0, 2, h, 512, lambda m, ps, tok: [S.act(qT[:, m, :], ps, ACT.Copy, tok, c=0,
                                                                    scale=0.125)])
    K.linear("ewi", None, 8, 256, 2, h, 512, lambda m, ps, tok: [S.act(kT[:, m, :], ps, ACT.Copy, tok, c=0)])
    t_qk = S.last
    token_rows(K, "ewi", None, 512, 512, h, ht, vt)
    K.linear("ewi", None, 8, 1024, 4, h, 512, lambda m, ps, tok: [S.act(r[:, m, :], ps, ACT.Silu, tok, c=0)])
    t_v = S.last
    K.barrier()
    A.at = att_at
    kd, kt_ = KQ[0][:, :, 0:128], KQ[1][:, 0, 0:256]
    eb = KQ[1][:, 1, 0:2]
    for d, order in ((0, (0, 1, 2)), (1, (1, 0, 3))):
        for n_, tt in enumerate(order):
            s = slice(tt * 128, tt * 128 + 128)
            last = tt * 128 + (127 if d == 0 else 0)
            for ft in range(2):
                t = S.act(kd[:, ft, :], bs[d][:, ft, s], ACT.Exp, t_b, V.last, T.last,
                          bias=bs[d][:, ft, last:last + 1], scale=-1.0)
            t = S.act(eb.unsqueeze(2), bs[d][:, :, last:last + 1], ACT.Exp, V.last)
            t = V.tt(kd, kd, kT[:, :, s], MUL, t)
            T.wait(t)
            b, tk = K.transpose_to([(kd[:, ft, :], 128 * ft) for ft in range(2)], 128)
            t = V.cp(kt_, b.t[:, 0:256], tk)
            b.free = [t]
            T.wait(t)
            b = K.bank()
            for ft in range(2):
                for p in range(2):
                    hd = 2 * ft + p
                    T.mm(b.t[64 * p:64 * p + 64, ft * 128:ft * 128 + 128], kt_[:, hd * 64:hd * 64 + 64],
                         vt[:, tt, hd * 128:hd * 128 + 128], True, True)
            tk = T.mark()
            for ft in range(2):
                if n_ == 0:
                    t = V.cp(ST[d][0][:, ft, :], b.t[:, ft * 128:ft * 128 + 128], tk)
                else:
                    t = V.stt(ST[d][n_][:, ft, :], ST[d][n_ - 1][:, ft, :], eb[:, ft:ft + 1],
                              b.t[:, ft * 128:ft * 128 + 128], MUL, ADD, tk)
            b.free = [t]
    t_st = V.last
    ATT = [[A.get(4, 128) for _ in range(2)] for _ in range(2)]
    t_gm = t_wg

    def pairs(k_, q_, put):
        for p in range(2):
            for tp in range(2):
                b = K.bank()
                for t2 in range(2):
                    for ft in range(2):
                        s = slice((2 * tp + t2) * 128, (2 * tp + t2) * 128 + 128)
                        T.mm(b.t[:, (2 * t2 + ft) * 128:(2 * t2 + ft) * 128 + 128],
                             k_[64 * p:64 * p + 64, ft, s], q_[64 * p:64 * p + 64, ft, s], True, True)
                tk = T.mark()
                b.free = [put(ATT[p][tp], b.t[:, :].rearrange("p (a b) -> p a b", a=4), tk)]

    T.wait(t_qk)
    V.wait(t_gm)
    pairs(kT, qT, lambda a, ps, tk: V.tt(a, ps, glam[:, 14:15, :].broadcast_to([128, 4, 128]), MUL, tk, c=0))
    kq_free = [[T.last, t_st], [T.last, t_st]]
    n_ = 0
    for lv in range(7):
        for d in range(2):
            w = 1 << lv
            kq = KQ[n_ % 2]

            def halves(x):
                return x.rearrange("p a b -> p (a b)").rearrange("p (n s w) -> p n s w", s=2, w=w)

            bv, dv, kv, qv = halves(bs[d]), halves(kq), halves(kT), halves(qT)
            nb = 512 // w
            ref = (bv[:, :, 0, w - 1:w] if d == 0 else bv[:, :, 1, 0:1]).broadcast_to([128, nb, w])
            lo, up = bv[:, :, 0, :], bv[:, :, 1, :]
            if d == 0:
                t0 = V.tt(dv[:, :, 0, :], ref, lo, SUB, *kq_free[n_ % 2], c=0)
                t1 = G.tt(dv[:, :, 1, :], up, ref, SUB, t_b, *kq_free[n_ % 2], c=0)
            else:
                t0 = V.tt(dv[:, :, 0, :], lo, ref, SUB, *kq_free[n_ % 2], c=0)
                t1 = G.tt(dv[:, :, 1, :], ref, up, SUB, t_b, *kq_free[n_ % 2], c=0)
            flat = kq.rearrange("p a b -> p (a b)")
            te = S.act(flat, flat, ACT.Exp, t0, t1, c=0)
            a, b_ = (kv, qv) if d == 0 else (qv, kv)
            t0 = V.tt(dv[:, :, 0, :], dv[:, :, 0, :], a[:, :, 0, :], MUL, te, c=0)
            t1 = G.tt(dv[:, :, 1, :], dv[:, :, 1, :], b_[:, :, 1, :], MUL, te, c=0)
            T.wait(t0, t1)
            mk = glam[:, 7 * d + lv:7 * d + lv + 1, :].bitcast(U32).broadcast_to([128, 4, 128])
            pairs(kq, kq, lambda x, ps, tk: V.do(lambda e, x=x, ps=ps, mk=mk: e.copy_predicated(x, mk, ps), tk, c=1))
            kq_free[n_ % 2] = [T.last]
            n_ += 1
    QE = KQ
    for d in range(2):
        flat = QE[d].rearrange("p a b -> p (a b)")
        t = S.act(flat, bs[d].rearrange("p a b -> p (a b)"), ACT.Exp, T.last, c=0)
        t = V.tt(QE[d], QE[d], qT, MUL, t, c=0)
    t_att = V.last
    T.wait(t_att)
    sq, rs = bs[0][:, 0, :], bs[0][:, 1, :]
    before = [{1: 0, 2: 1, 3: 2}, {0: 0, 3: 1, 2: 2}]
    sqf = []
    for hd in range(4):
        ft, p = hd // 2, hd % 2
        b = K.bank()
        for tt in range(4):
            s = slice(tt * 128, tt * 128 + 128)
            o = b.t[:, s]
            inter = [(d, before[d][tt]) for d in range(2) if tt in before[d]]
            T.mm(o, vt[:, tt, hd * 128:hd * 128 + 128], ATT[p][tt // 2][:, (tt % 2) * 2 + ft, :], True, not inter)
            for x, (d, n_) in enumerate(inter):
                T.mm(o, ST[d][n_][64 * p:64 * p + 64, ft, :], QE[d][64 * p:64 * p + 64, ft, s], False,
                     x == len(inter) - 1)
        tk = T.mark()
        t = V.cp(oT[:, hd, :], b.t[:, :], tk)
        b.free = [t]
        t = S.act(sq, oT[:, hd, :], ACT.Square, t, *sqf)
        T.wait(t)
        b = K.bank()
        T.mm(b.t[:, :], K.onesD[:, :], sq, True, True)
        sqf = [T.mark()]
        t = S.act(rs, b.t[:, :], ACT.Sqrt, T.last, V.last, bias=K.eps[:, 1:2], scale=8.0)
        b.free = [t]
        V.rec(rs, t)
        V.stt(oT[:, hd, :], oT[:, hd, :], K.v("gng"), rs, MUL, MUL)
        V.tt(oT[:, hd, :], oT[:, hd, :], r[:, hd, :], MUL, t_v)
    K.barrier()
    A.at = base
    cq, ck, krr = A.get(3, 512), A.get(1, 512), A.get(512)
    K.linear("ewi", None, 8, 1568, 3, h, 512, lambda m, ps, tok: [S.act(cq[:, m, :], ps, ACT.Copy, tok, c=0)])
    K.linear("ewi", None, 8, 1952, 1, h, 512, lambda m, ps, tok: [S.act(ck[:, m, :], ps, ACT.Copy, tok, c=0)])
    K.linear("ewi", None, 8, 2016, 1, h, 512,
             lambda m, ps, tok: [S.act(krr[64:128, :], ps[64:128, :], ACT.Copy, tok, c=0)])
    K.A.free = [T.last]
    t_c = S.last
    qn, qr, kn, v2, oM = A.get(4, 512), A.get(4, 512), A.get(4, 512), A.get(4, 512), A.get(4, 512)
    cos, sin, rsw = A.get(256), A.get(256), A.get(64)
    K.cst("cos", cos)
    K.cst("sin", sin)
    K.cst("rsw", rsw)
    t_rope = K.landed()
    P = [A.get(512) for _ in range(2)]
    PT = [A.get(4, 128) for _ in range(2)]
    st = A.get(8)
    rs = P[0]
    for x, nt, key, w in ((cq, 3, "qng", 1024.0 / 384), (ck, 1, "kvng", 8.0)):
        b = K.bank()
        for m in range(nt):
            t = S.act(P[1], x[:, m, :], ACT.Square, t_c, T.last)
            T.wait(t)
            T.mm(b.t[:, :], K.onesD[:, :], P[1], m == 0, m == nt - 1)
            T.mark()
        t = S.act(rs, b.t[:, :], ACT.Sqrt, T.last, V.last, bias=K.eps[:, 1:2], scale=w)
        b.free = [t]
        V.rec(rs, t)
        for m in range(nt):
            V.stt(x[:, m, :], x[:, m, :], K.v(key, m), rs, MUL, MUL)
    tn = V.last

    def lin32(name, kt, col, x, put):
        w = K.ring.get(name, None, 0, kt, col, 128, False)
        T.wait(*w.toks, tn)
        b = K.bank()
        for k in range(kt):
            T.mm(b.t[:, :], w.f[:, k, :], x[:, k, :], k == 0, k == kt - 1)
        tk = T.mark()
        w.end(tk)
        b.free = [put(b.t, tk)]

    for hd in range(4):
        lin32("uq", 3, 192 * hd, cq, lambda ps, tk: S.act(qn[:, hd, :], ps[:, :], ACT.Copy, tk, c=0))
        lin32("uq", 3, 192 * hd + 64, cq, lambda ps, tk: S.act(qr[64:128, hd, :], ps[64:128, :], ACT.Copy, tk, c=0))
        lin32("ukv", 1, 256 * hd, ck, lambda ps, tk: S.act(kn[:, hd, :], ps[:, :], ACT.Copy, tk, c=0))
        w = K.ring.get("ukv", None, 0, 1, 256 * hd + 128, 128, False)
        T.wait(*w.toks)
        b = K.bank()
        for tt in range(4):
            T.mm(b.t[:, tt * 128:tt * 128 + 128], ck[:, 0, tt * 128:tt * 128 + 128], w.f[:, 0, :], True, True)
        tk = T.mark()
        w.end(tk)
        t = S.act(v2[:, :, hd * 128:hd * 128 + 128], b.t[:, :].rearrange("p (a b) -> p a b", a=4), ACT.Copy, tk, c=0)
        b.free = [t]
    t_q = S.last
    V.wait(t_rope, t_q)
    T.wait(t_rope, t_q)
    q = slice(64, 128)
    for x in [qr[q, i, 256:512] for i in range(4)] + [krr[q, 256:512]]:
        b = K.bank()
        T.mm(b.t[q, 0:256], rsw[q, :], x, True, True)
        tk = T.mark()
        V.tt(x, x, cos[q], MUL, tk)
        V.tt(P[0][q, 0:256], b.t[q, 0:256], sin[q], MUL)
        b.free = [V.last]
        V.tt(x, x, P[0][q, 0:256], ADD)
    T.wait(V.last)
    S.wait(V.last)
    work = [(hd, qt) for hd in range(4) for qt in range(4)]
    scale = 192.0 ** -0.5
    pf, ptf = [[], []], [[], []]
    stage = {}

    def scores(n_):
        hd, qt = work[n_]
        i = n_ % 2
        nk = 512 if qt >= 2 else 256
        s = slice(qt * 128, qt * 128 + 128)
        b = K.bank()
        T.mm(b.t[:, 0:nk], qn[:, hd, s], kn[:, hd, 0:nk], True, False)
        T.mm(b.t[:, 0:nk], qr[q, hd, s], krr[q, 0:nk], False, True)
        tk = T.mark()
        stage[n_] = soft(b, nk, i, st[:, 4 * i:4 * i + 4], P[i], tk, scale, pf[i])

    def soft(b, nk, i, s4, p, tk, sc, free):
        mx, sm = s4[:, 0:1], s4[:, 1:2]
        V.red(mx, b.t[:, 0:nk], MAX, tk, *free)
        V.ts(mx, mx, -sc, None, MUL, None)
        t = S.act(p[:, 0:nk], b.t[:, 0:nk], ACT.Exp, V.last, *free, c=0, bias=mx, scale=sc, accum_out=sm)
        b.free = [t]
        V.rec(sm, t)
        return V.ts(p[:, 0:nk], p[:, 0:nk], sm, None, MUL, None)

    def values(n_):
        hd, qt = work[n_]
        i = n_ % 2
        nk = 512 if qt >= 2 else 256
        T.wait(stage[n_])
        b, tk = K.transpose_to([(P[i][:, a * 128:a * 128 + 128], a * 128) for a in range(nk // 128)], 128)
        pf[i] = [tk]
        t = V.cp(PT[i][:, 0:nk // 128, :], b.t[:, 0:nk].rearrange("p (a b) -> p a b", b=128), tk, *ptf[i])
        b.free = [t]
        T.wait(t)
        b = K.bank()
        for a in range(nk // 128):
            T.mm(b.t[:, 0:128], v2[:, a, hd * 128:hd * 128 + 128], PT[i][:, a, :], a == 0, a == nk // 128 - 1)
        tk = T.mark()
        ptf[i] = [tk]
        t = S.act(oM[:, hd, qt * 128:qt * 128 + 128], b.t[:, 0:128], ACT.Copy, tk, c=0)
        b.free = [t]

    for n_ in range(17):
        if n_ < 16:
            scores(n_)
        if n_ >= 1:
            values(n_ - 1)
    toks = []
    for m in range(8):
        src = oT[:, m, :] if m < 4 else oM[:, m - 4, :]
        toks = K.split(h.hi[:, m, :], h.lo[:, m, :], src, S.last, V.last, *K.A.free)

    K.mean_begin(512)
    K.linear("ewo", None, 8, 0, 8, h, 512,
             residual(K, X, lambda m, v: mod[:, 40 + m, v:v + 1], BOTH, t_alpha), xtoks=toks)
    K.A.free = [T.last]
    K.barrier()
    A.at = 0
    sq, rs, tmp = A.get(8, 512), A.get(512), A.get(2, 512)
    K.h_ready = K.layer_norm(X, 512, 1, sq, rs, lead_in(K, 0, 48, 512, X, tmp, ALPHA2))
    K.barrier(pe=False)
    ctx.close()


def odd(K):
    T, V, S, G = K.T, K.V, K.S, K.G
    ctx = ExitStack()
    NAR = 19900
    A = Arena(K.sb("ar4", [128, NAR], F32, ctx), NAR)
    X = K.X[:, :, :]
    XL = X[:, :, 256:512]
    mod = K.mod2[1]
    TT = A.get(16, 384)
    K.load(TT, K.dram["rpb"].rearrange("p h m c -> p h (m c)"))
    qT, kT, vt = A.get(8, 256), A.get(8, 512), A.get(4, 1024)
    P = [A.get(512) for _ in range(2)]
    PT = A.get(4, 256)
    PT2 = A.get(4, 256)
    st = A.get(8)
    nm = A.get(64)
    K.cst("namask", nm)
    t_tt = K.landed()
    ht, t_alpha = K.h_ready, K.x_ready
    h = View3(K.A, 8, 512)
    hl = HalfView(h, 256)
    for hd in range(16):
        x = TT[:, hd, :].rearrange("p (m c) -> p m c", m=6)
        G.tt(x, x, nm.unsqueeze(1).broadcast_to([128, 6, 64]), ADD, t_tt, c=0)
    t_tt = G.last
    K.linear("nwi", None, 8, 0, 8, hl, 256, lambda m, ps, tok: [S.act(qT[:, m, :], ps, ACT.Copy, tok, c=0)], xtoks=ht)
    K.linear("nwi", None, 8, 1024, 8, h, 512, lambda m, ps, tok: [S.act(kT[:, m, :], ps, ACT.Copy, tok, c=0)])
    token_rows(K, "nwi", None, 2048, 1024, h, ht, vt)
    K.A.free = [T.last]
    t_v = S.last
    T.wait(t_v)
    V.wait(t_tt)
    PTs = [PT, PT2]
    pf, ptf = [[], []], [[], []]
    stage = {}
    ob = [None]

    def scores(n_):
        hd, qt = n_ // 2, n_ % 2
        i = n_ % 2
        p, m = 64 * (hd % 2), hd // 2
        b = K.bank()
        T.mm(b.t[:, :], qT[p:p + 64, m, qt * 128:qt * 128 + 128], kT[p:p + 64, m, :], True, True)
        tk = T.mark()
        V.stt(P[i][:, 256:512], b.t[:, 256:512], 0.125, TT[:, hd, (2 - 2 * qt) * 64:(2 - 2 * qt) * 64 + 256],
              MUL, ADD, tk, *pf[i], c=0)
        V.ts(P[i][:, 0:256], b.t[:, 0:256], 0.125, None, MUL, None, c=0)
        b.free = [V.last]
        mx, sm = st[:, 4 * i:4 * i + 1], st[:, 4 * i + 1:4 * i + 2]
        V.red(mx, P[i], MAX)
        V.ts(mx, mx, -1.0, None, MUL, None)
        t = S.act(P[i], P[i], ACT.Exp, V.last, c=0, bias=mx, accum_out=sm)
        V.rec(sm, t)
        stage[n_] = V.ts(P[i], P[i], sm, None, MUL, None)

    def turned(n_):
        hd, qt = n_ // 2, n_ % 2
        i = n_ % 2
        pt = PTs[hd % 2]
        T.wait(stage[n_])
        b, tk = K.transpose_to([(P[i][:, a * 128:a * 128 + 128], a * 128) for a in range(4)], 128)
        pf[i] = [tk]
        t = S.act(pt[:, :, qt * 128:qt * 128 + 128], b.t[:, :].rearrange("p (a b) -> p a b", a=4), ACT.Copy, tk,
                  *ptf[hd % 2], c=0)
        b.free = [t]

    def values(hd):
        p, m = 64 * (hd % 2), hd // 2
        T.wait(S.last)
        b = K.bank()
        for a in range(4):
            T.mm(b.t[p:p + 64, 0:256], vt[:, a, hd * 64:hd * 64 + 64], PTs[hd % 2][:, a, :], a == 0, a == 3)
        tk = T.mark()
        ptf[hd % 2] = [tk]
        t = S.act(qT[p:p + 64, m, :], b.t[p:p + 64, 0:256], ACT.Copy, tk, c=0)
        b.free = [t]

    for n_ in range(33):
        if n_ < 32:
            scores(n_)
        if n_ >= 1:
            turned(n_ - 1)
            if n_ % 2 == 0:
                values(n_ // 2 - 1)
    v8 = View3(K.A, 8, 256)
    for m in range(8):
        toks = K.split(v8.hi[:, m, :], v8.lo[:, m, :], qT[:, m, :], S.last, *K.A.free)

    K.mean_begin(256)
    K.linear("nwo", None, 8, 0, 8, v8, 256,
             residual(K, XL, lambda m, v: mod[:, 40 + m, 0:1], LAT, t_alpha), xtoks=toks)
    K.A.free = [T.last]
    K.barrier()
    A.at = 0
    sq, rs, tmp = A.get(8, 256), A.get(256), A.get(2, 512)
    K.h_ready = K.layer_norm(XL, 256, 1, sq, rs, lead_in(K, 1, 48, 256, XL, tmp, ALPHA2))
    K.barrier(pe=False)
    ctx.close()


def block_two(K):
    V = K.V
    K.load(K.X[:, :, 0:256], K.dram["ctx2T"].rearrange("(k p) n -> p k n", p=128))
    K.t_in = K.landed()
    fix = {1: 1, 4: 1, 7: 1, 2: 2, 8: 2}
    jobs = K.ada2
    K.finish(jobs[0])
    V.wait(V.last, K.t_in)
    with ExitStack() as ctx:
        tmp = K.sb("tmp2", [128, 2, 512], F32, ctx)
        mod = K.mod2[0]
        used = [[], []]
        K.h_ready = []
        for k in range(8):
            r = scaled_split(K, K.X[:, k, :], k, 512, K.A, lambda k, v: (mod[:, 8 + k, v:v + 1],
                                                                        mod[:, k, v:v + 1]), tmp, used,
                             [V.last, K.t_in])
            K.h_ready.append(r)
            K.x_ready = [K.G.ts(K.X[:, k, :], K.X[:, k, :], ALPHA2, None, MUL, None, *r, c=0)]
        K.barrier(pe=False)
    K.jobs.append(jobs[1])
    K.phase("ffn")
    ffn(K, 0, "f1i", "f1o", 0, 512, (0, 24, 512))
    K.phase("even")
    even(K)
    K.phase("ffn")
    ffn(K, 0, "f2i", "f2o", 48, 512, (1, 0, 512), [jobs[1]])
    K.phase("ffn")
    ffn(K, 1, "f1i", "f1o", 0, 512, (1, 24, 512))
    K.phase("odd")
    odd(K)
    K.phase("ffn")
    ffn(K, 1, "f2i", "f2o", 48, 256, None)
    K.phase("end")

MODE = "all"


def build(nc, dram, out, plan, mode):
    with ExitStack() as ctx:
        K = Kern(nc, dram, plan, ctx)
        setup(K)
        if mode != "two":
            block_one(K, "mix" if mode == "mix" else None)
        else:
            fix2 = {1: 1, 4: 1, 7: 1, 2: 2, 8: 2}
            K.phase("start")
            K.ada2 = [conditioning(K, "ada_w", l, 0, 72, 2, K.v("ada_b", 72 * l, 72), K.mod2[l], fix2)
                      for l in range(2)]
            K.jobs.append(K.ada2[0])
        if mode in ("all", "two"):
            block_two(K)
        s_out = K.sem("s_out")
        K.barrier()
        K.dma(out.rearrange("(k p) n -> p k n", p=128), K.X[:, :, 256:512], s_out)
        K.D.items.append(lambda e: e.wait_ge(s_out, 16))
        if plan is None:
            return K.asked
        block = ctx.enter_context(nc.Block())

        @block.sync
        def _(eng):
            K.D.run(eng)

        @block.tensor
        def _(eng):
            K.T.run(eng)

        @block.vector
        def _(eng):
            K.V.run(eng)

        @block.scalar
        def _(eng):
            K.S.run(eng)

        @block.gpsimd
        def _(eng):
            K.G.run(eng)


def kernel(**I):
    import concourse.bacc as _bacc
    from concourse.bass_utils import run_bass_kernel_spmd as _run

    def col(a, n=128):
        return np.ascontiguousarray(np.asarray(a).reshape(-1, n).T)

    vec = np.zeros((128, NVEC), np.float32)

    def put(key, a):
        vec[:a.shape[0], VOFF[key]:VOFF[key] + a.shape[1]] = a

    I = {k: np.asarray(a) for k, a in I.items()}
    put("c", col(I["c"]))
    put("cc", col(I["c_ctx"]))
    put("b_ada", col(I["b_ada"]))
    put("b_gate", col(I["b_gate"]))
    put("conv_w", np.concatenate([col(I["conv_w"][0, i]) for i in range(5)], 1))
    put("conv_b", col(I["conv_b"]))
    put("ng", col(I["ssd_norm_g"]))
    put("pscale", col(I["pool_scale"]))
    for a, b in (("ln1g", "ln1_g"), ("ln1b", "ln1_b"), ("ln2g", "ln2_g"), ("ln2b", "ln2_b")):
        put(a, col(I[b]))
    put("dskip", col(np.repeat(I["d_skip"].reshape(-1), 64)))
    put("dtb", I["dt_bias"].reshape(64, 1))
    put("alog", I["a_log"].reshape(64, 1))
    put("c2", col(I["c_2"]))
    put("cc2", col(I["c_ctx_2"]))
    put("ada_b", col(I["ada_b_2"]))
    put("bgf", col(I["gla_bg_f_2"]))
    put("bgb", col(I["gla_bg_b_2"]))
    put("gng", col(I["gla_norm_g_2"]))
    put("qng", col(I["mla_q_norm_g_2"]))
    put("kvng", col(I["mla_kv_norm_g_2"]))
    rp = I["na_rpb_2"][0]
    p = np.arange(128)
    m = np.arange(6)
    dr = m[None, :] - 2 - (p // 64)[:, None] + 7
    dc = np.clip(np.arange(64)[None, :] - (p % 64)[:, None] + 15, 0, 30)
    rpb = rp[:, dr[:, :, None], dc[:, None, :]].transpose(1, 0, 2, 3)

    arrays = {
        "vec": vec, "cst": constants(), "rpb": np.ascontiguousarray(rpb),
        "xT": np.ascontiguousarray(I["x"][0].T), "ctxT": np.ascontiguousarray(I["ctx"][0].T),
        "ctx2T": np.ascontiguousarray(I["ctx_2"][0].T),
        "w_ada": I["w_ada"][0], "w_in": I["w_in"][0], "pool_w": I["pool_w"][0],
        "w_branch_a": I["w_branch_a"][0], "w_branch_b": I["w_branch_b"][0], "w_out": I["w_out"][0],
        "w_rg": I["w_router_group"][0], "w_re": I["w_router_expert"][0],
        "b_rg": I["b_router_group"].reshape(1, 4), "b_re": I["b_router_expert"].reshape(1, 32),
        "w_eg": I["w_expert_gate"][0], "w_eu": I["w_expert_up"][0], "w_ed": I["w_expert_down"][0],
        "ada_w": I["ada_w_2"], "f1i": I["ffn1_w_in_2"], "f1o": I["ffn1_w_out_2"],
        "f2i": I["ffn2_w_in_2"], "f2o": I["ffn2_w_out_2"], "ewi": I["even_w_in_2"][0],
        "wg2f": I["gla_wg2_f_2"][0], "wg2b": I["gla_wg2_b_2"][0], "uq": I["mla_w_uq_2"][0],
        "ukv": I["mla_w_ukv_2"][0], "ewo": I["even_w_out_2"][0], "nwi": I["na_w_in_2"][0],
        "nwo": I["na_w_out_2"][0],
    }
    arrays = {k: np.ascontiguousarray(a) for k, a in arrays.items()}

    def program(plan):
        nc = _bacc.Bacc("TRN2", target_bir_lowering=False, num_devices=1)
        dram = {k: nc.dram_tensor("in_" + k, a.shape, F32, kind="ExternalInput").ap() for k, a in arrays.items()}
        out = nc.dram_tensor("out_0", (1024, 256), F32, kind="ExternalOutput").ap()
        return nc, build(nc, dram, out, plan, MODE)

    _, plan = program(None)
    nc, _ = program(plan)
    r = _run(nc, [{"in_" + k: a for k, a in arrays.items()}], core_ids=[0])
    return np.ascontiguousarray(r.results[0]["out_0"].T)[None]
```

```python
from contextlib import ExitStack

import concourse.bass as bass
from concourse import mybir
import numpy as np

F32 = mybir.dt.float32
F32R = mybir.dt.float32r
U32 = mybir.dt.uint32
ALU = mybir.AluOpType
ACT = mybir.ActivationFunctionType
AX = mybir.AxisListType
MUL, ADD, SUB, MIN, MAX = ALU.mult, ALU.add, ALU.subtract, ALU.min, ALU.max
ALPHA1 = 2.0 ** 0.25
ALPHA2 = 4.0 ** 0.25
NSLOT = 3
SLOT = 2048

VEC = [("c", 8), ("cc", 8), ("b_ada", 48), ("b_gate", 16), ("conv_w", 120), ("conv_b", 24), ("ng", 16),
       ("pscale", 8), ("ln1g", 8), ("ln1b", 8), ("ln2g", 8), ("ln2b", 8), ("dskip", 16), ("dtb", 1),
       ("alog", 1), ("c2", 8), ("cc2", 8), ("ada_b", 144), ("bgf", 2), ("bgb", 2), ("gng", 1), ("qng", 3),
       ("kvng", 1)]
VOFF, _n = {}, 0
for _k, _c in VEC:
    VOFF[_k] = _n
    _n += _c
NVEC = _n

CST = [("ident", 128), ("triu", 128), ("tril", 128), ("rsw", 64), ("cos", 256), ("sin", 256), ("pool", 1024),
       ("namask", 64), ("glam", 15 * 128), ("iota8", 8),
       ("iotar", 128), ("iotac", 1)]
COFF, _n = {}, 0
for _k, _c in CST:
    COFF[_k] = _n
    _n += _c
NCST = _n


def constants():
    out = np.zeros((128, NCST), np.float32)

    def put(key, a):
        out[:a.shape[0], COFF[key]:COFF[key] + a.shape[1]] = a

    i = np.arange(128)
    put("ident", np.eye(128, dtype=np.float32))
    put("triu", (i[:, None] <= i[None, :]).astype(np.float32))
    put("tril", (i[:, None] >= i[None, :]).astype(np.float32))
    r = np.zeros((64, 64), np.float32)
    for a in range(32):
        r[2 * a + 1, 2 * a] = -1.0
        r[2 * a, 2 * a + 1] = 1.0
    put("rsw", np.concatenate([r, r]))
    t = np.arange(256)
    inv = (np.float32(10000.0) ** (-np.arange(16, dtype=np.float32) / np.float32(16))).astype(np.float32)
    ang = np.concatenate([(t // 64).astype(np.float32)[:, None] * inv, (t % 64).astype(np.float32)[:, None] * inv], -1)
    put("cos", np.tile(np.repeat(np.cos(ang).T, 2, axis=0), (2, 1)).astype(np.float32))
    put("sin", np.tile(np.repeat(np.sin(ang).T, 2, axis=0), (2, 1)).astype(np.float32))
    p = np.zeros((4, 4, 64), np.float32)
    for g, k in enumerate((2, 4, 8, 16)):
        def cnt(n):
            a = np.arange(n)
            return (np.clip(a - k // 2 + k, 0, n) - np.clip(a - k // 2, 0, n)).astype(np.float32)
        p[g] = 1.0 / (cnt(4)[:, None] * cnt(64)[None, :])
    put("pool", np.broadcast_to(p.reshape(1, 1024), (128, 1024)))
    c = np.arange(128) % 64
    s = np.clip(c - 8, 0, 48)[:, None]
    k = np.arange(64)[None, :]
    put("namask", np.where((k >= s) & (k < s + 16), 0.0, -1e30).astype(np.float32))
    m = np.zeros((128, 15, 128), np.float32)
    for lv in range(7):
        h = 1 << lv
        same = (i[:, None] // (2 * h)) == (i[None, :] // (2 * h))
        low = (i[:, None] // h) % 2 == 0
        up = (i[None, :] // h) % 2 == 1
        m[:, lv] = same & low & up
        m[:, 7 + lv] = m[:, lv].T
    m[:, 14] = np.eye(128)
    put("glam", m.reshape(128, -1))
    put("iota8", np.broadcast_to(8.0 - np.arange(8, dtype=np.float32)[None], (128, 8)))
    put("iotar", np.broadcast_to(np.arange(128, dtype=np.float32)[None], (128, 128)))
    put("iotac", np.arange(128, dtype=np.float32)[:, None])
    return out


class Queue:

    def __init__(self, sem):
        self.sem, self.n, self.items, self.seen = sem, 0, [], {}

    def wait(self, *toks):
        for s, v in toks:
            if self.seen.get(id(s), 0) < v:
                self.seen[id(s)] = v
                self.items.append(lambda e, s=s, v=v: e.wait_ge(s, v))

    @property
    def last(self):
        return (self.sem, self.n)

    def run(self, eng):
        for f in self.items:
            f(eng)


class Vec(Queue):

    def do(self, f, *toks, c=1):
        if c and self.n:
            self.wait((self.sem, self.n))
        self.wait(*toks)
        self.n += 1
        self.items.append(lambda e: f(e).then_inc(self.sem, 1))
        return self.last

    def tt(self, o, a, b, op, *t, c=1):
        return self.do(lambda e: e.tensor_tensor(o, a, b, op), *t, c=c)

    def ts(self, o, a, s1, s2, o1, o2, *t, c=1):
        if s2 is None:
            return self.do(lambda e: e.tensor_scalar(o, a, s1, None, o1), *t, c=c)
        return self.do(lambda e: e.tensor_scalar(o, a, s1, s2, o1, o2), *t, c=c)

    def stt(self, o, a, s, b, o1, o2, *t, c=1):
        return self.do(lambda e: e.scalar_tensor_tensor(out=o, in0=a, scalar=s, in1=b, op0=o1, op1=o2), *t, c=c)

    def cp(self, o, a, *t, c=1):
        return self.do(lambda e: e.tensor_copy(o, a), *t, c=c)

    def rec(self, x, *t, c=1):
        return self.do(lambda e: e.reciprocal(x, x), *t, c=c)

    def red(self, o, a, op, *t, c=1):
        return self.do(lambda e: e.tensor_reduce(o, a, AX.X, op), *t, c=c)

    def act(self, o, a, f, *t, c=1, **k):
        return self.do(lambda e: e.activation(o, a, f, **k), *t, c=c)


class Mat(Queue):

    def mm(self, o, w, x, start, stop, skip=False):
        self.items.append([o, w, x, start, stop, skip, None])

    def tr(self, o, a, ident):
        self.items.append([o, a, ident, None, None, None, None])

    def mark(self):
        it = self.items[-1]
        if it[6] is None:
            self.n += 1
            it[6] = True
        return self.last

    def run(self, eng):
        for it in self.items:
            if not isinstance(it, list):
                it(eng)
                continue
            o, w, x, start, stop, skip, inc = it
            if start is None:
                r = eng.transpose(o, w, x)
            elif skip:
                r = eng.matmul(o, w, x, start=start, stop=stop, skip_group_check=True)
            else:
                r = eng.matmul(o, w, x, start=start, stop=stop)
            if inc:
                r.then_inc(self.sem, 1)


class Bank:
    def __init__(self, t):
        self.t, self.free = t, []


class Arena:
    def __init__(self, t, n):
        self.t, self.n, self.at = t, n, 0

    def get(self, *dims):
        k = 1
        for d in dims:
            k *= d
        a = self.t[:, self.at:self.at + k]
        self.at += k
        assert self.at <= self.n, (self.at, self.n)
        if len(dims) == 2:
            return a.rearrange("p (a b) -> p a b", a=dims[0])
        if len(dims) == 3:
            return a.rearrange("p (a b c) -> p a b c", a=dims[0], b=dims[1])
        return a


class Ring:

    def __init__(self, K, plan, sems):
        self.K, self.plan, self.asked, self.sems = K, plan, [], sems
        self.until = 10 ** 9
        self.loaded = self.cut = self.used = self.base = 0
        self.raw_free, self.done, self.part, self.cuts = {}, {}, {}, {}

    def spec(self, j):
        return self.plan[j]

    def advance(self, cut=True):
        K = self.K
        while True:
            j = self.loaded
            moved = False
            if j < min(len(self.plan), self.until) and (j < self.base + NSLOT or j - NSLOT in self.raw_free):
                name, lead, row, kt, col, cols, split = self.plan[j]
                if j >= self.base + NSLOT:
                    K.D.wait(*self.raw_free[j - NSLOT])
                src = K.dram[name] if lead is None else K.dram[name][lead]
                src = src[row:row + kt * 128, col:col + cols].rearrange("(k p) n -> p k n", p=128)
                dst = K.RAW[:, j % NSLOT, 0:kt * cols].rearrange("p (k n) -> p k n", k=kt)
                K.dma(dst, src, self.sems[j % NSLOT])
                self.loaded += 1
                moved = True
            j = self.cut
            if cut and j < self.loaded and j <= self.used + 2 and (j < self.base + NSLOT or j - NSLOT in self.done):
                name, lead, row, kt, col, cols, split = self.plan[j]
                here = (self.sems[j % NSLOT], 16 * (j // NSLOT + 1))
                if split:
                    n = kt * cols
                    free = self.done[j - NSLOT] if j >= self.base + NSLOT else []
                    raw = K.RAW[:, j % NSLOT, 0:n]
                    a = K.S.act(K.HR[:, j % NSLOT, 0:n], raw, ACT.Copy, here, *free, c=0)
                    b = K.V.tt(K.LR[:, j % NSLOT, 0:n], raw, K.HR[:, j % NSLOT, 0:n].bitcast(F32), SUB, here, a,
                               *free, c=0)
                    self.cuts[j] = [a, b]
                    self.raw_free[j] = [b]
                else:
                    self.cuts[j] = [here]
                self.cut += 1
                moved = True
            if not moved:
                return

    def get(self, *spec):
        self.asked.append(spec)
        j = len(self.asked) - 1
        if self.plan is None or j >= len(self.plan):
            self.plan = (self.plan or []) + [spec]
        assert self.plan[j] == spec and j < self.until, (j, self.plan[j], spec)
        self.used = j
        self.advance()
        assert self.cut > j, j
        return W(self, j, spec)


class W:
    def __init__(self, ring, j, spec):
        K = ring.K
        _, _, _, kt, _, cols, split = spec
        self.ring, self.j, self.split, self.toks = ring, j, split, ring.cuts[j]

        def view(t):
            return t[:, j % NSLOT, 0:kt * cols].rearrange("p (k n) -> p k n", k=kt)

        if split:
            self.hi, self.lo = view(K.HR), view(K.LR)
        else:
            self.f = view(K.RAW)

    def end(self, tok):
        self.ring.done[self.j] = [tok]
        if not self.split:
            self.ring.raw_free[self.j] = [tok]


class X3:

    def __init__(self, hi, lo):
        self.hi, self.lo, self.ready, self.free = hi, lo, [], []


class Kern:
    def __init__(self, nc, dram, plan, ctx):
        self.nc, self.dram, self.ctx = nc, dram, ctx
        sem = self.sem
        self.T, self.V, self.S, self.G = Mat(sem("s_pe")), Vec(sem("s_dve")), Vec(sem("s_act")), Vec(sem("s_pool"))
        self.D = Queue(None)
        plan = plan or {}
        self.plans, self.asked = plan, {}
        self.s_in, self.n_in, self.groups = None, 0, 0
        self.ring = Ring(self, plan.get("main"), [sem(f"s_ring{i}") for i in range(NSLOT)])
        self.ring.until = plan.get("split", 10 ** 9)
        self.asked["main"] = self.ring.asked
        sb = self.sb
        self.RAW = sb("RAW", [128, NSLOT, SLOT], F32)
        self.HR = sb("HR", [128, NSLOT, SLOT], F32R)
        self.LR = sb("LR", [128, NSLOT, SLOT], F32R)
        self.X = sb("X", [128, 8, 512], F32)
        self.AH = sb("AH", [128, 4096], F32R)
        self.AL = sb("AL", [128, 4096], F32R)
        self.vec = sb("vec", [128, NVEC], F32)
        self.ident = sb("ident", [128, 128], F32)
        self.onesD = sb("onesD", [128, 128], F32)
        self.ones = sb("ones", [128, 256], F32)
        self.eps = sb("eps", [128, 2], F32)
        self.mod1 = sb("mod1", [128, 48, 2], F32)
        self.mod2 = [sb(f"mod2{i}", [128, 72, 2], F32) for i in range(2)]
        self.csil = sb("csil", [128, 8, 4], F32)
        self.CS = sb("CS", [128, 184], F32R)
        self.mrow = [sb(f"mrow{i}", [8, 256], F32) for i in range(2)]
        self.mst = [sb(f"mst{i}", [128, 8, 8], F32) for i in range(2)]
        self.row_free, self.mst_free, self.jobs, self.nrow = [[], []], [[], []], [], 0
        self.lo, self.hi = 0, 8
        self.extra = 0
        self.banks = [Bank(ctx.enter_context(nc.psum_tensor(f"ps{i}", [128, 512], F32))) for i in range(8)]
        self.bi = 0
        self.A = X3(self.AH, self.AL)

    def sem(self, name):
        return self.ctx.enter_context(self.nc.semaphore(name))

    def sb(self, name, shape, dt, ctx=None):
        return (ctx or self.ctx).enter_context(self.nc.sbuf_tensor(name, shape, dt))

    def v(self, key, i=0, n=1):
        return self.vec[:, VOFF[key] + i:VOFF[key] + i + n]

    def dma(self, dst, src, sem):
        self.D.items.append(lambda e: e.dma_start(dst, src).then_inc(sem, 16))

    def load(self, dst, src):
        if self.s_in is None:
            self.s_in, self.n_in = self.sem(f"s_in{self.groups}"), 0
            self.groups += 1
        self.dma(dst, src, self.s_in)
        self.n_in += 16

    def landed(self):
        t, self.s_in = (self.s_in, self.n_in), None
        return t

    def cst(self, key, dst, rows=128, off=0, n=None):
        n = n or dict(CST)[key]
        self.load(dst, self.dram["cst"][0:rows, COFF[key] + off:COFF[key] + off + n])

    def phase(self, name):
        pass

    def step(self, n=1):
        while n and self.jobs:
            if next(self.jobs[0], None) is None:
                self.jobs.pop(0)
            else:
                n -= 1

    def finish(self, job):
        while job in self.jobs:
            self.step()
        self.V.wait(self.V.last)
        return self.V.last

    def bank(self, lo=None, hi=None):
        lo, hi = self.lo if lo is None else lo, self.hi if hi is None else hi
        self.bi += 1
        if self.bi >= hi or self.bi < lo:
            self.bi = lo
        b = self.banks[self.bi]
        self.T.wait(*b.free)
        return b

    def barrier(self, pe=True):
        ends = [q.last for q in (self.T, self.V, self.S, self.G) if q.n]
        for q in (self.T, self.V, self.S, self.G, self.D)[0 if pe else 1:]:
            q.wait(*ends)

    def prod(self, o, w, ws, x, xs, first, last, skip=False):
        if w.split:
            self.T.mm(o, w.hi[ws], x.hi[xs], first, False, skip)
            self.T.mm(o, w.hi[ws], x.lo[xs], False, False, skip)
            self.T.mm(o, w.lo[ws], x.hi[xs], False, last, skip)
        else:
            self.T.mm(o, w.f[ws], x[xs], first, last, skip)

    def linear(self, name, lead, kt, c0, nt, x, n, evac, row=0, split=True, xtoks=(), bg=True, per=None):
        T = self.T
        per = per or SLOT // kt // 128
        xk = xtoks if xtoks and isinstance(xtoks[0], list) else []
        if xk:
            xtoks = ()
        for a in range(0, nt, per):
            m = min(per, nt - a)
            w = self.ring.get(name, lead, row, kt, c0 + a * 128, m * 128, split)
            T.wait(*w.toks, *xtoks)
            if xk and a == 0:
                bs = [self.bank() for _ in range(m)]
                for k in range(kt):
                    T.wait(*xk[k])
                    for i in range(m):
                        self.prod(bs[i].t[:, 0:n], w, (slice(None), k, slice(i * 128, i * 128 + 128)), x,
                                  (slice(None), k, slice(0, n)), k == 0, k == kt - 1)
                tok = T.mark()
                w.end(tok)
                for i in range(m):
                    bs[i].free = evac(i, bs[i].t[:, 0:n], tok)
                if bg:
                    self.step()
                continue
            for i in range(m):
                b = self.bank()
                for k in range(kt):
                    self.prod(b.t[:, 0:n], w, (slice(None), k, slice(i * 128, i * 128 + 128)), x,
                              (slice(None), k, slice(0, n)), k == 0, k == kt - 1)
                tok = T.mark()
                if i == m - 1:
                    w.end(tok)
                b.free = evac(a + i, b.t[:, 0:n], tok)
            if bg:
                self.step()
        return T.last

    def split(self, dst_hi, dst_lo, src, *toks):
        a = self.S.act(dst_hi, src, ACT.Copy, *toks, c=0)
        b = self.V.tt(dst_lo, src, dst_hi.bitcast(F32), SUB, a, *toks, c=0)
        return [a, b]

    def reopen(self):
        self.ring.until = 10 ** 9
        self.asked["split"] = len(self.ring.asked)
        self.ring.base = len(self.ring.asked)
        self.ahead(False)

    def ahead(self, cut=True):
        if self.plans:
            self.ring.advance(cut)

    def branch(self, name, flag, taken, body):
        self.barrier()
        main = self.T, self.V, self.S, self.G, self.D, self.ring
        sem = self.sem
        self.T, self.V, self.S, self.G = Mat(sem(f"{name}_pe")), Vec(sem(f"{name}_dve")), \
            Vec(sem(f"{name}_act")), Vec(sem(f"{name}_pool"))
        self.D = Queue(None)
        self.ring = Ring(self, self.plans.get(name), [sem(f"{name}_ring{i}") for i in range(NSLOT)])
        self.asked[name] = self.ring.asked
        for b in self.banks:
            b.free = []
        self.A.free = []
        body()
        self.barrier()
        for b in self.banks:
            b.free = []
        self.A.free = []
        self.extra += sum(1 for x in self.T.items if isinstance(x, list)) * (name == "some")
        subs = self.T, self.V, self.S, self.G, self.D
        self.T, self.V, self.S, self.G, self.D, self.ring = main
        for q, sub in zip(main, subs):
            def part(e, sub=sub):
                v = e.value_load(flag)
                with e.If(v > 0) if taken else e.If(v < 1):
                    sub.run(e)
            q.items.append(part)

    def mean_begin(self, n):
        self.hi = 7
        self.mb = self.banks[7]
        self.mb_n, self.mb_k = n, 0
        self.T.wait(*self.mb.free)

    def mean_add(self, xk, tok):
        self.T.wait(tok)
        self.T.mm(self.mb.t[:, 0:self.mb_n], self.onesD[:, :], xk, self.mb_k == 0, self.mb_k == 7)
        self.mb_k += 1
        self.T.mark()

    def layer_norm(self, x, n, eps, sq, rs, post, pre=None):
        T, V, S = self.T, self.V, self.S
        b, b2 = self.mb, self.banks[6]
        self.hi = 6
        T.wait(*b2.free)
        t = T.last
        for k in range(8):
            t1 = V.tt(x[:, k, :], x[:, k, :], b.t[:, 0:n], SUB, t, c=0)
            t2 = S.act(sq[:, k, :], x[:, k, :], ACT.Square, t1, c=0)
            T.wait(t2)
            T.mm(b2.t[:, 0:n], self.onesD[:, :], sq[:, k, :], k == 0, k == 7)
        b.free = [t1]
        t = T.mark()
        t = S.act(rs, b2.t[:, 0:n], ACT.Sqrt, t, bias=self.eps[:, eps:eps + 1])
        b2.free = [t]
        self.hi = 8
        t = V.rec(rs, t)
        out, scaled = [], []
        for k in range(10):
            if k < 8:
                scaled.append(V.tt(x[:, k, :], x[:, k, :], rs, MUL, t, c=0))
                if pre:
                    scaled[k] = pre(k)
            if k >= 2:
                out.append(post(k - 2, scaled[k - 2]) or [scaled[k - 2]])
        return out

    def transpose_to(self, blocks, width):
        b = self.bank()
        for src, col in blocks:
            q, p = src.shape[0], src.shape[1]
            sp = src.start_partition()
            self.T.tr(b.t[0:p, col:col + q], src, self.ident[sp:sp + q, sp:sp + q])
        return b, self.T.mark()


def setup(K):
    T, V, S, G, D = K.T, K.V, K.S, K.G, K.D
    K.load(K.vec[:, :], K.dram["vec"])
    K.cst("ident", K.ident[:, :])
    K.load(K.X[:, :, 256:512], K.dram["xT"].rearrange("(k p) n -> p k n", p=128))
    K.load(K.X[:, :, 0:256], K.dram["ctxT"].rearrange("(k p) n -> p k n", p=128))
    t = K.t_in = K.landed()
    G.do(lambda e: e.memset(K.onesD[:, :], 1.0 / 1024), c=0)
    G.do(lambda e: e.memset(K.ones[:, :], 1.0), c=0)
    G.do(lambda e: e.memset(K.eps[:, 0:1], 1e-5), c=0)
    G.do(lambda e: e.memset(K.eps[:, 1:2], 1e-6), c=0)
    for i, key in enumerate(("c", "cc", "c2", "cc2")):
        t = S.act(K.csil[:, :, i], K.v(key, 0, 8), ACT.Silu, t, c=0)
    V.do(lambda e: e.memset(K.CS[:, :].bitcast(F32), 0.0), c=0)
    cs = K.CS[:, 0:64].rearrange("p (k c) -> p k c", k=8)
    V.cp(cs[:, :, 0:4], K.csil[:, :, :], t)
    K.t_cs = V.tt(cs[:, :, 4:8], K.csil[:, :, :], cs[:, :, 0:4].bitcast(F32), SUB)
    K.barrier()


def conditioning(K, name, lead, t0, nt, v0, bias, dst, fix):
    T, V, S = K.T, K.V, K.S
    for g in range(t0, t0 + nt, 8):
        j = (g // 8) % 2
        st = K.mst[j]
        for a in range(0, 8, 2):
            w = K.ring.get(name, lead, 0, 8, (g + a) * 128, 256, True)
            T.wait(K.t_cs, *w.toks)
            b = K.bank()
            for k in range(8):
                T.mm(b.t[:, 0:256], K.CS[:, 8 * k:8 * k + 128], w.hi[:, k, :], k == 0, False)
                T.mm(b.t[:, 0:256], K.CS[:, 8 * k:8 * k + 128], w.lo[:, k, :], False, k == 7)
            tk = T.mark()
            w.end(tk)
            i = K.nrow % 2
            K.nrow += 1
            row = K.mrow[i]
            t = S.act(row[:, :], b.t[0:8, 0:256], ACT.Copy, tk, *K.row_free[i], c=0)
            b.free = [t]
            yield True
            T.wait(t)
            b, tk = K.transpose_to([(row[:, q * 128:q * 128 + 128], 8 * q) for q in range(2)], 8)
            K.row_free[i] = [tk]
            t = S.act(st[:, a:a + 2, :], b.t[:, 0:16].rearrange("p (q c) -> p q c", q=2), ACT.Copy, tk,
                      *K.mst_free[j], c=0)
            b.free = [t]
        o = dst[:, g:g + 8, :]
        V.tt(o, st[:, :, v0:v0 + 2], st[:, :, 4 + v0:6 + v0], ADD, t)
        K.mst_free[j] = [V.last]
        V.tt(o, o, bias[:, g:g + 8].unsqueeze(2).broadcast_to([128, 8, 2]), ADD)
        how = fix.get(g // 8)
        if how == 1:
            V.ts(o, o, 1.0, None, ADD, None)
        elif how == 2:
            V.ts(o, o, 0.5, None, MUL, None)


def scaled_split(K, src, k, n, dst, mods, tmp, used, toks):
    S = K.S
    halves = [(0, 256, 1), (256, 512, 0)] if n == 512 else [(0, 256, 0)]
    tb = tmp[:, k % 2, 0:n]
    for a, z, v in halves:
        sc, sh = mods(k, v)
        t = S.act(tb[:, a:z], src[:, a:z], ACT.Identity, *toks, *used[k % 2], *dst.free, c=0, scale=sc, bias=sh)
    used[k % 2] = K.split(dst.hi[:, k * n:(k + 1) * n], dst.lo[:, k * n:(k + 1) * n], tb, t)
    return used[k % 2]


def modulated(K, src, dst, n, sc, sh, tmp, toks):
    V = K.V
    used = [[], []]
    ready = []
    halves = [(0, 256, 1), (256, 512, 0)] if n == 512 else [(0, 256, 0)]
    for k in range(8):
        tb = tmp[:, k % 2, 0:n]
        for a, z, v in halves:
            t = V.ts(tb[:, a:z], src[:, k, a:z], sc(k, v), sh(k, v), MUL, ADD, *toks, *used[k % 2],
                     *dst.free, c=0)
        used[k % 2] = K.split(dst.hi[:, k * n:(k + 1) * n], dst.lo[:, k * n:(k + 1) * n], tb, t)
        ready = used[k % 2]
    dst.ready = ready
    return ready


class View3:
    split = True

    def __init__(self, x, kt, n, at=0):
        self.hi = x.hi[:, at:at + kt * n].rearrange("p (k n) -> p k n", k=kt)
        self.lo = x.lo[:, at:at + kt * n].rearrange("p (k n) -> p k n", k=kt)


def block_one(K, stop=None):
    T, V, S, G, D = K.T, K.V, K.S, K.G, K.D
    ctx = ExitStack()
    NAR = 19900
    A = Arena(K.sb("ar1", [128, NAR], F32, ctx), NAR)
    X, A3 = K.X, K.A
    mod = K.mod1
    fix = {1: 1, 4: 1}
    K.phase("start")
    first = conditioning(K, "w_ada", None, 0, 16, 0, K.v("b_ada", 0, 48), mod, fix)
    K.jobs.append(first)
    t_mod = K.finish(first)
    rest = conditioning(K, "w_ada", None, 16, 32, 0, K.v("b_ada", 0, 48), mod, fix)
    K.jobs.append(rest)
    fix2 = {1: 1, 4: 1, 7: 1, 2: 2, 8: 2}
    K.ada2 = [conditioning(K, "ada_w", l, 0, 72, 2, K.v("ada_b", 72 * l, 72), K.mod2[l], fix2) for l in range(2)]
    K.jobs.append(K.ada2[0])

    def mcol(i):
        return lambda k, v: mod[:, 8 * i + k, v:v + 1]

    xsC, xsL = A.get(16, 256), A.get(16, 256)
    BT, CT = A.get(4, 512), A.get(4, 256)
    dtT, aT, acs = A.get(512), A.get(512), A.get(512)
    tokC, tokL, dtL = A.get(2, 64), A.get(2, 64), A.get(2, 64)
    triu, tril = A.get(128), A.get(128)
    K.cst("triu", triu)
    K.cst("tril", tril)
    tri_t = K.landed()
    base = A.at
    tmp = A.get(2, 512)
    h = View3(A3, 8, 512)
    used, ht = [[], []], []
    for k in range(8):
        ht.append(scaled_split(K, X[:, k, :], k, 512, A3, lambda k, v: (mcol(1)(k, v), mcol(0)(k, v)), tmp, used,
                               [t_mod, K.t_in]))
    K.phase("xbc")
    e1, e2, e3 = A.get(512), A.get(512), A.get(512)
    negA = A.get(1)
    r = slice(0, 64)
    K.linear("w_in", None, 8, 5120, 1, h, 512, lambda m, ps, tok: [
        V.ts(dtT[r], ps[r, :], K.v("dtb")[r], None, ADD, None, tok, c=0)], xtoks=ht)
    t = V.stt(e1[r], dtT[r], -1.0, dtT[r], MUL, MIN)
    t = S.act(e1[r], e1[r], ACT.Exp, t)
    t = V.ts(e2[r], e1[r], 1.0, None, ADD, None, t)
    t = S.act(e3[r], e2[r], ACT.Ln, t)
    t = V.ts(aT[r], e2[r], 1.0, None, ALU.is_equal, None, t)
    t = V.stt(e2[r], e2[r], -1.0, aT[r], ADD, ADD, t)
    t = V.tt(e3[r], e3[r], aT[r], ADD)
    t = V.rec(e2[r])
    t = V.tt(e3[r], e3[r], e1[r], MUL)
    t = V.tt(e3[r], e3[r], e2[r], MUL)
    t = V.stt(dtT[r], dtT[r], 0.0, e3[r], MAX, ADD)
    t = S.act(negA[r], K.v("alog")[r], ACT.Exp)
    t = V.ts(negA[r], negA[r], -1.0, None, MUL, None, t)
    t = V.ts(aT[r], dtT[r], negA[r], None, MUL, None, t)
    for s in (0, 256):
        t = V.do(lambda e, s=s: e.tensor_tensor_scan(acs[0:32, s:s + 256], K.ones[0:32, 0:256],
                                                     aT[0:32, s:s + 256], 0.0, MUL, ADD))
        t = V.do(lambda e, s=s: e.tensor_tensor_scan(acs[32:64, s:s + 256][:, ::-1], K.ones[32:64, 0:256],
                                                     aT[32:64, s:s + 256][:, ::-1], 0.0, MUL, ADD), c=0)
    ta = S.act(e1[0:32, 0:256], acs[0:32, 0:256], ACT.Exp, t, bias=acs[0:32, 255:256], scale=-1.0)
    ta = S.act(e1[32:64, 0:256], acs[32:64, 0:256], ACT.Exp, t, bias=acs[32:64, 0:1], scale=-1.0)
    t = V.tt(e1[r, 0:256], e1[r, 0:256], dtT[r, 0:256], MUL, ta)
    t_dec = t
    pads = [A.get(2, 260) for _ in range(3)]
    accs = [A.get(2, 256) for _ in range(2)]
    zt = []
    for p in pads:
        G.do(lambda e, p=p: e.memset(p[:, :, 0:2], 0.0), c=0)
        zt.append(G.do(lambda e, p=p: e.memset(p[:, :, 258:260], 0.0), c=0))
    pad_free, acc_free = [[z] for z in zt], [[], []]

    silus = []

    def conv_tile(m, ps, tok):
        p, a = pads[m % 3], accs[m % 2]
        lat = m >= 20
        sl = slice(1, 2) if lat else slice(0, 2)
        n = 1 if lat else 2
        src = ps.rearrange("p (s n) -> p s n", s=n)
        t1 = S.act(p[:, sl, 2:258], src, ACT.Copy, tok, *pad_free[m % 3], c=0)
        t2 = S.act(a[:, sl, :], p[:, sl, 0:256], ACT.Identity, t1, *acc_free[m % 2], c=0,
                   scale=K.v("conv_w", m), bias=K.v("conv_b", m))
        for i in range(1, 5):
            t2 = V.stt(a[:, sl, :], p[:, sl, i:i + 256], K.v("conv_w", 24 * i + m), a[:, sl, :], MUL, ADD, t2)
        pad_free[m % 3] = [t2]
        silus.append((m, a, t2))
        if len(silus) > 1:
            silu()
        return [t1]

    def silu():
        m, a, t2 = silus.pop(0)
        if m < 16:
            S.act(xsC[:, m, :], a[:, 0, :], ACT.Silu, t2, c=0)
            t3 = S.act(xsL[:, m, :], a[:, 1, :], ACT.Silu, t2, c=0)
        elif m < 20:
            t3 = S.act(BT[:, m - 16, :].rearrange("p (s n) -> p s n", s=2), a[:, :, :], ACT.Silu, t2, c=0)
        else:
            t3 = S.act(CT[:, m - 20, :], a[:, 1, :], ACT.Silu, t2, c=0)
        acc_free[m % 2] = [t3]

    K.linear("w_in", None, 8, 2048, 6, h, 512, conv_tile)
    T.wait(t_dec)
    b, tk = K.transpose_to([(src[0:64, s + j * 128:s + j * 128 + 128], 64 * (2 * i + j))
                            for i, (src, s) in enumerate(((e1, 0), (acs, 256), (dtT, 256))) for j in range(2)], 64)
    for i, dst in enumerate((tokC, tokL, dtL)):
        t = V.cp(dst, b.t[:, 128 * i:128 * i + 128].rearrange("p (j c) -> p j c", j=2), tk, c=0)
    b.free = [t]
    K.linear("w_in", None, 8, 2816, 14, h, 512, lambda m, ps, tok: conv_tile(6 + m, ps, tok))
    hl = HalfView(h, 256)
    K.linear("w_in", None, 8, 4608, 4, hl, 256, lambda m, ps, tok: conv_tile(20 + m, ps, tok))
    silu()
    K.barrier()
    K.phase('ssd')
    A.at = base
    Bk = A.get(2, 128)
    xd = A.get(2, 2, 512)
    S0 = A.get(2, 512)
    CB = A.get(2, 384)
    NB = 6
    SEG = [A.get(384) for _ in range(NB)]
    EC = [X[:, i, 0:256] for i in range(NB)]
    seg_free = [[] for _ in range(NB)]
    n = 0
    s0_t, yfree = [], []
    for g in range(4):
        b, tk = K.transpose_to([(BT[:, g, j * 128:j * 128 + 128], 128 * j) for j in range(2)], 128)
        tB = S.act(Bk, b.t[:, 0:256].rearrange("p (j c) -> p j c", j=2), ACT.Copy, tk, *s0_t, c=0)
        b.free = [tB]
        prev_s = s0_t
        for j in range(2):
            b, tk = K.transpose_to([(xsC[:, 4 * g + q, j * 128:j * 128 + 128], 128 * q) for q in range(4)], 128)
            for d in range(2):
                wcol = tokC[:, j, 32 * d + 8 * g:32 * d + 8 * g + 8].unsqueeze(2).broadcast_to([128, 8, 64])
                t = V.tt(xd[:, d, j, :].rearrange("p (h c) -> p h c", h=8),
                         b.t[:, :].rearrange("p (h c) -> p h c", h=8), wcol, MUL, tk, *prev_s, *yfree, c=0)
            b.free = [t]
        T.wait(t, tB)
        for d in range(2):
            b = K.bank()
            for j in range(2):
                T.mm(b.t[:, :], Bk[:, j, :], xd[:, d, j, :], j == 0, j == 1)
            tk = T.mark()
            ts = S.act(S0[:, d, :], b.t[:, :], ACT.Copy, tk, *prev_s, *yfree, c=0)
            b.free = [ts]
        s0_t = [ts]
        for j in range(2):
            b = K.bank()
            T.mm(b.t[:, 0:256], BT[:, g, 256 + j * 128:384 + j * 128], CT[:, g, :], True, True)
            tk = T.mark()
            if j == 0:
                V.tt(CB[:, 0, 0:128], b.t[:, 0:128], triu, MUL, tk, tri_t, *yfree, c=0)
                V.cp(CB[:, 0, 128:256], b.t[:, 128:256], c=0)
                t = V.tt(CB[:, 1, 0:128], b.t[:, 0:128], tril, MUL, c=0)
            else:
                V.tt(CB[:, 0, 256:384], b.t[:, 128:256], triu, MUL, tk, c=0)
                V.cp(CB[:, 1, 128:256], b.t[:, 0:128], c=0)
                t = V.tt(CB[:, 1, 256:384], b.t[:, 128:256], tril, MUL, c=0)
            b.free = [t]
        tCB = t
        for j in range(2):
            b, tk = K.transpose_to([(xsL[:, 4 * g + q, j * 128:j * 128 + 128], 128 * q) for q in range(4)], 128)
            for d in range(2):
                wcol = dtL[:, j, 32 * d + 8 * g:32 * d + 8 * g + 8].unsqueeze(2).broadcast_to([128, 8, 64])
                t = V.tt(xd[:, d, j, :].rearrange("p (h c) -> p h c", h=8),
                         b.t[:, :].rearrange("p (h c) -> p h c", h=8), wcol, MUL, tk, T.last, c=0)
            b.free = [t]
        tx = t
        pend, diffs = [], []

        def head_products(item, yb):
            hh, d, i, tg, tq = item
            T.wait(tg, tq, tx, *s0_t)
            po = 64 * (hh % 2)
            o = yb.t[po:po + 64, :]
            c = (hh % 8) * 64
            T.mm(o[:, 0:256], S0[:, d, c:c + 64], EC[i], d == 0, False)
            for j in range(2):
                cols = (slice(0, 256) if j == 0 else slice(128, 256)) if d == 0 else \
                    (slice(0, 128) if j == 0 else slice(0, 256))
                so = (0 if j == 0 else 256) if d == 0 else (0 if j == 0 else 128)
                T.mm(o[:, cols], xd[:, d, j, c:c + 64], SEG[i][:, so:so + cols.stop - cols.start], False,
                     d == 1 and j == 1)
            seg_free[i] = [T.mark()]

        K.hi = 6
        todo = [(hh, d) for hh in range(8 * g, 8 * g + 8) for d in range(2)]
        yb = None
        for q in range(len(todo) + LAG):
            if q < len(todo):
                hh, d = todo[q]
                i = n % NB
                n += 1
                row = 32 * d + hh
                b = K.bank()
                T.mm(b.t[:, 0:256], K.ident[0:64, row:row + 1].broadcast_to([64, 128]), acs[0:64, 256:512],
                     True, True)
                tk = T.mark()
                if d == 0:
                    parts = [(slice(0, 256), slice(0, 256), 0), (slice(128, 256), slice(256, 384), 1)]
                else:
                    parts = [(slice(0, 128), slice(0, 128), 0), (slice(0, 256), slice(128, 384), 1)]
                te = S.act(EC[i], b.t[:, 0:256], ACT.Exp, tk, *seg_free[i], c=0)
                for src, dst, j in parts:
                    t = V.ts(SEG[i][:, dst], b.t[:, src], tokL[:, j, row:row + 1], 0.0, SUB, MIN, te,
                             *seg_free[i], c=0)
                b.free = [te, t]
                tq = G.tt(EC[i], EC[i], CT[:, g, :], MUL, te, c=0)
                diffs.append((hh, d, i, t, tq))
            if len(diffs) > (q < len(todo)):
                hh, d, i, t, tq = diffs.pop(0)
                t2 = S.act(SEG[i], SEG[i], ACT.Exp, t, c=0)
                tg = (V if d == 0 else G).tt(SEG[i], SEG[i], CB[:, d, :], MUL, t2, tCB, c=0)
                pend.append((hh, d, i, tg, tq))
            if q % 2 == 1:
                K.step()
            if q >= LAG:
                item = pend.pop(0)
                if item[0] % 2 == 0 and item[1] == 0:
                    yb = K.bank(6, 8)
                head_products(item, yb)
                if item[0] % 2 == 1 and item[1] == 1:
                    m = item[0] // 2
                    t = V.stt(xsL[:, m, :], xsL[:, m, :], K.v("dskip", m), yb.t[:, 0:256], MUL, ADD, T.last,
                              c=0)
                    yb.free = [t]
        K.hi = 8
        yfree = [T.last]
        s0_t = [ts, T.last]
    K.barrier()
    K.phase('z')
    A.at = base
    gates = xsC
    u = BT.rearrange("p a b -> p (a b)").rearrange("p (m n) -> p m n", m=8)
    K.linear("w_in", None, 8, 5184, 8, hl, 256,
             lambda m, ps, tok: [S.act(u[:, m, :], ps, ACT.Copy, tok, c=0)])
    t_u = S.last
    pc = A.get(1024)
    K.cst("pool", pc)
    t_pc = K.landed()
    P0 = [A.get(4, 80) for _ in range(2)]
    P1 = [A.get(4, 80) for _ in range(2)]
    for p in P0:
        t_z = G.do(lambda e, p=p: e.memset(p, 0.0), c=0)
    for p in P1:
        t_z = G.do(lambda e, p=p: e.memset(p, 0.0), c=0)
    G.wait(t_z, t_u, t_pc)
    df = X[:, :, 0:256]
    for m in range(8):
        k = (2, 4, 8, 16)[m // 2]
        uu = u[:, m, :].rearrange("p (r c) -> p r c", r=4)
        a, b2 = P0[m % 2], P1[m % 2]
        c = slice(8, 72)
        if k == 2:
            G.tt(a[:, 1:4, c], uu[:, 1:4, :], uu[:, 0:3, :], ADD)
            G.cp(a[:, 0:1, c], uu[:, 0:1, :])
        elif k == 4:
            G.tt(a[:, 0, c], uu[:, 0, :], uu[:, 1, :], ADD)
            G.tt(a[:, 3, c], uu[:, 2, :], uu[:, 3, :], ADD)
            G.tt(a[:, 1, c], a[:, 0, c], uu[:, 2, :], ADD)
            G.tt(a[:, 2, c], a[:, 3, c], uu[:, 1, :], ADD)
            G.tt(a[:, 2, c], a[:, 2, c], uu[:, 0, :], ADD)
            G.tt(a[:, 3, c], a[:, 3, c], uu[:, 1, :], ADD)
        else:
            G.tt(a[:, 0, c], uu[:, 0, :], uu[:, 1, :], ADD)
            G.tt(a[:, 0, c], a[:, 0, c], uu[:, 2, :], ADD)
            G.tt(a[:, 0, c], a[:, 0, c], uu[:, 3, :], ADD)
            G.cp(a[:, 1:4, c], a[:, 0:1, c].broadcast_to([128, 3, 64]))
        src, dst = a, b2
        G.tt(dst[:, :, 1:80], src[:, :, 0:79], src[:, :, 1:80], ADD)
        src, dst = dst, src
        sh, w_ = 1, 2
        while w_ < k:
            G.tt(dst[:, :, 8:72] if w_ * 2 == k else dst[:, :, 4:76],
                 (src[:, :, 8 - sh:72 - sh] if w_ * 2 == k else src[:, :, 4 - sh:76 - sh]),
                 (src[:, :, 8 + sh:72 + sh] if w_ * 2 == k else src[:, :, 4 + sh:76 + sh]), ADD)
            src, dst = dst, src
            sh, w_ = sh * 2, w_ * 2
        d = df[:, m, :].rearrange("p (r c) -> p r c", r=4)
        G.tt(d, src[:, :, 8:72], pc[:, (m // 2) * 256:(m // 2) * 256 + 256].rearrange("p (r c) -> p r c", r=4),
             MUL)
        t_df = G.tt(d, d, uu, SUB)
        G.do(lambda e, a=a: e.memset(a, 0.0))
        G.do(lambda e, b2=b2: e.memset(b2, 0.0))
    sil = [A.get(256) for _ in range(2)]
    sq = [A.get(256) for _ in range(2)]
    sil_free = [[], []]
    ssq = K.banks[7]
    T.wait(*ssq.free)
    sqt, squares = [], []

    def z_tile(m, ps, tok):
        i = m % 2
        t1 = S.act(sil[i], ps, ACT.Silu, tok, *sil_free[i], c=0)
        t2 = V.tt(xsL[:, m, :], xsL[:, m, :], sil[i], MUL, t1, c=0)
        t3 = S.act(sq[i], xsL[:, m, :], ACT.Square, t2, *(sqt[m - 2:m - 1] if m >= 2 else []), c=0)
        sil_free[i] = [t2]
        squares.append((m, t3))
        if m:
            square_sum()
        return [t1]

    def square_sum():
        m, t3 = squares.pop(0)
        T.wait(t3)
        T.mm(ssq.t[:, 0:256], K.onesD[:, :], sq[m % 2], m == 0, m == 15)
        sqt.append(T.mark())

    K.hi = 7
    K.linear("w_in", None, 8, 0, 16, hl, 256, z_tile)
    square_sum()
    K.hi = 8
    rz = A.get(256)
    t = S.act(rz, ssq.t[:, 0:256], ACT.Sqrt, T.last, bias=K.eps[:, 0:1], scale=0.5)
    ssq.free = [t]
    t_rz = V.rec(rz, t)
    K.linear("w_in", None, 8, 6208, 16, hl, 256,
             lambda m, ps, tok: [S.act(gates[:, m, :], ps, ACT.Sigmoid, tok, c=0, bias=K.v("b_gate", m))])
    t_g = S.last
    A3.free = [T.last]
    yv = View3(A3, 16, 256)
    ynt = []
    t_y = V.last
    for m in range(16):
        t = S.act(yv.hi[:, m, :], xsL[:, m, :], ACT.Copy, t_y, *A3.free, c=0, scale=K.v("ng", m))
        t2 = V.stt(yv.lo[:, m, :], xsL[:, m, :], K.v("ng", m), yv.hi[:, m, :].bitcast(F32), MUL, SUB, t, c=0)
        ynt.append([t, t2])
    merged = A.get(8, 256)

    def a_tile(m, ps, tok):
        V.tt(merged[:, m, :], ps, rz, MUL, tok, t_rz, c=0)
        t = V.last
        G.tt(merged[:, m, :], merged[:, m, :], gates[:, m, :], MUL, t, t_g, c=0)
        return [t]

    K.linear("w_branch_a", None, 16, 0, 8, yv, 256, a_tile, xtoks=ynt)
    A3.free = [T.last]
    K.phase('pool')
    yp, yp_t = xsL[:, 0:8, :], []
    for g in range(4):
        w = K.ring.get("pool_w", g, 0, 2, 0, 256, False)
        T.wait(*w.toks, t_df)
        for i in range(2):
            b = K.bank()
            for k in range(2):
                T.mm(b.t[:, 0:256], w.f[:, k, i * 128:i * 128 + 128], df[:, 2 * g + k, :], k == 0, k == 1)
            tk = T.mark()
            if i == 1:
                w.end(tk)
            m = 2 * g + i
            t = V.ts(yp[:, m, :], b.t[:, 0:256], K.v("pscale", m), None, MUL, None, tk, c=0)
            b.free = [t]
            yp_t.append(t)
    v8, vm = View3(A3, 8, 256), View3(A3, 8, 256, 2048)
    v8_free = A3.free
    tt_ = [K.split(v8.hi[:, m, :], v8.lo[:, m, :], yp[:, m, :], yp_t[m], *v8_free) for m in range(8)]
    gt = [A.get(256) for _ in range(2)]
    gfree = [[], []]
    merged_t, vm_t = [], []

    def b_tile(m, ps, tok):
        t1 = V.tt(gt[m % 2], ps, gates[:, 8 + m, :], MUL, tok, t_g, *gfree[m % 2], c=0)
        t2 = G.tt(merged[:, m, :], merged[:, m, :], gt[m % 2], ADD, t1)
        gfree[m % 2] = [t2]
        merged_t.append(t2)
        if m:
            merged_split(m - 1)
        return [t1]

    def merged_split(m):
        vm_t.append(K.split(vm.hi[:, m, :], vm.lo[:, m, :], merged[:, m, :], merged_t[m], *v8_free))

    K.linear("w_branch_b", None, 8, 0, 8, v8, 256, b_tile, xtoks=tt_)
    merged_split(7)
    XL = X[:, :, 256:512]

    t_a = G.ts(XL, XL, ALPHA1, None, MUL, None, *ht[7])
    K.finish(rest)
    K.finish(K.ada2[0])
    K.mean_begin(256)
    K.linear("w_out", None, 8, 0, 8, vm, 256, residual(K, XL, lambda m, v: mod[:, 16 + m, 0:1], LAT, [t_a]),
             xtoks=vm_t)
    A3.free = [T.last]
    K.barrier()
    ctx.close()
    ctx = ExitStack()
    NAR = 3200
    A = Arena(K.sb("ar2", [128, NAR], F32, ctx), NAR)
    sqb, rs = X[:, :, 0:256], A.get(256)
    h32 = A.get(8, 256)

    wr = A.get(8, 36)
    K.load(wr[:, :, 0:4], K.dram["w_rg"].rearrange("(k p) n -> p k n", p=128))
    for g in range(4):
        K.load(wr[:, :, 4 + 8 * g:12 + 8 * g], K.dram["w_re"][g].rearrange("(k p) n -> p k n", p=128))
    br = A.get(36)
    K.load(br[0:1, 0:4], K.dram["b_rg"])
    K.load(br[0:1, 4:36], K.dram["b_re"])
    iota = A.get(8)
    K.cst("iota8", iota)
    t_wr = t_io = K.landed()
    bsel = A.get(128)
    K.cst("triu", bsel)
    t_sel = K.landed()

    def pre1(k):
        return V.ts(XL[:, k, :], XL[:, k, :], K.v("ln1g", k), K.v("ln1b", k), MUL, ADD)

    def post1(k, t):
        return [S.act(h32[:, k, :], XL[:, k, :], ACT.Identity, t, c=0, scale=mod[:, 32 + k, 0:1],
                      bias=mod[:, 24 + k, 0:1])]

    h32_t = K.layer_norm(XL, 256, 0, sqb, rs, post1, pre1)
    t = V.last
    K.phase("moe")
    if stop == "mix":
        ctx.close()
        return
    t = S.last
    t_a = G.ts(XL, XL, ALPHA1, None, MUL, None, t)
    if K.two:
        K.D.wait(T.last)
        K.load(X[:, :, 0:256], K.dram["ctx2T"].rearrange("(k p) n -> p k n", p=128))
        t_ctx = K.landed()
    lg = A.get(2, 36)
    WT = A.get(2, 32)
    MK = A.get(2, 32)
    T.wait(t_wr)
    V.wait(t)
    for j in range(2):
        b = K.bank()
        for k in range(8):
            T.wait(*h32_t[k])
            T.mm(b.t[:, 0:36], h32[:, k, j * 128:j * 128 + 128], wr[:, k, :], k == 0, False)
        T.mm(b.t[:, 0:36], K.ones[0:1, 0:128], br[0:1, :], False, True)
        tk = T.mark()
        t = V.cp(lg[:, j, :], b.t[:, 0:36], tk, c=0)
        b.free = [t]
    V.wait(t_io)
    L, LE = lg[:, :, 0:4], lg[:, :, 4:36].rearrange("p j (g e) -> p j g e", g=4)
    mx, m1, m2, km, sm, w0, w1 = (A.get(2, 1) for _ in range(7))
    oh, ex = A.get(2, 4), A.get(2, 4)
    key, les, o1, o2, le2, t8, u8 = (A.get(2, 8) for _ in range(7))

    def over(x, n_):
        return x.broadcast_to([128, 2, n_])

    def first_of(x, n_, out, m_):
        k_ = key[:, :, 0:n_]
        V.red(m_, x, MAX)
        V.tt(out, x, over(m_, n_), ALU.is_ge)
        V.tt(k_, out, iota[:, 0:n_].unsqueeze(1).broadcast_to([128, 2, n_]), MUL)
        V.red(km, k_, MAX)
        V.tt(out, k_, over(km, n_), ALU.is_equal)

    first_of(L, 4, oh, mx)
    V.tt(ex, L, over(mx, 4), SUB)
    t = S.act(ex, ex, ACT.Exp, V.last)
    V.tt(les, LE[:, :, 0, :], over(oh[:, :, 0:1], 8), MUL)
    for g in range(1, 4):
        V.tt(t8, LE[:, :, g, :], over(oh[:, :, g:g + 1], 8), MUL)
        V.tt(les, les, t8, ADD)
    first_of(les, 8, o1, m1)
    V.stt(le2, o1, -3e38, les, MUL, ADD)
    first_of(le2, 8, o2, m2)
    V.tt(w0, m2, m1, SUB)
    t = S.act(w0, w0, ACT.Exp, V.last)
    V.ts(w1, w0, 1.0, None, ADD, None, t)
    V.red(sm, ex, ADD)
    V.tt(w1, w1, sm, MUL)
    V.rec(w1)
    V.tt(w0, w0, w1, MUL)
    V.tt(t8, o1, over(w1, 8), MUL)
    V.tt(u8, o2, over(w0, 8), MUL)
    V.tt(t8, t8, u8, ADD)
    V.tt(o1, o1, o2, ADD)
    for g in range(4):
        V.tt(WT[:, :, 8 * g:8 * g + 8], t8, over(oh[:, :, g:g + 1], 8), MUL, c=g == 0)
        V.tt(MK[:, :, 8 * g:8 * g + 8], o1, over(oh[:, :, g:g + 1], 8), MUL, c=0)
    pos = A.get(2, 32)
    cnt = A.get(4)
    flag = K.sb("flag", [128, 1], mybir.dt.int32, ctx)
    V.tt(bsel, bsel, K.ident[:, :], SUB, t_sel)
    T.wait(V.last)
    b = K.bank()
    T.mm(b.t[:, 0:32], bsel, MK[:, 0, :], True, True)
    T.mm(b.t[:, 32:64], bsel, MK[:, 1, :], True, False)
    T.mm(b.t[:, 32:64], K.ones[:, 0:128], MK[:, 0, :], False, True)
    T.mm(b.t[:, 64:96], K.ones[:, 0:128], MK[:, 0, :], True, False)
    T.mm(b.t[:, 64:96], K.ones[:, 0:128], MK[:, 1, :], False, True)
    tk = T.mark()
    V.stt(pos, b.t[:, 0:64].rearrange("p (j e) -> p j e", j=2), 1.0, MK, ADD, MUL, tk)
    V.ts(pos, pos, -1.0, None, ADD, None)
    V.red(cnt[:, 0:1], b.t[:, 64:96], MAX)
    b.free = [V.last]
    V.ts(cnt[:, 0:1], cnt[:, 0:1], CAP, None, ALU.is_gt, None)
    V.cp(flag[:, :], cnt[:, 0:1])
    K.finish(K.ada2[0])
    jobs, K.jobs = K.jobs, []
    hold = ExitStack()
    K.branch("all", flag[0:1, 0:1], True, lambda: experts_all(K, v8, h32, WT, hold))
    hold.close()
    K.branch("some", flag[0:1, 0:1], False, lambda: experts_some(K, h32, WT, pos, hold))
    hold.close()
    K.reopen()
    K.jobs = jobs
    yb = K.banks[4:8]
    K.barrier()
    A3.free = [T.last]
    ready = [[] for _ in range(8)]
    if K.two:
        tmp = K.sb("tmp2", [128, 4, 256], F32, hold)
        m2 = K.mod2[0]
        used = [[] for _ in range(4)]

        def half(k, s, v, i, *toks):
            t = S.act(tmp[:, i, :], X[:, k, s:s + 256], ACT.Identity, *toks, *used[i], c=0,
                      scale=m2[:, 8 + k, v:v + 1], bias=m2[:, k, v:v + 1])
            o = slice(k * 512 + s, k * 512 + s + 256)
            used[i] = K.split(A3.hi[:, o], A3.lo[:, o], tmp[:, i, :], t)
            return used[i]
    K.lo, K.hi = 0, 8
    K.mb, K.mb_n, K.mb_k = K.banks[3], 256, 0
    T.wait(*K.mb.free)
    K.bi = 4
    tv = []
    for m in range(8):
        t = V.stt(XL[:, m, :], yb[m // 2].t[:, 256 * (m % 2):256 * (m % 2) + 256], mod[:, 40 + m, 0:1],
                  XL[:, m, :], MUL, ADD, T.last, t_a, c=0)
        tv.append(t)
    for b in yb:
        b.free = [t]
    for m in range(8):
        K.mean_add(XL[:, m, :], tv[m])

    if K.two:
        S.wait(t_ctx)
        for k in range(8):
            ready[k] = half(k, 0, 1, k % 2)

    if K.two:
        K.ahead()

    def pre2(k):
        return V.ts(XL[:, k, :], XL[:, k, :], K.v("ln2g", k), K.v("ln2b", k), MUL, ADD)

    def post2(k, t):
        if K.two:
            r = half(k, 256, 0, 2 + k % 2, t) + ready[k]
            K.x_ready = [G.ts(X[:, k, :], X[:, k, :], ALPHA2, None, MUL, None, *r, c=0)]
            return r

    K.h_ready = K.layer_norm(XL, 256, 0, h32, rs, post2, pre2)
    K.barrier(pe=not K.two)
    hold.close()
    ctx.close()


def experts_all(K, v8, h32, WT, ctx):
    T, V, S, G, A3 = K.T, K.V, K.S, K.G, K.A
    NAR = 9600
    A = Arena(K.sb("ar_all", [128, NAR], F32, ctx), NAR)
    for m in range(8):
        ht = K.split(v8.hi[:, m, :], v8.lo[:, m, :], h32[:, m, :])
    b, tk = K.transpose_to([(WT[:, j, :], 128 * j) for j in range(2)], 32)
    wT = A.get(256)
    t = V.cp(wT[0:32, :], b.t[0:32, 0:256], tk)
    b.free = [t]
    T.wait(t)
    wbc = A.get(32, 256)
    for e_ in range(0, 32, 2):
        b = K.bank()
        for i in range(2):
            T.mm(b.t[:, 256 * i:256 * i + 256], K.ident[0:32, e_ + i:e_ + i + 1].broadcast_to([32, 128]),
                 wT[0:32, :], True, True)
        tk = T.mark()
        t = S.act(wbc[:, e_:e_ + 2, :], b.t[:, :].rearrange("p (i n) -> p i n", i=2), ACT.Copy, tk, c=0)
        b.free = [t]
    t_w = t
    EH = [K.sb(f"EH{i}", [128, 4, 256], F32R, ctx) for i in range(2)]
    EL = [K.sb(f"EL{i}", [128, 4, 256], F32R, ctx) for i in range(2)]
    sg, pr = [A.get(256) for _ in range(2)], [A.get(256) for _ in range(2)]
    sgf, prf, ehf = [[], []], [[], []], [[], []]
    yb = K.banks[4:8]
    K.lo, K.hi = 0, 4
    for b in yb:
        T.wait(*b.free)
    down = None
    for e_ in range(33):
        nxt = None
        if e_ < 32:
            E3 = X3(EH[e_ % 2], EL[e_ % 2])
            E3.split = True
            toks = []
            for p in range(2):
                wg = K.ring.get("w_eg", e_, 0, 8, 256 * p, 256, True)
                bs = []
                T.wait(*wg.toks, *ht)
                for i in range(2):
                    b = K.bank()
                    bs.append(b)
                    for k in range(8):
                        K.prod(b.t[:, 0:256], wg, (slice(None), k, slice(i * 128, i * 128 + 128)), v8,
                               (slice(None), k, slice(0, 256)), k == 0, k == 7)
                wg.end(T.mark())
                wu = K.ring.get("w_eu", e_, 0, 8, 256 * p, 256, True)
                T.wait(*wu.toks)
                for i in range(2):
                    b = bs[i]
                    for k in range(8):
                        K.prod(b.t[:, 256:512], wu, (slice(None), k, slice(i * 128, i * 128 + 128)), v8,
                               (slice(None), k, slice(0, 256)), k == 0, k == 7)
                    tk = T.mark()
                    if i == 1:
                        wu.end(tk)
                    m = 2 * p + i
                    q = m % 2
                    t1 = S.act(sg[q], b.t[:, 0:256], ACT.Silu, tk, *sgf[q], c=0)
                    t2 = V.tt(pr[q], sg[q], b.t[:, 256:512], MUL, t1, *prf[q], c=0)
                    sgf[q], b.free = [t2], [t2]
                    t3 = G.tt(pr[q], pr[q], wbc[:, e_, :], MUL, t2, t_w, c=0)
                    toks = K.split(E3.hi[:, m, :], E3.lo[:, m, :], pr[q], t3, *ehf[e_ % 2])
                    prf[q] = toks
            nxt = (e_, E3, toks)
        if down is not None:
            de, E3d, dt_ = down
            for half in range(2):
                w = K.ring.get("w_ed", de, 0, 4, 512 * half, 512, True)
                T.wait(*w.toks, *dt_)
                for i in range(4):
                    m = 4 * half + i
                    o = yb[m // 2].t[:, 256 * (m % 2):256 * (m % 2) + 256]
                    for k in range(4):
                        K.prod(o, w, (slice(None), k, slice(i * 128, i * 128 + 128)), E3d,
                               (slice(None), k, slice(0, 256)), de == 0 and k == 0 and m % 2 == 0,
                               de == 31 and k == 3, skip=True)
                w.end(T.mark())
            ehf[de % 2] = [T.last]
            K.step()
        down = nxt


def experts_some(K, h32, WT, pos, ctx):
    T, V, S, G, A3 = K.T, K.V, K.S, K.G, K.A

    def pair(name, *shape, n=1):
        return [[K.sb(f"{name}{q}{i}", [128, *shape], F32R, ctx) for q in "hl"] for i in range(n)]

    HTK, = pair("htk", 2, 1024)
    HT = pair("hts", 4, 128, n=2)
    YE = pair("ye", 1024, n=2)
    SEL = [K.sb(f"sel{i}", [128, 2, 512], F32R, ctx) for i in range(2)]
    SELT = [K.sb(f"selt{i}", [128, 256], F32R, ctx) for i in range(3)]
    WHL = K.sb("whl", [128, 2, 32, 2], F32R, ctx)
    NAR = 2100
    A = Arena(K.sb("ar_some", [128, NAR], F32, ctx), NAR)
    iot, pT = A.get(129), A.get(256)
    iotar, iotac = iot[:, 0:128], iot[:, 128:129]
    sg, hid, ws = [A.get(256) for _ in range(2)], [A.get(512) for _ in range(2)], A.get(32, 2)
    wsum = A.get(32)
    K.cst("iotar", iot, n=129)
    t_i = K.landed()
    XG = [K.AH[:, :].rearrange("p (k n) -> p k n", k=8), K.AL[:, :].rearrange("p (k n) -> p k n", k=8)]
    for j in range(2):
        for q in range(2):
            b, tk = K.transpose_to([(h32[:, 4 * q + m, j * 128:j * 128 + 128], 128 * m) for m in range(4)], 128)
            s = slice(512 * q, 512 * q + 512)
            a = S.act(HTK[0][:, j, s], b.t[:, :], ACT.Copy, tk, c=0)
            t_h = V.tt(HTK[1][:, j, s], b.t[:, :], HTK[0][:, j, s].bitcast(F32), SUB, a, c=0)
            b.free = [t_h]
    V.cp(WHL[:, :, :, 0], WT)
    t_whl = V.tt(WHL[:, :, :, 1], WT, WHL[:, :, :, 0].bitcast(F32), SUB)
    b, tk = K.transpose_to([(pos[:, j, :], 128 * j) for j in range(2)], 32)
    t_pT = V.cp(pT[0:32, :], b.t[0:32, 0:256], tk)
    b.free = [t_pT]
    V.wait(t_i)
    sel_free, selt_free, xg_free, sgf, hidf, htf, yef = [[], []], [[], [], []], [], [[], []], [[], []], [[], []], \
        [[], []]
    sel_t, xg_t, selt_t, ws_t, hid_t, ht_t, ye_t = {}, {}, {}, {}, {}, {}, {}

    def select(g):
        for j in range(2):
            for q in range(4):
                e_ = 4 * g + q
                t = V.ts(SEL[g % 2][:, j, 128 * q:128 * q + 128], iotar, pos[:, j, e_:e_ + 1], None, ALU.is_equal,
                         None, *sel_free[g % 2], c=0)
        sel_t[g] = t

    def gather(g):
        T.wait(sel_t[g], t_h)
        for k in range(8):
            for part in range(2):
                b = K.bank()
                for j in range(2):
                    T.mm(b.t[:, :], HTK[part][:, j, k * 128:k * 128 + 128], SEL[g % 2][:, j, :], j == 0, j == 1)
                tk = T.mark()
                if part == 0:
                    t1 = S.act(XG[0][:, k, :], b.t[:, :], ACT.Copy, tk, *xg_free, c=0)
                    b.free = [t1]
                else:
                    t2 = V.cp(XG[1][:, k, :], b.t[:, :], tk, *xg_free, c=0)
                    b.free = [t2]
        xg_t[g] = [t1, t2]
        T.wait(t_whl)
        b = K.bank()
        for q in range(4):
            for j in range(2):
                T.mm(b.t[:, 2 * q:2 * q + 2], SEL[g % 2][:, j, 128 * q:128 * q + 128], WHL[:, j, 4 * g + q, :],
                     j == 0, j == 1)
        tk = T.mark()
        sel_free[g % 2] = [tk]
        t = V.cp(ws[:, 4 * g:4 * g + 4, :], b.t[:, 0:8].rearrange("p (q c) -> p q c", c=2), tk)
        b.free = [t]
        ws_t[g] = V.tt(wsum[:, 4 * g:4 * g + 4], ws[:, 4 * g:4 * g + 4, 0], ws[:, 4 * g:4 * g + 4, 1], ADD)

    def row_select(e_):
        i = e_ % 3
        T.wait(t_pT)
        b = K.bank()
        T.mm(b.t[:, 0:256], K.ident[0:32, e_:e_ + 1].broadcast_to([32, 128]), pT[0:32, :], True, True)
        tk = T.mark()
        selt_t[e_] = V.ts(SELT[i][:, :], b.t[:, 0:256], iotac, None, ALU.is_equal, None, tk, *selt_free[i], c=0)
        b.free = [selt_t[e_]]

    def gate_up(e_):
        g, q, i = e_ // 4, e_ % 4, e_ % 2
        T.wait(*xg_t[g])
        s = slice(128 * q, 128 * q + 128)
        for p in range(2):
            b = K.bank()
            for n_, name in enumerate(("w_eg", "w_eu")):
                w = K.ring.get(name, e_, 0, 8, 256 * p, 256, True)
                T.wait(*w.toks)
                o = b.t[:, 256 * n_:256 * n_ + 256]
                for k in range(8):
                    T.mm(o, XG[0][:, k, s], w.hi[:, k, :], k == 0, False)
                    T.mm(o, XG[0][:, k, s], w.lo[:, k, :], False, False)
                    T.mm(o, XG[1][:, k, s], w.hi[:, k, :], False, k == 7)
                w.end(T.mark())
            tk = T.last
            t1 = S.act(sg[p], b.t[:, 0:256], ACT.Silu, tk, *sgf[p], c=0)
            t2 = V.stt(hid[i][:, 256 * p:256 * p + 256], b.t[:, 256:512], wsum[:, e_:e_ + 1], sg[p], MUL, MUL, t1,
                       ws_t[g], *hidf[i], c=0)
            b.free, sgf[p] = [t2], [t2]
        hid_t[e_] = t2
        if q == 3:
            del xg_free[:]
            xg_free.append(T.last)

    def turn(e_):
        i = e_ % 2
        T.wait(hid_t[e_])
        b, tk = K.transpose_to([(hid[i][:, 128 * k:128 * k + 128], 128 * k) for k in range(4)], 128)
        hidf[i] = [tk]
        src = b.t[:, :].rearrange("p (k n) -> p k n", k=4)
        a = S.act(HT[i][0][:, :, :], src, ACT.Copy, tk, *htf[i], c=0)
        t = V.tt(HT[i][1][:, :, :], src, HT[i][0][:, :, :].bitcast(F32), SUB, a, c=0)
        b.free = [t]
        ht_t[e_] = [a, t]

    def down(e_):
        i = e_ % 2
        T.wait(*ht_t[e_])
        for half in range(2):
            w = K.ring.get("w_ed", e_, 0, 4, 512 * half, 512, True)
            T.wait(*w.toks)
            b = K.bank()
            for k in range(4):
                T.mm(b.t[:, :], HT[i][0][:, k, :], w.hi[:, k, :], k == 0, False)
                T.mm(b.t[:, :], HT[i][0][:, k, :], w.lo[:, k, :], False, False)
                T.mm(b.t[:, :], HT[i][1][:, k, :], w.hi[:, k, :], False, k == 3)
            tk = T.mark()
            w.end(tk)
            s = slice(512 * half, 512 * half + 512)
            a = S.act(YE[i][0][:, s], b.t[:, :], ACT.Copy, tk, *yef[i], c=0)
            t = V.tt(YE[i][1][:, s], b.t[:, :], YE[i][0][:, s].bitcast(F32), SUB, a, c=0)
            b.free = [t]
        htf[i] = [T.last]
        ye_t[e_] = [a, t]

    def scatter(e_):
        i = e_ % 2
        T.wait(*ye_t[e_], selt_t[e_])
        for m in range(8):
            o = yb[m // 2].t[:, 256 * (m % 2):256 * (m % 2) + 256]
            for part in range(2):
                T.mm(o, YE[i][part][:, m * 128:m * 128 + 128], SELT[e_ % 3][:, :],
                     e_ == 0 and part == 0 and m % 2 == 0, e_ == 31 and part == 1, True)
        tk = T.mark()
        yef[i], selt_free[e_ % 3] = [tk], [tk]

    yb = K.banks[4:8]
    K.lo, K.hi = 0, 4
    select(0)
    gather(0)
    select(1)
    for e_ in range(34):
        if e_ < 32:
            gate_up(e_)
            row_select(e_)
        if e_ % 4 == 3 and e_ < 31:
            gather(e_ // 4 + 1)
            if e_ < 27:
                select(e_ // 4 + 2)
        if e_ >= 2:
            scatter(e_ - 2)
        if 1 <= e_ <= 32:
            down(e_ - 1)
        if e_ < 32:
            turn(e_)
    K.lo, K.hi = 0, 8


CAP = 128.0
LAG = 5


class HalfView:
    split = True

    def __init__(self, v, s):
        self.hi, self.lo = v.hi[:, :, s:s + 256], v.lo[:, :, s:s + 256]


def lead_in(K, l, base, n, x, tmp, alpha):
    mod = K.mod2[l] if l is not None else K.mod1
    used = [[], []]
    K.x_ready = []

    def post(k, t):
        r = scaled_split(K, x[:, k, :], k, n, K.A, lambda k, v: (mod[:, base + 8 + k, v:v + 1],
                                                                mod[:, base + k, v:v + 1]), tmp, used, [t])
        K.x_ready = [K.G.ts(x[:, k, :], x[:, k, :], alpha, None, MUL, None, *r, c=0)]
        return r

    return post


def residual(K, x, gate, halves, toks):
    wait = []

    def put(m, ps, tok):
        for a, z, v in halves:
            t = K.V.stt(x[:, m, a:z], ps[:, a:z], gate(m, v), x[:, m, a:z], MUL, ADD, tok, *toks, c=0)
        if wait:
            K.mean_add(*wait.pop())
        wait.append((x[:, m, :], t))
        if m == 7:
            K.mean_add(*wait.pop())
        return [t]

    return put


BOTH, LAT = [(0, 256, 1), (256, 512, 0)], [(0, 256, 0)]


def ffn(K, l, win, wout, base, n, nxt, jobs=()):
    T, V, S, G = K.T, K.V, K.S, K.G
    ctx = ExitStack()
    BH, BL = (K.sb(f"{q}{win}{l}", [128, 12, 512], F32R, ctx) for q in ("BH", "BL"))
    NAR = 7680
    A = Arena(K.sb(f"arf{win}{l}", [128, NAR], F32, ctx), NAR)
    sq, rs, tmp, sg, pr = A.get(8, 512)[:, :, 0:n], A.get(512)[:, 0:n], A.get(2, 512), A.get(2, 512), A.get(2, 512)
    X = K.X[:, :, 512 - n:512]
    mod = K.mod2[l]
    ht, t_a = K.h_ready, K.x_ready
    h = View3(K.A, 8, n)
    hid = X3(BH, BL)
    hid.split = True
    f = {"sg": [[], []], "pr": [[], []]}
    hfree = []
    for first, cnt in ((0, 12), (12, 10)):
        toks = []
        for p in range(cnt // 2):
            c0 = (first + 2 * p) * 128
            wg = K.ring.get(win, l, 0, 8, c0, 256, True)
            T.wait(*wg.toks)
            bs = [(K.bank(), K.bank()) for _ in range(2)]
            for k in range(8):
                T.wait(*ht[k])
                for i in range(2):
                    K.prod(bs[i][0].t[:, 0:n], wg, (slice(None), k, slice(i * 128, i * 128 + 128)), h,
                           (slice(None), k, slice(0, n)), k == 0, k == 7)
            wg.end(T.mark())
            wu = K.ring.get(win, l, 0, 8, 2816 + c0, 256, True)
            T.wait(*wu.toks)
            for i in range(2):
                b, b2 = bs[i]
                for k in range(8):
                    K.prod(b2.t[:, 0:n], wu, (slice(None), k, slice(i * 128, i * 128 + 128)), h,
                           (slice(None), k, slice(0, n)), k == 0, k == 7)
                tk = T.mark()
                if i == 1:
                    wu.end(tk)
                m = 2 * p + i
                t1 = S.act(sg[:, i, 0:n], b.t[:, 0:n], ACT.Silu, tk, *f["sg"][i], c=0)
                b.free = [t1]
                t2 = V.tt(pr[:, i, 0:n], sg[:, i, 0:n], b2.t[:, 0:n], MUL, t1, *f["pr"][i], c=0)
                b2.free, f["sg"][i] = [t2], [t2]
                toks = K.split(BH[:, m, 0:n], BL[:, m, 0:n], pr[:, i, 0:n], t2, *hfree)
                f["pr"][i] = toks

        if first == 0:
            def down(m, ps, tok):
                for a, z, v in (BOTH if n == 512 else LAT):
                    t = V.stt(X[:, m, a:z], ps[:, a:z], mod[:, base + 16 + m, v:v + 1], X[:, m, a:z], MUL, ADD,
                              tok, *t_a, c=0)
                return [t]
        else:
            K.mean_begin(n)
            down = residual(K, X, lambda m, v: mod[:, base + 16 + m, v:v + 1], BOTH if n == 512 else LAT, t_a)
        K.linear(wout, l, cnt, 0, 8, hid, n, down, row=first * 128, xtoks=toks, bg=False)
        hfree = [T.last]
    K.A.free = [T.last]
    for j in jobs:
        K.finish(j)
    post = lead_in(K, *nxt[:3], X, tmp, ALPHA2) if nxt else lambda k, t: None
    K.h_ready = K.layer_norm(X, n, 1, sq, rs, post)
    K.barrier(pe=False)
    ctx.close()


def log1p_exp(K, dst, z, e1, e2, tz):
    V, S = K.V, K.S
    V.stt(e1, z, -1.0, z, MUL, MIN, tz)
    t = S.act(e1, e1, ACT.Exp, V.last)
    V.ts(e2, e1, 1.0, None, ADD, None, t)
    t = S.act(dst, e2, ACT.Ln, V.last)
    one = z_eq = K.lp
    V.ts(one, e2, 1.0, None, ALU.is_equal, None, t)
    V.stt(e2, e2, -1.0, one, ADD, ADD)
    V.tt(dst, dst, z_eq, ADD)
    V.rec(e2)
    V.tt(dst, dst, e1, MUL)
    return V.tt(dst, dst, e2, MUL)


def token_rows(K, name, lead, c0, ncol, h, ht, dst):
    T, S = K.T, K.S
    for a in range(0, ncol, 256):
        w = K.ring.get(name, lead, 0, 8, c0 + a, 256, True)
        T.wait(*w.toks)
        for tt in range(4):
            b = K.bank()
            o = b.t[:, 0:256]
            for k in range(8):
                s = (slice(None), k, slice(tt * 128, tt * 128 + 128))
                T.mm(o, h.hi[s], w.hi[:, k, :], k == 0, False)
                T.mm(o, h.hi[s], w.lo[:, k, :], False, False)
                T.mm(o, h.lo[s], w.hi[:, k, :], False, k == 7)
            tk = T.mark()
            if tt == 3:
                w.end(tk)
            t = S.act(dst[:, tt, a:a + 256], o, ACT.Copy, tk, c=0)
            b.free = [t]
    return t


def even(K):
    T, V, S, G = K.T, K.V, K.S, K.G
    ctx = ExitStack()
    NAR = 19900
    A = Arena(K.sb("ar3", [128, NAR], F32, ctx), NAR)
    X = K.X[:, :, :]
    mod = K.mod2[0]
    oT = A.get(4, 512)
    base = A.at
    ht, t_alpha = K.h_ready, K.x_ready
    h = View3(K.A, 8, 512)
    A.at = base
    qT, kT, vt, r = A.get(2, 512), A.get(2, 512), A.get(4, 512), A.get(4, 512)
    bs = [A.get(2, 512) for _ in range(2)]
    glam_at = A.at
    glam = A.get(15, 128)
    K.cst("glam", glam.rearrange("p a b -> p (a b)"))
    KQ = [A.get(2, 512) for _ in range(2)]
    ST = [[A.get(2, 128) for _ in range(3)] for _ in range(2)]
    att_at = A.at
    lr, WG, e1, e2, K.lp, z = A.get(512), A.get(2, 256), A.get(512), A.get(512), A.get(512), A.get(512)
    t_z = G.do(lambda e: e.memset(WG[0:32], 0.0))
    K.D.wait(t_z)
    K.load(WG[0:16, 0, :], K.dram["wg2f"])
    K.load(WG[16:32, 1, :], K.dram["wg2b"])
    t_wg = K.landed()
    K.linear("ewi", None, 8, 0, 2, h, 512, lambda m, ps, tok: [S.act(qT[:, m, :], ps, ACT.Copy, tok, c=0,
                                                                    scale=0.125)], bg=False, xtoks=ht)
    K.linear("ewi", None, 8, 1536, 1, h, 512, lambda m, ps, tok: [S.act(lr[0:32], ps[0:32], ACT.Copy, tok)])
    t_lr = S.last
    T.wait(t_lr, t_wg)
    K.gate_t = None

    def decays():
        for d in range(2):
            for ft in range(2):
                b = K.bank()
                T.mm(b.t[:, :], WG[0:32, d, ft * 128:ft * 128 + 128], lr[0:32, :], True, True)
                tk = T.mark()
                V.ts(z, b.t[:, :], K.v("bgf" if d == 0 else "bgb", ft), None, ADD, None, tk)
                b.free = [V.last]
                yield True
                e3 = KQ[0][:, 0, :]
                log1p_exp(K, e3, z, e1, e2, V.last)
                yield True
                V.ts(z, z, 0.0, 0.0625, MIN, MUL)
                V.stt(z, e3, -0.0625, z, MUL, ADD)
                for tt in range(4):
                    s = slice(tt * 128, tt * 128 + 128)
                    o, i = (bs[d][:, ft, s], z[:, s]) if d == 0 else (bs[d][:, ft, s][:, ::-1], z[:, s][:, ::-1])
                    V.do(lambda e, o=o, i=i: e.tensor_tensor_scan(o, K.ones[:, 0:128], i, 0.0, MUL, ADD), c=tt == 0)
                yield True

    job = decays()

    def go(n):
        for _ in range(n):
            next(job, None)

    go(1)
    go(2)
    K.linear("ewi", None, 8, 256, 2, h, 512, lambda m, ps, tok: [S.act(kT[:, m, :], ps, ACT.Copy, tok, c=0)],
             bg=False)
    t_qk = S.last
    go(3)
    token_rows(K, "ewi", None, 512, 256, h, ht, vt)
    go(3)
    token_rows(K, "ewi", None, 768, 256, h, ht, vt[:, :, 256:512])
    t_vt = S.last
    go(9)
    t_b = V.last
    r_tile = lambda m, ps, tok: [S.act(r[:, m, :], ps, ACT.Silu, tok, c=0)]
    K.linear("ewi", None, 8, 1024, 2, h, 512, r_tile, bg=False)
    K.linear("ewi", None, 8, 1280, 2, h, 512, lambda m, ps, tok: r_tile(m + 2, ps, tok), bg=False)
    t_v = S.last
    K.barrier(pe=False)
    T.wait(t_v)
    A.at = att_at
    todo = [(d, n_, tt) for d, order in ((0, (0, 1, 2)), (1, (1, 0, 3))) for n_, tt in enumerate(order)]
    kds = [KQ[0][:, :, 128 * i:128 * i + 128] for i in range(2)]
    kts = [KQ[1][:, 0, 256 * i:256 * i + 256] for i in range(2)]
    ebs = [KQ[1][:, 1, 2 * i:2 * i + 2] for i in range(2)]
    kd_t, kd_free, kt_free, eb_free = {}, [[], []], [[], []], [[], []]

    def decayed(j):
        d, n_, tt = todo[j]
        kd, eb, i = kds[j % 2], ebs[j % 2], j % 2
        s = slice(tt * 128, tt * 128 + 128)
        last = tt * 128 + (127 if d == 0 else 0)
        for ft in range(2):
            S.act(kd[:, ft, :], bs[d][:, ft, s], ACT.Exp, t_b, *kd_free[i], c=0, bias=bs[d][:, ft, last:last + 1],
                  scale=-1.0)
        t = S.act(eb.unsqueeze(2), bs[d][:, :, last:last + 1], ACT.Exp, *eb_free[i], c=0)
        kd_t[j] = V.tt(kd, kd, kT[:, :, s], MUL, t, c=0)

    decayed(0)
    for j, (d, n_, tt) in enumerate(todo):
        if j < 5:
            decayed(j + 1)
        kd, kt_, eb, i = kds[j % 2], kts[j % 2], ebs[j % 2], j % 2
        T.wait(kd_t[j])
        b, tk = K.transpose_to([(kd[:, ft, :], 128 * ft) for ft in range(2)], 128)
        kd_free[i] = [tk]
        t_kt = V.cp(kt_, b.t[:, 0:256], tk, *kt_free[i], c=0)
        b.free = [t_kt]
        K.step()
        T.wait(t_kt)
        b = K.bank()
        for ft in range(2):
            for p in range(2):
                hd = 2 * ft + p
                T.mm(b.t[64 * p:64 * p + 64, ft * 128:ft * 128 + 128], kt_[:, hd * 64:hd * 64 + 64],
                     vt[:, tt, hd * 128:hd * 128 + 128], True, True)
        tk = T.mark()
        kt_free[i] = [tk]
        for ft in range(2):
            if n_ == 0:
                t = V.cp(ST[d][0][:, ft, :], b.t[:, ft * 128:ft * 128 + 128], tk)
            else:
                t = V.stt(ST[d][n_][:, ft, :], ST[d][n_ - 1][:, ft, :], eb[:, ft:ft + 1],
                          b.t[:, ft * 128:ft * 128 + 128], MUL, ADD, tk)
        b.free, eb_free[i] = [t], [t]
    t_st = V.last
    ATT = [[A.get(4, 128) for _ in range(2)] for _ in range(2)]
    t_gm = t_wg

    def pairs(k_, q_, put):
        for p in range(2):
            for tp in range(2):
                b = K.bank()
                for t2 in range(2):
                    for ft in range(2):
                        s = slice((2 * tp + t2) * 128, (2 * tp + t2) * 128 + 128)
                        T.mm(b.t[:, (2 * t2 + ft) * 128:(2 * t2 + ft) * 128 + 128],
                             k_[64 * p:64 * p + 64, ft, s], q_[64 * p:64 * p + 64, ft, s], True, True)
                tk = T.mark()
                b.free = [put(ATT[p][tp], b.t[:, :].rearrange("p (a b) -> p a b", a=4), tk)]

    T.wait(t_qk)
    V.wait(t_gm)
    pairs(kT, qT, lambda a, ps, tk: V.tt(a, ps, glam[:, 14:15, :].broadcast_to([128, 4, 128]), MUL, tk, c=0))
    kq_free = [[T.last, t_st], [T.last, t_st]]
    parts = [(lv, d) for lv in range(7) for d in range(2)]
    kq_t = {}

    def referred(n_):
        lv, d = parts[n_]
        w = 1 << lv
        kq = KQ[n_ % 2]

        def halves(x):
            return x.rearrange("p a b -> p (a b)").rearrange("p (n s w) -> p n s w", s=2, w=w)

        bv, dv, kv, qv = halves(bs[d]), halves(kq), halves(kT), halves(qT)
        nb = 512 // w
        ref = (bv[:, :, 0, w - 1:w] if d == 0 else bv[:, :, 1, 0:1]).broadcast_to([128, nb, w])
        lo, up = bv[:, :, 0, :], bv[:, :, 1, :]
        if d == 0:
            t0 = V.tt(dv[:, :, 0, :], ref, lo, SUB, *kq_free[n_ % 2], c=0)
            t1 = G.tt(dv[:, :, 1, :], up, ref, SUB, t_b, *kq_free[n_ % 2], c=0)
        else:
            t0 = V.tt(dv[:, :, 0, :], lo, ref, SUB, *kq_free[n_ % 2], c=0)
            t1 = G.tt(dv[:, :, 1, :], ref, up, SUB, t_b, *kq_free[n_ % 2], c=0)
        flat = kq.rearrange("p a b -> p (a b)")
        te = S.act(flat, flat, ACT.Exp, t0, t1, c=0)
        a, b_ = (kv, qv) if d == 0 else (qv, kv)
        t0 = V.tt(dv[:, :, 0, :], dv[:, :, 0, :], a[:, :, 0, :], MUL, te, c=0)
        t1 = G.tt(dv[:, :, 1, :], dv[:, :, 1, :], b_[:, :, 1, :], MUL, te, c=0)
        kq_t[n_] = [t0, t1]

    referred(0)
    for n_, (lv, d) in enumerate(parts):
        if n_ < 13:
            referred(n_ + 1)
        T.wait(*kq_t[n_])
        mk = glam[:, 7 * d + lv:7 * d + lv + 1, :].bitcast(U32).broadcast_to([128, 4, 128])
        pairs(KQ[n_ % 2], KQ[n_ % 2],
              lambda x, ps, tk, mk=mk: V.do(lambda e: e.copy_predicated(x, mk, ps), tk, c=1))
        kq_free[n_ % 2] = [T.last]
        K.step(2)
    QE = KQ
    for d in range(2):
        flat = QE[d].rearrange("p a b -> p (a b)")
        t = S.act(flat, bs[d].rearrange("p a b -> p (a b)"), ACT.Exp, T.last, c=0)
        t = V.tt(QE[d], QE[d], qT, MUL, t, c=0)
    t_att = V.last
    A.at = glam_at
    cq = A.get(3, 512)
    mla_at = A.at
    A.at = base + 1024
    ck, krr = A.get(1, 512), A.get(512)
    S.wait(t_att, G.last)
    K.linear("ewi", None, 8, 1568, 3, h, 512, lambda m, ps, tok: [S.act(cq[:, m, :], ps, ACT.Copy, tok, c=0)],
             bg=False)
    T.wait(t_att)
    sqs, rss = [bs[0][:, i, :] for i in range(2)], [bs[1][:, i, :] for i in range(2)]
    before = [{1: 0, 2: 1, 3: 2}, {0: 0, 3: 1, 2: 2}]
    got = {}

    def read(hd):
        ft, p = hd // 2, hd % 2
        b = K.bank()
        for tt in range(4):
            s = slice(tt * 128, tt * 128 + 128)
            o = b.t[:, s]
            inter = [(d, before[d][tt]) for d in range(2) if tt in before[d]]
            T.mm(o, vt[:, tt, hd * 128:hd * 128 + 128], ATT[p][tt // 2][:, (tt % 2) * 2 + ft, :], True, not inter)
            for x, (d, n_) in enumerate(inter):
                T.mm(o, ST[d][n_][64 * p:64 * p + 64, ft, :], QE[d][64 * p:64 * p + 64, ft, s], False,
                     x == len(inter) - 1)
        tk = T.mark()
        t = V.cp(oT[:, hd, :], b.t[:, :], tk, c=0)
        b.free = [t]
        got[hd] = t

    sqf, rsf = [[], []], [[], []]
    read(0)
    for hd in range(4):
        if hd < 3:
            read(hd + 1)
        sq, rs, i = sqs[hd % 2], rss[hd % 2], hd % 2
        t = S.act(sq, oT[:, hd, :], ACT.Square, got[hd], *sqf[i], c=0)
        T.wait(t)
        b = K.bank()
        T.mm(b.t[:, :], K.onesD[:, :], sq, True, True)
        tk = T.mark()
        sqf[i] = [tk]
        t = S.act(rs, b.t[:, :], ACT.Sqrt, tk, *rsf[i], bias=K.eps[:, 1:2], scale=8.0)
        b.free = [t]
        V.rec(rs, t)
        rsf[i] = [V.stt(oT[:, hd, :], oT[:, hd, :], K.v("gng"), rs, MUL, MUL)]
        V.tt(oT[:, hd, :], oT[:, hd, :], r[:, hd, :], MUL, t_v)
        if hd == 0:
            K.linear("ewi", None, 8, 1952, 1, h, 512, lambda m, ps, tok: [S.act(ck[:, m, :], ps, ACT.Copy, tok, c=0)],
                     bg=False)
        if hd == 1:
            K.linear("ewi", None, 8, 2016, 1, h, 512,
                     lambda m, ps, tok: [S.act(krr[64:128, :], ps[64:128, :], ACT.Copy, tok, c=0)], bg=False)
            K.A.free = [T.last]
    K.barrier(pe=False)
    t_c = S.last
    A.at = base + 2048
    qn, qr, kn = A.get(4, 512), A.get(4, 512), A.get(4, 512)
    assert A.at == glam_at
    A.at = mla_at
    v2, oM = A.get(4, 512), A.get(4, 512)
    cos, sin, rsw = A.get(256), A.get(256), A.get(64)
    K.cst("cos", cos)
    K.cst("sin", sin)
    K.cst("rsw", rsw)
    t_rope = K.landed()
    P = [A.get(512) for _ in range(3)]
    PT = [A.get(4, 128) for _ in range(2)]
    st = A.get(12)
    rs, tn = P[0], []
    for x, nt, key, w in ((ck, 1, "kvng", 8.0), (cq, 3, "qng", 1024.0 / 384)):
        b = K.bank()
        for m in range(nt):
            t = S.act(P[1], x[:, m, :], ACT.Square, t_c, T.last)
            T.wait(t)
            T.mm(b.t[:, :], K.onesD[:, :], P[1], m == 0, m == nt - 1)
            T.mark()
        t = S.act(rs, b.t[:, :], ACT.Sqrt, T.last, V.last, bias=K.eps[:, 1:2], scale=w)
        b.free = [t]
        V.rec(rs, t)
        for m in range(nt):
            V.stt(x[:, m, :], x[:, m, :], K.v(key, m), rs, MUL, MUL)
        tn.append(V.last)

    def lin32(w, kt, col, x, put):
        b = K.bank()
        for k in range(kt):
            T.mm(b.t[:, :], w.f[:, k, col:col + 128], x[:, k, :], k == 0, k == kt - 1)
        b.free = [put(b.t, T.mark())]

    w = K.ring.get("ukv", None, 0, 1, 0, 1024, False)
    T.wait(*w.toks, tn[0])
    for hd in range(4):
        lin32(w, 1, 256 * hd, ck, lambda ps, tk: S.act(kn[:, hd, :], ps[:, :], ACT.Copy, tk, c=0))
        b = K.bank()
        for tt in range(4):
            T.mm(b.t[:, tt * 128:tt * 128 + 128], ck[:, 0, tt * 128:tt * 128 + 128],
                 w.f[:, 0, 256 * hd + 128:256 * hd + 256], True, True)
        tk = T.mark()
        t = V.cp(v2[:, :, hd * 128:hd * 128 + 128], b.t[:, :].rearrange("p (a b) -> p a b", a=4), tk, c=0)
        b.free = [t]
    w.end(T.last)
    for j in range(2):
        w = K.ring.get("uq", None, 0, 3, 384 * j, 384, False)
        T.wait(*w.toks, tn[1])
        for hd in (2 * j, 2 * j + 1):
            c0 = 192 * (hd % 2)
            lin32(w, 3, c0, cq, lambda ps, tk: S.act(qn[:, hd, :], ps[:, :], ACT.Copy, tk, c=0))
            lin32(w, 3, c0 + 64, cq, lambda ps, tk: S.act(qr[64:128, hd, :], ps[64:128, :], ACT.Copy, tk, c=0))
        w.end(T.last)
    t_v2 = V.last
    t_q = S.last
    V.wait(t_rope, t_q)
    T.wait(t_rope, t_q, t_v2)
    q = slice(64, 128)
    xs = [qr[q, i, 256:512] for i in range(4)] + [krr[q, 256:512]]
    turns = []
    for x in xs:
        b = K.bank()
        T.mm(b.t[q, 0:256], rsw[q, :], x, True, True)
        turns.append((b, T.mark()))
    for x, (b, tk) in zip(xs, turns):
        V.tt(x, x, cos[q], MUL, tk, c=0)
        V.tt(P[0][q, 0:256], b.t[q, 0:256], sin[q], MUL)
        b.free = [V.last]
        V.tt(x, x, P[0][q, 0:256], ADD)
    T.wait(V.last)
    S.wait(V.last)
    work = [(hd, qt) for hd in range(4) for qt in range(4)]
    scale = 192.0 ** -0.5
    pf, ptf = [[], [], []], [[], []]
    exps, stage, pts = {}, {}, {}

    def scores(n_):
        hd, qt = work[n_]
        i = n_ % 3
        nk = 512 if qt >= 2 else 256
        s = slice(qt * 128, qt * 128 + 128)
        b = K.bank()
        T.mm(b.t[:, 0:nk], qn[:, hd, s], kn[:, hd, 0:nk], True, False)
        T.mm(b.t[:, 0:nk], qr[q, hd, s], krr[q, 0:nk], False, True)
        tk = T.mark()
        mx, sm = st[:, 4 * i:4 * i + 1], st[:, 4 * i + 1:4 * i + 2]
        V.red(mx, b.t[:, 0:nk], MAX, tk, *pf[i])
        V.ts(mx, mx, -scale, None, MUL, None)
        exps[n_] = S.act(P[i][:, 0:nk], b.t[:, 0:nk], ACT.Exp, V.last, *pf[i], c=0, bias=mx, scale=scale,
                         accum_out=sm)
        b.free = [exps[n_]]

    def shares(n_):
        i = n_ % 3
        nk = 512 if work[n_][1] >= 2 else 256
        sm = st[:, 4 * i + 1:4 * i + 2]
        V.rec(sm, exps[n_])
        stage[n_] = V.ts(P[i][:, 0:nk], P[i][:, 0:nk], sm, None, MUL, None)

    def turned(n_):
        i = n_ % 3
        j = n_ % 2
        nk = 512 if work[n_][1] >= 2 else 256
        T.wait(stage[n_])
        b, tk = K.transpose_to([(P[i][:, a * 128:a * 128 + 128], a * 128) for a in range(nk // 128)], 128)
        pf[i] = [tk]
        pts[n_] = V.cp(PT[j][:, 0:nk // 128, :], b.t[:, 0:nk].rearrange("p (a b) -> p a b", b=128), tk, *ptf[j])
        b.free = [pts[n_]]

    def values(n_):
        hd, qt = work[n_]
        i = n_ % 2
        nk = 512 if qt >= 2 else 256
        T.wait(pts[n_])
        b = K.bank()
        for a in range(nk // 128):
            T.mm(b.t[:, 0:128], v2[:, a, hd * 128:hd * 128 + 128], PT[i][:, a, :], a == 0, a == nk // 128 - 1)
        tk = T.mark()
        ptf[i] = [tk]
        t = S.act(oM[:, hd, qt * 128:qt * 128 + 128], b.t[:, 0:128], ACT.Copy, tk, c=0)
        b.free = [t]

    toks = [K.split(h.hi[:, m, :], h.lo[:, m, :], oT[:, m, :], *K.A.free) for m in range(4)]
    for n_ in range(19):
        if n_ < 16:
            scores(n_)
        K.step()
        if n_ >= 3:
            values(n_ - 3)
            if n_ % 4 == 2:
                m = 3 + n_ // 4
                toks.append(K.split(h.hi[:, m, :], h.lo[:, m, :], oM[:, m - 4, :], S.last, *K.A.free))
        if 2 <= n_ < 18:
            turned(n_ - 2)
        if 1 <= n_ < 17:
            shares(n_ - 1)
    K.mean_begin(512)
    K.linear("ewo", None, 8, 0, 8, h, 512,
             residual(K, X, lambda m, v: mod[:, 40 + m, v:v + 1], BOTH, t_alpha), xtoks=toks)
    K.A.free = [T.last]
    K.barrier()
    A.at = 0
    sq, rs, tmp = A.get(8, 512), A.get(512), A.get(2, 512)
    K.h_ready = K.layer_norm(X, 512, 1, sq, rs, lead_in(K, 0, 48, 512, X, tmp, ALPHA2))
    K.barrier(pe=False)
    ctx.close()


def odd(K):
    T, V, S, G = K.T, K.V, K.S, K.G
    ctx = ExitStack()
    NAR = 20044
    A = Arena(K.sb("ar4", [128, NAR], F32, ctx), NAR)
    X = K.X[:, :, :]
    XL = X[:, :, 256:512]
    mod = K.mod2[1]
    TT = A.get(16, 384)
    K.load(TT, K.dram["rpb"].rearrange("p h m c -> p h (m c)"))
    qT, kT, vt = A.get(8, 256), A.get(8, 512), A.get(4, 1024)
    P = [A.get(512) for _ in range(3)]
    PT = A.get(4, 256)
    PT2 = A.get(4, 256)
    st = A.get(12)
    nm = A.get(64)
    K.cst("namask", nm)
    t_tt = K.landed()
    ht, t_alpha = K.h_ready, K.x_ready
    h = View3(K.A, 8, 512)
    hl = HalfView(h, 256)
    for hd in range(16):
        x = TT[:, hd, :].rearrange("p (m c) -> p m c", m=6)
        G.tt(x, x, nm.unsqueeze(1).broadcast_to([128, 6, 64]), ADD, t_tt, c=0)
    t_tt = G.last
    K.linear("nwi", None, 8, 0, 8, hl, 256, lambda m, ps, tok: [S.act(qT[:, m, :], ps, ACT.Copy, tok, c=0,
                                                                     scale=0.125)], xtoks=ht)
    K.linear("nwi", None, 8, 1024, 8, h, 512, lambda m, ps, tok: [S.act(kT[:, m, :], ps, ACT.Copy, tok, c=0)])
    token_rows(K, "nwi", None, 2048, 1024, h, ht, vt)
    K.A.free = [T.last]
    t_v = S.last
    T.wait(t_v)
    V.wait(t_tt)
    PTs = [PT, PT2]
    pf, ptf = [[], [], []], [[], []]
    exps, stage, pts = {}, {}, {}

    def scores(n_):
        hd, qt = n_ // 2, n_ % 2
        i = n_ % 3
        p, m = 64 * (hd % 2), hd // 2
        b = K.bank()
        T.mm(b.t[:, :], qT[p:p + 64, m, qt * 128:qt * 128 + 128], kT[p:p + 64, m, :], True, True)
        tk = T.mark()
        V.tt(P[i][:, 256:512], b.t[:, 256:512], TT[:, hd, (2 - 2 * qt) * 64:(2 - 2 * qt) * 64 + 256], ADD,
             tk, *pf[i], c=0)
        V.cp(P[i][:, 0:256], b.t[:, 0:256], c=0)
        b.free = [V.last]
        mx, sm = st[:, 4 * i:4 * i + 1], st[:, 4 * i + 1:4 * i + 2]
        V.red(mx, P[i], MAX)
        V.ts(mx, mx, -1.0, None, MUL, None)
        exps[n_] = S.act(P[i], P[i], ACT.Exp, V.last, c=0, bias=mx, accum_out=sm)

    def shares(n_):
        i = n_ % 3
        sm = st[:, 4 * i + 1:4 * i + 2]
        V.rec(sm, exps[n_])
        stage[n_] = V.ts(P[i], P[i], sm, None, MUL, None)

    def turned(n_):
        hd, qt = n_ // 2, n_ % 2
        i = n_ % 3
        pt = PTs[hd % 2]
        T.wait(stage[n_])
        b, tk = K.transpose_to([(P[i][:, a * 128:a * 128 + 128], a * 128) for a in range(4)], 128)
        pf[i] = [tk]
        t = S.act(pt[:, :, qt * 128:qt * 128 + 128], b.t[:, :].rearrange("p (a b) -> p a b", a=4), ACT.Copy, tk,
                  *ptf[hd % 2], c=0)
        b.free, pts[hd] = [t], t

    def values(hd):
        p, m = 64 * (hd % 2), hd // 2
        T.wait(pts[hd])
        b = K.bank()
        for a in range(4):
            T.mm(b.t[p:p + 64, 0:256], vt[:, a, hd * 64:hd * 64 + 64], PTs[hd % 2][:, a, :], a == 0, a == 3)
        tk = T.mark()
        ptf[hd % 2] = [tk]
        t = S.act(qT[p:p + 64, m, :], b.t[p:p + 64, 0:256], ACT.Copy, tk, c=0)
        b.free = [t]

    v8, toks = View3(K.A, 8, 256), []
    for n_ in range(36):
        if n_ < 32:
            scores(n_)
        if n_ >= 4 and n_ % 2 == 0:
            values(n_ // 2 - 2)
            if n_ % 4 == 2:
                m = n_ // 4 - 1
                toks.append(K.split(v8.hi[:, m, :], v8.lo[:, m, :], qT[:, m, :], S.last, *K.A.free))
        if 2 <= n_ < 34:
            turned(n_ - 2)
        if 1 <= n_ < 33:
            shares(n_ - 1)
    K.mean_begin(256)
    K.linear("nwo", None, 8, 0, 8, v8, 256,
             residual(K, XL, lambda m, v: mod[:, 40 + m, 0:1], LAT, t_alpha), xtoks=toks)
    K.A.free = [T.last]
    K.barrier()
    A.at = 0
    sq, rs, tmp = A.get(8, 256), A.get(256), A.get(2, 512)
    K.h_ready = K.layer_norm(XL, 256, 1, sq, rs, lead_in(K, 1, 48, 256, XL, tmp, ALPHA2))
    K.barrier(pe=False)
    ctx.close()


def lead_alone(K):
    V = K.V
    K.load(K.X[:, :, 0:256], K.dram["ctx2T"].rearrange("(k p) n -> p k n", p=128))
    K.t_in = K.landed()
    jobs = K.ada2
    K.finish(jobs[0])
    V.wait(V.last, K.t_in)
    with ExitStack() as ctx:
        tmp = K.sb("tmp2", [128, 2, 512], F32, ctx)
        mod = K.mod2[0]
        used = [[], []]
        K.h_ready = []
        for k in range(8):
            r = scaled_split(K, K.X[:, k, :], k, 512, K.A, lambda k, v: (mod[:, 8 + k, v:v + 1],
                                                                        mod[:, k, v:v + 1]), tmp, used,
                             [V.last, K.t_in])
            K.h_ready.append(r)
            K.x_ready = [K.G.ts(K.X[:, k, :], K.X[:, k, :], ALPHA2, None, MUL, None, *r, c=0)]
        K.barrier(pe=False)


def block_two(K, alone):
    jobs = K.ada2
    if alone:
        lead_alone(K)
    K.jobs.append(jobs[1])
    K.phase("ffn")
    ffn(K, 0, "f1i", "f1o", 0, 512, (0, 24, 512))
    K.phase("even")
    even(K)
    K.phase("ffn")
    ffn(K, 0, "f2i", "f2o", 48, 512, (1, 0, 512), [jobs[1]])
    K.phase("ffn")
    ffn(K, 1, "f1i", "f1o", 0, 512, (1, 24, 512))
    K.phase("odd")
    odd(K)
    K.phase("ffn")
    ffn(K, 1, "f2i", "f2o", 48, 256, None)
    K.phase("end")

MODE = "all"


def build(nc, dram, out, plan, mode):
    with ExitStack() as ctx:
        K = Kern(nc, dram, plan, ctx)
        K.two = mode == "all"
        setup(K)
        if mode != "two":
            block_one(K, "mix" if mode == "mix" else None)
        else:
            fix2 = {1: 1, 4: 1, 7: 1, 2: 2, 8: 2}
            K.phase("start")
            K.ada2 = [conditioning(K, "ada_w", l, 0, 72, 2, K.v("ada_b", 72 * l, 72), K.mod2[l], fix2)
                      for l in range(2)]
            K.jobs.append(K.ada2[0])
        if mode in ("all", "two"):
            block_two(K, mode == "two")
        s_out = K.sem("s_out")
        K.barrier()
        K.dma(out.rearrange("(k p) n -> p k n", p=128), K.X[:, :, 256:512], s_out)
        K.D.items.append(lambda e: e.wait_ge(s_out, 16))
        if plan is None:
            return K.asked
        block = ctx.enter_context(nc.Block())

        @block.sync
        def _(eng):
            K.D.run(eng)

        @block.tensor
        def _(eng):
            K.T.run(eng)

        @block.vector
        def _(eng):
            K.V.run(eng)

        @block.scalar
        def _(eng):
            K.S.run(eng)

        @block.gpsimd
        def _(eng):
            K.G.run(eng)


def kernel(**I):
    import concourse.bacc as _bacc
    from concourse.bass_utils import run_bass_kernel_spmd as _run

    def col(a, n=128):
        return np.ascontiguousarray(np.asarray(a).reshape(-1, n).T)

    vec = np.zeros((128, NVEC), np.float32)

    def put(key, a):
        vec[:a.shape[0], VOFF[key]:VOFF[key] + a.shape[1]] = a

    I = {k: np.asarray(a) for k, a in I.items()}
    put("c", col(I["c"]))
    put("cc", col(I["c_ctx"]))
    put("b_ada", col(I["b_ada"]))
    put("b_gate", col(I["b_gate"]))
    put("conv_w", np.concatenate([col(I["conv_w"][0, i]) for i in range(5)], 1))
    put("conv_b", col(I["conv_b"]))
    put("ng", col(I["ssd_norm_g"]))
    put("pscale", col(I["pool_scale"]))
    for a, b in (("ln1g", "ln1_g"), ("ln1b", "ln1_b"), ("ln2g", "ln2_g"), ("ln2b", "ln2_b")):
        put(a, col(I[b]))
    put("dskip", col(np.repeat(I["d_skip"].reshape(-1), 64)))
    put("dtb", I["dt_bias"].reshape(64, 1))
    put("alog", I["a_log"].reshape(64, 1))
    put("c2", col(I["c_2"]))
    put("cc2", col(I["c_ctx_2"]))
    put("ada_b", col(I["ada_b_2"]))
    put("bgf", col(I["gla_bg_f_2"]))
    put("bgb", col(I["gla_bg_b_2"]))
    put("gng", col(I["gla_norm_g_2"]))
    put("qng", col(I["mla_q_norm_g_2"]))
    put("kvng", col(I["mla_kv_norm_g_2"]))
    rp = I["na_rpb_2"][0]
    p = np.arange(128)
    m = np.arange(6)
    dr = m[None, :] - 2 - (p // 64)[:, None] + 7
    dc = np.clip(np.arange(64)[None, :] - (p % 64)[:, None] + 15, 0, 30)
    rpb = rp[:, dr[:, :, None], dc[:, None, :]].transpose(1, 0, 2, 3)

    arrays = {
        "vec": vec, "cst": constants(), "rpb": np.ascontiguousarray(rpb),
        "xT": np.ascontiguousarray(I["x"][0].T), "ctxT": np.ascontiguousarray(I["ctx"][0].T),
        "ctx2T": np.ascontiguousarray(I["ctx_2"][0].T),
        "w_ada": I["w_ada"][0], "w_in": I["w_in"][0], "pool_w": I["pool_w"][0],
        "w_branch_a": I["w_branch_a"][0], "w_branch_b": I["w_branch_b"][0], "w_out": I["w_out"][0],
        "w_rg": I["w_router_group"][0], "w_re": I["w_router_expert"][0],
        "b_rg": I["b_router_group"].reshape(1, 4), "b_re": I["b_router_expert"].reshape(1, 32),
        "w_eg": I["w_expert_gate"][0], "w_eu": I["w_expert_up"][0], "w_ed": I["w_expert_down"][0],
        "ada_w": I["ada_w_2"], "f1i": I["ffn1_w_in_2"], "f1o": I["ffn1_w_out_2"],
        "f2i": I["ffn2_w_in_2"], "f2o": I["ffn2_w_out_2"], "ewi": I["even_w_in_2"][0],
        "wg2f": I["gla_wg2_f_2"][0], "wg2b": I["gla_wg2_b_2"][0], "uq": I["mla_w_uq_2"][0],
        "ukv": I["mla_w_ukv_2"][0], "ewo": I["even_w_out_2"][0], "nwi": I["na_w_in_2"][0],
        "nwo": I["na_w_out_2"][0],
    }
    arrays = {k: np.ascontiguousarray(a) for k, a in arrays.items()}

    def program(plan):
        nc = _bacc.Bacc("TRN2", target_bir_lowering=False, num_devices=1)
        dram = {k: nc.dram_tensor("in_" + k, a.shape, F32, kind="ExternalInput").ap() for k, a in arrays.items()}
        out = nc.dram_tensor("out_0", (1024, 256), F32, kind="ExternalOutput").ap()
        return nc, build(nc, dram, out, plan, MODE)

    _, plan = program(None)
    nc, _ = program(plan)
    r = _run(nc, [{"in_" + k: a for k, a in arrays.items()}], core_ids=[0])
    return np.ascontiguousarray(r.results[0]["out_0"].T)[None]
```
